# Optimizing a Trainium2 kernel written in Bass

```python
import jax, jax.numpy as jnp
from jax import lax
import numpy as np

D_MODEL = 1024
BATCH = 1
SEQ = 1024
DEPTH = 1

CTX_LEN = 256
GRID_W = 64
EXPAND = 2
D_INNER = EXPAND * D_MODEL
D_FOURIER = D_INNER // 4
FOURIER_GROUP = 64
N_FOURIER_GROUPS = D_FOURIER // FOURIER_GROUP
D_SSD = D_INNER - D_FOURIER
SSD_HEAD_DIM = 64
N_SSD_HEADS = D_SSD // SSD_HEAD_DIM
N_BC_GROUPS = 4
HEADS_PER_GROUP = N_SSD_HEADS // N_BC_GROUPS
D_STATE = 128
CONV_K = 3
CONV_CH = D_SSD + 2 * N_BC_GROUPS * D_STATE
CHUNK = 128
D_PROJ = 2 * D_FOURIER + D_SSD + CONV_CH + 2 * N_SSD_HEADS
PROJ_SPLITS = (D_FOURIER, 2 * D_FOURIER, 2 * D_FOURIER + D_SSD, 2 * D_FOURIER + D_SSD + CONV_CH)
EPS = 1e-6


def rmsnorm(x, w):
    xf = x.astype(jnp.float32)
    xf = xf * lax.rsqrt(jnp.mean(xf * xf, axis=-1, keepdims=True) + EPS)
    return xf.astype(x.dtype) * w

def segsum(a):
    cum = jnp.cumsum(a, axis=-1)
    diff = cum[..., :, None] - cum[..., None, :]
    t = a.shape[-1]
    mask = jnp.tril(jnp.ones((t, t), dtype=bool))
    return jnp.where(mask, diff, -jnp.inf)

def ssd_chunked(x, dt, A, B, C, h0):
    bsz, length, g, r, p = x.shape
    n = B.shape[-1]
    nc = length // CHUNK
    xc = (x * dt[..., None]).reshape(bsz, nc, CHUNK, g, r, p)
    bc = B.reshape(bsz, nc, CHUNK, g, n)
    cc = C.reshape(bsz, nc, CHUNK, g, n)
    a = (dt * A).reshape(bsz, nc, CHUNK, g, r).transpose(0, 3, 4, 1, 2)
    a_cum = jnp.cumsum(a, axis=-1)
    lmat = jnp.exp(segsum(a))
    cb = jnp.einsum('bclgn,bcsgn->bgcls', cc, bc)
    y_diag = jnp.einsum('bgcls,bgrcls,bcsgrp->bclgrp', cb, lmat, xc)
    decay_states = jnp.exp(a_cum[..., -1:] - a_cum)
    states = jnp.einsum('bcsgn,bgrcs,bcsgrp->bcgrpn', bc, decay_states, xc)
    states = jnp.concatenate([h0[:, None], states], axis=1)
    chunk_a = jnp.pad(a_cum[..., -1], ((0, 0), (0, 0), (0, 0), (1, 0)))
    decay_chunk = jnp.exp(segsum(chunk_a))
    new_states = jnp.einsum('bgrzc,bcgrpn->bzgrpn', decay_chunk, states)
    prev_states, h_final = new_states[:, :-1], new_states[:, -1]
    y_off = jnp.einsum('bclgn,bcgrpn,bgrcl->bclgrp', cc, prev_states, jnp.exp(a_cum))
    y = (y_diag + y_off).reshape(bsz, length, g, r, p)
    return y, h_final

def depthwise_conv_grid(u, w, bias, rows, cols):
    bsz, length, ch = u.shape
    img = u.reshape(bsz, rows, cols, ch)
    out = lax.conv_general_dilated(img, w[:, :, None, :], window_strides=(1, 1), padding='SAME',
                                   dimension_numbers=('NHWC', 'HWIO', 'NHWC'), feature_group_count=ch)
    return jax.nn.silu(out.reshape(bsz, length, ch) + bias)

def fourier_mixer(u, zf, w_f, b_f):
    bsz, length, _ = u.shape
    uf = u.astype(jnp.float32).reshape(bsz, length, N_FOURIER_GROUPS, FOURIER_GROUP)
    mixed = jnp.fft.fft2(uf, axes=(1, 3), norm='ortho').real.reshape(bsz, length, D_FOURIER)
    mixed = mixed.astype(u.dtype) @ w_f + b_f
    return mixed * jax.nn.silu(zf)

def ssd_mixer(xbc, dt_raw, zs, dt_bias, a_log, d_skip, norm_w, h0_f, h0_b):
    bsz, length, _ = xbc.shape
    f32 = jnp.float32
    g, r, p, n = N_BC_GROUPS, HEADS_PER_GROUP, SSD_HEAD_DIM, D_STATE
    xs, bm, cm = jnp.split(xbc.astype(f32), [D_SSD, D_SSD + g * n], axis=-1)
    xs = xs.reshape(bsz, length, g, r, p)
    bm = bm.reshape(bsz, length, g, n)
    cm = cm.reshape(bsz, length, g, n)
    dt = jax.nn.softplus(dt_raw.astype(f32).reshape(bsz, length, 2, N_SSD_HEADS) + dt_bias.astype(f32))
    A = -jnp.exp(a_log.astype(f32)).reshape(2, g, r)
    dt_f = dt[:, :, 0].reshape(bsz, length, g, r)
    dt_b = dt[:, :, 1].reshape(bsz, length, g, r)
    flip = lambda t: jnp.flip(t, axis=1)
    y_f, h_f = ssd_chunked(xs, dt_f, A[0], bm, cm, h0_f)
    y_b, h_b = ssd_chunked(flip(xs), flip(dt_b), A[1], flip(bm), flip(cm), h0_b)
    y = y_f + flip(y_b) + d_skip.astype(f32).reshape(g, r)[:, :, None] * xs
    gated = y.reshape(bsz, length, g, r * p) * jax.nn.silu(zs.astype(f32)).reshape(bsz, length, g, r * p)
    gated = gated * lax.rsqrt(jnp.mean(gated * gated, axis=-1, keepdims=True) + EPS)
    out = gated.reshape(bsz, length, D_SSD).astype(zs.dtype) * norm_w
    return out, h_f, h_b

def token_mixer(h, rows, cols, w_in, conv_w, conv_b, dt_bias, a_log, d_skip, ssd_norm_w,
                w_fourier, b_fourier, h0_f, h0_b):
    u, zf, zs, xbc, dt_raw = jnp.split(h @ w_in, PROJ_SPLITS, axis=-1)
    four = fourier_mixer(u, zf, w_fourier, b_fourier)
    xbc = depthwise_conv_grid(xbc, conv_w, conv_b, rows, cols)
    ssd, h_f, h_b = ssd_mixer(xbc, dt_raw, zs, dt_bias, a_log, d_skip, ssd_norm_w, h0_f, h0_b)
    return jnp.concatenate([four, ssd], axis=-1), h_f, h_b

def first_inputs(seed: int = 0) -> dict:
    key = jax.random.key(seed)
    ks = jax.random.split(key, 20)
    f32 = jnp.float32
    nrm = lambda k, shape, s: jax.random.normal(k, shape, f32) * s
    dt0 = jnp.exp(jax.random.uniform(ks[9], (DEPTH, 2, N_SSD_HEADS), f32,
                                     minval=np.log(1e-3), maxval=np.log(1e-1)))
    return {
        "x": nrm(ks[0], (BATCH, SEQ, D_MODEL), 1.0),
        "c": nrm(ks[1], (BATCH, D_MODEL), 1.0),
        "ctx": nrm(ks[2], (BATCH, CTX_LEN, D_MODEL), 1.0),
        "c_ctx": nrm(ks[3], (D_MODEL,), 1.0),
        "norm_w": 1.0 + nrm(ks[4], (DEPTH, D_MODEL), 0.05),
        "w_ada": nrm(ks[5], (DEPTH, D_MODEL, 3 * D_MODEL), 0.5 * D_MODEL ** -0.5),
        "b_ada": nrm(ks[6], (DEPTH, 3 * D_MODEL), 0.02),
        "w_in": nrm(ks[7], (DEPTH, D_MODEL, D_PROJ), D_MODEL ** -0.5),
        "conv_w": nrm(ks[8], (DEPTH, CONV_K, CONV_K, CONV_CH), 1.0 / CONV_K),
        "conv_b": nrm(ks[10], (DEPTH, CONV_CH), 0.02),
        "dt_bias": dt0 + jnp.log(-jnp.expm1(-dt0)),
        "a_log": jnp.log(jax.random.uniform(ks[11], (DEPTH, 2, N_SSD_HEADS), f32, minval=1.0, maxval=16.0)),
        "d_skip": 1.0 + nrm(ks[12], (DEPTH, N_SSD_HEADS), 0.1),
        "ssd_norm_w": 1.0 + nrm(ks[13], (DEPTH, D_SSD), 0.05),
        "w_fourier": nrm(ks[14], (DEPTH, D_FOURIER, D_FOURIER), D_FOURIER ** -0.5),
        "b_fourier": nrm(ks[15], (DEPTH, D_FOURIER), 0.02),
        "w_out": nrm(ks[16], (DEPTH, D_INNER, D_MODEL), D_INNER ** -0.5),
        "final_norm_w": 1.0 + nrm(ks[17], (D_MODEL,), 0.05),
    }

def first_block(x, c, ctx, c_ctx, norm_w, w_ada, b_ada, w_in, conv_w, conv_b, dt_bias, a_log, d_skip,
              ssd_norm_w, w_fourier, b_fourier, w_out, final_norm_w):
    bsz, seq_len, _ = x.shape
    ctx_len = ctx.shape[1]
    rows = seq_len // GRID_W
    zeros_state = jnp.zeros((bsz, N_BC_GROUPS, HEADS_PER_GROUP, SSD_HEAD_DIM, D_STATE), jnp.float32)
    silu_c = jax.nn.silu(c)
    silu_cc = jax.nn.silu(c_ctx)
    for i in range(DEPTH):
        mod = silu_c @ w_ada[i] + b_ada[i]
        shift, scale, gate = jnp.split(mod, 3, axis=-1)
        mod_c = silu_cc @ w_ada[i] + b_ada[i]
        shift_c, scale_c, gate_c = jnp.split(mod_c, 3, axis=-1)
        layer = (w_in[i], conv_w[i], conv_b[i], dt_bias[i], a_log[i], d_skip[i], ssd_norm_w[i],
                 w_fourier[i], b_fourier[i])
        hc = rmsnorm(ctx, norm_w[i]) * (1.0 + scale_c) + shift_c
        ctx_mix, h_f, h_b = token_mixer(hc, 1, ctx_len, *layer, zeros_state, zeros_state)
        hx = rmsnorm(x, norm_w[i]) * (1.0 + scale[:, None]) + shift[:, None]
        x_mix, _, _ = token_mixer(hx, rows, GRID_W, *layer, h_f, h_b)
        x = x + gate[:, None] * (x_mix @ w_out[i])
        if i < DEPTH - 1:
            ctx = ctx + gate_c * (ctx_mix @ w_out[i])
    return rmsnorm(x, final_norm_w)


CHUNK_2 = 64
Q_BLOCK = 128
HEAD_DIM = 64
N_HEADS_FOX = 8
N_HEADS_DSA = 8
IDX_HEADS = 8
IDX_DIM = 64
TOPK_MAX = 256
ROPE_THETA = 10000.0
N_GROUPS = 4
EXPERTS_PER_GROUP = 8
N_EXPERTS = N_GROUPS * EXPERTS_PER_GROUP
TOP_K_INNER = 2
D_EXPERT = 512

W_FOX = N_HEADS_FOX * HEAD_DIM
W_DSA = N_HEADS_DSA * HEAD_DIM
IN_SPLITS = (W_FOX, W_FOX, W_FOX, N_HEADS_FOX,
             W_DSA, HEAD_DIM, HEAD_DIM,
             IDX_HEADS * IDX_DIM, IDX_DIM, IDX_HEADS,
             D_MODEL, D_MODEL)
IN_COLS = 3 * W_FOX + N_HEADS_FOX + W_DSA + 2 * HEAD_DIM + IDX_HEADS * IDX_DIM + IDX_DIM + IDX_HEADS + 2 * D_MODEL


def rmsnorm_2(x, g):
    xf = x.astype(jnp.float32)
    y = xf * lax.rsqrt(jnp.mean(xf * xf, axis=-1, keepdims=True) + EPS)
    return (y * g.astype(jnp.float32)).astype(x.dtype)

def rope(x, pos):
    half = x.shape[-1] // 2
    inv = ROPE_THETA ** (-jnp.arange(half, dtype=jnp.float32) / half)
    ang = pos.astype(jnp.float32)[..., None] * inv
    cos = jnp.cos(ang)[:, :, None, :]
    sin = jnp.sin(ang)[:, :, None, :]
    x1 = x[..., :half].astype(jnp.float32)
    x2 = x[..., half:].astype(jnp.float32)
    out = jnp.concatenate([x1 * cos - x2 * sin, x2 * cos + x1 * sin], axis=-1)
    return out.astype(x.dtype)

def forgetting_attention(q, k, v, log_f):
    B, S, H, D = q.shape
    Ft = jnp.cumsum(log_f, axis=1).transpose(0, 2, 1)
    scale = D ** -0.5
    outs = []
    for start in range(0, S, Q_BLOCK):
        end = start + Q_BLOCK
        s = jnp.einsum('bqhd,bkhd->bhqk', q[:, start:end], k[:, :end],
                       preferred_element_type=jnp.float32) * scale
        s = s + Ft[:, :, start:end, None] - Ft[:, :, None, :end]
        tq = jnp.arange(start, end)[:, None]
        tk = jnp.arange(end)[None, :]
        s = jnp.where(tk <= tq, s, -jnp.inf)
        p = jax.nn.softmax(s, axis=-1)
        outs.append(jnp.einsum('bhqk,bkhd->bqhd', p.astype(v.dtype), v[:, :end]))
    return jnp.concatenate(outs, axis=1)

def dsa_attention(q, k, v, qi, ki, wi):
    B, S, H, D = q.shape
    topk = min(TOPK_MAX, S // 4)
    chunk_id = jnp.arange(S) // CHUNK_2
    scale = D ** -0.5
    gather = jax.vmap(lambda arr, ids: arr[ids])
    outs = []
    for start in range(0, S, Q_BLOCK):
        end = start + Q_BLOCK
        kk = min(topk, end)
        dots = jnp.einsum('bqhd,bkd->bqhk', qi[:, start:end], ki[:, :end],
                          preferred_element_type=jnp.float32)
        score = jnp.einsum('bqh,bqhk->bqk', wi[:, start:end].astype(jnp.float32), jax.nn.relu(dots))
        cq = chunk_id[start:end]
        allowed = chunk_id[:end][None, :] <= cq[:, None]
        score = jnp.where(allowed[None], score, -jnp.inf)
        _, idx = lax.top_k(score, kk)
        valid = chunk_id[idx] <= cq[None, :, None]
        kg = gather(k[:, :end], idx)
        vg = gather(v[:, :end], idx)
        s = jnp.einsum('bqhd,bqkd->bhqk', q[:, start:end], kg,
                       preferred_element_type=jnp.float32) * scale
        s = jnp.where(valid[:, None], s, -jnp.inf)
        p = jax.nn.softmax(s, axis=-1)
        outs.append(jnp.einsum('bhqk,bqkd->bqhd', p.astype(vg.dtype), vg))
    return jnp.concatenate(outs, axis=1)

def hierarchical_moe(h, w_grp, b_grp, w_exp, b_exp, w1, w3, w2):
    N, D = h.shape
    g_logits = jnp.matmul(h, w_grp).astype(jnp.float32) + b_grp.astype(jnp.float32)
    g_prob = jax.nn.softmax(g_logits, axis=-1)
    g_idx = jnp.argmax(g_logits, axis=-1)
    g_w = jnp.take_along_axis(g_prob, g_idx[:, None], axis=1)[:, 0]
    e_logits = (jnp.matmul(h, w_exp).astype(jnp.float32) + b_exp.astype(jnp.float32))
    e_logits = e_logits.reshape(N, N_GROUPS, EXPERTS_PER_GROUP)
    e_logits = jnp.take_along_axis(e_logits, g_idx[:, None, None], axis=1)[:, 0]
    e_prob = jax.nn.softmax(e_logits, axis=-1)
    top_p, top_local = lax.top_k(e_prob, TOP_K_INNER)
    top_p = top_p / jnp.sum(top_p, axis=-1, keepdims=True)
    weights = (g_w[:, None] * top_p).reshape(-1)
    expert = (g_idx[:, None] * EXPERTS_PER_GROUP + top_local).reshape(-1)
    order = jnp.argsort(expert)
    tok = order // TOP_K_INNER
    xs = h[tok]
    sizes = jnp.bincount(expert, length=N_EXPERTS).astype(jnp.int32)
    a = lax.ragged_dot(xs, w1, sizes)
    b = lax.ragged_dot(xs, w3, sizes)
    y = lax.ragged_dot(jax.nn.silu(a) * b, w2, sizes)
    y = (y * weights[order][:, None]).astype(h.dtype)
    return jax.ops.segment_sum(y, tok, num_segments=N)

def second_inputs(seed: int = 0) -> dict:
    key = jax.random.key(seed)
    ks = jax.random.split(key, 24)
    f32 = jnp.float32
    nrm = lambda k, shape, fan: jax.random.normal(k, shape, f32) * fan ** -0.5
    L = DEPTH
    x = jax.random.normal(ks[0], (BATCH, SEQ, D_MODEL), f32)
    c = jax.random.normal(ks[1], (BATCH, D_MODEL), f32)
    offsets = jax.random.randint(ks[2], (BATCH,), 0, 64) * CHUNK_2
    positions = (offsets[:, None] + jnp.arange(SEQ)[None, :]).astype(jnp.int32)
    return {
        'x': x,
        'c': c,
        'positions': positions,
        'ada_w': nrm(ks[3], (L, D_MODEL, 6 * D_MODEL), D_MODEL) * 0.5,
        'ada_b': jax.random.normal(ks[4], (L, 6 * D_MODEL), f32) * 0.02,
        'norm1_g': 1.0 + 0.05 * jax.random.normal(ks[5], (L, D_MODEL), f32),
        'norm2_g': 1.0 + 0.05 * jax.random.normal(ks[6], (L, D_MODEL), f32),
        'w_in': nrm(ks[7], (L, D_MODEL, IN_COLS), D_MODEL),
        'b_fgt': jax.random.uniform(ks[8], (L, N_HEADS_FOX), f32, 1.0, 4.0),
        'b_gate': jax.random.normal(ks[9], (L, 2 * D_MODEL), f32) * 0.02,
        'qn_fox': 1.0 + 0.05 * jax.random.normal(ks[10], (L, HEAD_DIM), f32),
        'kn_fox': 1.0 + 0.05 * jax.random.normal(ks[11], (L, HEAD_DIM), f32),
        'qn_dsa': 1.0 + 0.05 * jax.random.normal(ks[12], (L, HEAD_DIM), f32),
        'kn_dsa': 1.0 + 0.05 * jax.random.normal(ks[13], (L, HEAD_DIM), f32),
        'w_proj_fox': nrm(ks[14], (L, W_FOX, D_MODEL), W_FOX),
        'w_proj_dsa': nrm(ks[15], (L, W_DSA, D_MODEL), W_DSA),
        'w_out': nrm(ks[16], (L, D_MODEL, D_MODEL), D_MODEL),
        'router_w_grp': nrm(ks[17], (L, D_MODEL, N_GROUPS), D_MODEL),
        'router_b_grp': jax.random.normal(ks[18], (L, N_GROUPS), f32) * 0.01,
        'router_w_exp': nrm(ks[19], (L, D_MODEL, N_EXPERTS), D_MODEL),
        'router_b_exp': jax.random.normal(ks[20], (L, N_EXPERTS), f32) * 0.01,
        'exp_w1': nrm(ks[21], (L, N_EXPERTS, D_MODEL, D_EXPERT), D_MODEL),
        'exp_w3': nrm(ks[22], (L, N_EXPERTS, D_MODEL, D_EXPERT), D_MODEL),
        'exp_w2': nrm(ks[23], (L, N_EXPERTS, D_EXPERT, D_MODEL), D_EXPERT),
    }

def second_block(x, c, positions, ada_w, ada_b, norm1_g, norm2_g, w_in, b_fgt, b_gate,
              qn_fox, kn_fox, qn_dsa, kn_dsa, w_proj_fox, w_proj_dsa, w_out,
              router_w_grp, router_b_grp, router_w_exp, router_b_exp,
              exp_w1, exp_w3, exp_w2):
    B, S, D = x.shape
    split_at = np.cumsum(IN_SPLITS)[:-1].tolist()
    c_act = jax.nn.silu(c)
    for l in range(DEPTH):
        mod = jnp.matmul(c_act, ada_w[l]) + ada_b[l]
        sh1, sc1, gt1, sh2, sc2, gt2 = [m[:, None, :] for m in jnp.split(mod, 6, axis=-1)]

        h = rmsnorm_2(x, norm1_g[l]) * (1.0 + sc1) + sh1
        proj = jnp.matmul(h, w_in[l])
        (fq, fk, fv, flog, dq, dk, dv, iq, ik, iw, g_fox, g_dsa) = jnp.split(proj, split_at, axis=-1)

        fq = rmsnorm_2(fq.reshape(B, S, N_HEADS_FOX, HEAD_DIM), qn_fox[l])
        fk = rmsnorm_2(fk.reshape(B, S, N_HEADS_FOX, HEAD_DIM), kn_fox[l])
        fv = fv.reshape(B, S, N_HEADS_FOX, HEAD_DIM)
        log_f = jax.nn.log_sigmoid((flog + b_fgt[l]).astype(jnp.float32))
        out_fox = forgetting_attention(fq, fk, fv, log_f).reshape(B, S, W_FOX)

        dq = rope(rmsnorm_2(dq.reshape(B, S, N_HEADS_DSA, HEAD_DIM), qn_dsa[l]), positions)
        dk = rope(rmsnorm_2(dk.reshape(B, S, 1, HEAD_DIM), kn_dsa[l]), positions)[:, :, 0]
        iq = rope(iq.reshape(B, S, IDX_HEADS, IDX_DIM), positions)
        ik = rope(ik.reshape(B, S, 1, IDX_DIM), positions)[:, :, 0]
        out_dsa = dsa_attention(dq, dk, dv, iq, ik, iw).reshape(B, S, W_DSA)

        merged = (jax.nn.sigmoid(g_fox + b_gate[l, :D]) * jnp.matmul(out_fox, w_proj_fox[l])
                  + jax.nn.sigmoid(g_dsa + b_gate[l, D:]) * jnp.matmul(out_dsa, w_proj_dsa[l]))
        x = x + gt1 * jnp.matmul(merged, w_out[l])

        h2 = rmsnorm_2(x, norm2_g[l]) * (1.0 + sc2) + sh2
        y = hierarchical_moe(h2.reshape(B * S, D), router_w_grp[l], router_b_grp[l],
                             router_w_exp[l], router_b_exp[l],
                             exp_w1[l], exp_w3[l], exp_w2[l]).reshape(B, S, D)
        x = x + gt2 * y
    return x


def setup_inputs(seed=0):
    out = dict(first_inputs(seed))
    for name, value in second_inputs(seed + 1).items():
        if name != "x":
            out[name + "_2"] = value
    return out


def reference(
    x, c, ctx, c_ctx, norm_w, w_ada, b_ada, w_in, conv_w, conv_b, dt_bias, a_log, d_skip,
    ssd_norm_w, w_fourier, b_fourier, w_out, final_norm_w, c_2, positions_2, ada_w_2, ada_b_2,
    norm1_g_2, norm2_g_2, w_in_2, b_fgt_2, b_gate_2, qn_fox_2, kn_fox_2, qn_dsa_2, kn_dsa_2,
    w_proj_fox_2, w_proj_dsa_2, w_out_2, router_w_grp_2, router_b_grp_2, router_w_exp_2,
    router_b_exp_2, exp_w1_2, exp_w3_2, exp_w2_2,
):
    x = first_block(
        x, c, ctx, c_ctx, norm_w, w_ada, b_ada, w_in, conv_w, conv_b, dt_bias, a_log, d_skip,
        ssd_norm_w, w_fourier, b_fourier, w_out, final_norm_w,
    )
    return second_block(
        x, c_2, positions_2, ada_w_2, ada_b_2, norm1_g_2, norm2_g_2, w_in_2, b_fgt_2, b_gate_2,
        qn_fox_2, kn_fox_2, qn_dsa_2, kn_dsa_2, w_proj_fox_2, w_proj_dsa_2, w_out_2,
        router_w_grp_2, router_b_grp_2, router_w_exp_2, router_b_exp_2, exp_w1_2, exp_w3_2,
        exp_w2_2,
    )


_drawn_inputs = setup_inputs


def setup_inputs(seed=0):
    import zlib

    import numpy as np

    out = dict(_drawn_inputs(seed))
    spreads = {}
    factors = {'ctx': 8.0,
     'c_ctx': 8.0,
     'norm_w': 2.689,
     'conv_b': 5.427,
     'd_skip': 4.883,
     'ssd_norm_w': 3.558,
     'b_fourier': 8.0,
     'ada_b_2': 3.384,
     'norm1_g_2': 6.25,
     'norm2_g_2': 3.134,
     'b_gate_2': 8.0,
     'qn_fox_2': 8.0,
     'kn_fox_2': 8.0,
     'qn_dsa_2': 8.0,
     'kn_dsa_2': 8.0,
     'router_b_grp_2': 7.9,
     'router_b_exp_2': 8.0}
    for name, (base, spread) in spreads.items():
        noise = np.random.default_rng([zlib.crc32(name.encode()), seed]).standard_normal(out[name].shape)
        drawn = base * np.exp(spread * noise) if base else spread * noise
        out[name] = __import__('jax').numpy.asarray(drawn.astype(out[name].dtype))
    for name, factor in factors.items():
        out[name] = (out[name] * factor).astype(out[name].dtype)
    return out
```

```python
import numpy as np
import concourse.bass as bass
from concourse import mybir
from contextlib import ExitStack

F32, BF16, I32 = mybir.dt.float32, mybir.dt.bfloat16, mybir.dt.int32
U32 = mybir.dt.uint32
ALU, ACT, AX = mybir.AluOpType, mybir.ActivationFunctionType, mybir.AxisListType
START = 4096


class Ticket:
    def __init__(self, queue, base, step, loop):
        self.queue, self.base, self.step, self.loop = queue, base, step, loop

    def last_round(self, back=1):
        return Ticket(self.queue, self.base - back * self.step, self.step, self.loop)

    def value(self):
        return self.base if self.loop is None else self.loop * self.step + self.base


class Queue:
    def __init__(self, nc, eng, name, unit=1, start=START):
        self.eng, self.unit, self.sem = eng, unit, nc.alloc_semaphore(name)
        self.n, self.step, self.loop, self.counting = start, 0, None, False
        if start:
            eng.sem_inc(self.sem, start)

    def __call__(self, f, after=(), own=False, inc=True):
        if own:
            self.wait(self.last())
        self.wait(*after)
        if not self.counting:
            ins = f(self.eng)
            if inc:
                ins.then_inc(self.sem, self.unit)
        if inc:
            self.n += self.unit
        return self.last()

    def last(self):
        return Ticket(self, self.n, self.step, self.loop)

    def wait(self, *tickets):
        if self.counting:
            return
        for t in tickets:
            if t is not None:
                self.eng.wait_ge(t.queue.sem, t.value())


def run_loop(nc, queues, trips, body):
    before, marks = {q: q.n for q in queues}, {}
    for q in queues:
        q.counting = True
    body(0, marks)
    steps = {q: q.n - before[q] for q in queues}
    for t in marks.values():
        t.step = steps[t.queue]
    for q in queues:
        q.n, q.counting, q.step = before[q], False, steps[q]
    with nc.Fori(0, trips) as i:
        for q in queues:
            q.loop = i
        for t in marks.values():
            t.loop = i
        body(i, dict(marks))
    for q in queues:
        q.n, q.step, q.loop = before[q] + trips * steps[q], 0, None
D, SEQ, CTX, P, KD = 1024, 1024, 256, 128, 8
NT, NC = SEQ // P, CTX // P
DF, DS, NBC, NST = 512, 1536, 4, 128
NH, HP, HG = 24, 64, 6
CONV, GRID_H, GRID_W = 2560, 16, 64
COL_Z, COL_XBC, COL_DT = 512, 2560, 5120
EPS, FAR = 1e-6, -1e30
C_ID, C_LE, C_GE, C_GT, C_LT, C_ONE = range(6)


class Core:
    def __init__(self, nc, ctx):
        self.nc, self.ctx = nc, ctx
        self.T, self.V, self.A, self.G = (Queue(nc, e, n) for e, n in (
            (nc.tensor, "pe_done"), (nc.vector, "dve_done"), (nc.scalar, "act_done"), (nc.gpsimd, "pool_done")))
        self.load = [Queue(nc, nc.sync, f"load{j}_done", 16) for j in range(12)]
        self.store = [Queue(nc, nc.scalar, f"store{j}_done", 16) for j in range(8)]
        self.gather = [Queue(nc, nc.gpsimd, f"gather{j}_done", 16, 0) for j in range(4)]
        self.scatter = Queue(nc, nc.gpsimd, "scatter_done", 16, 0)
        self.queues = [self.T, self.V, self.A, self.G] + self.load + self.store + self.gather + [self.scatter]
        self.engines = [nc.tensor, nc.vector, nc.scalar, nc.gpsimd, nc.sync]
        self.bank = ctx.enter_context(nc.psum_tensor("banks", [P, 8, 512], F32))

    def settle(self):
        for e in self.engines:
            for q in self.queues:
                if q.n:
                    e.wait_ge(q.sem, q.n)

    def loop(self, trips, body):
        run_loop(self.nc, self.queues, trips, body)

    def mm(self, out, pairs, after=(), inc=True, start=True, stop=True):
        self.T.wait(*after)
        for n, (a, b) in enumerate(pairs):
            last = n == len(pairs) - 1
            self.T(lambda e: e.matmul(out, a(), b(), start=start and n == 0, stop=stop and last), inc=inc and last)
        return self.T.last()

    def tr(self, outs, ident, after=()):
        self.T.wait(*after)
        for n, (o, a) in enumerate(outs):
            self.T(lambda e: e.transpose(o(), a(), ident), inc=n == len(outs) - 1)
        return self.T.last()


class Room:
    def __init__(self, core):
        self.core, self.stack = core, ExitStack()

    def __call__(self, name, shape, dt=F32):
        return self.stack.enter_context(self.core.nc.sbuf_tensor(name, shape, dt))

    def __enter__(self):
        self.stack.__enter__()
        return self

    def __exit__(self, *a):
        self.core.settle()
        return self.stack.__exit__(*a)


def row(ap):
    return ap.partition_broadcast(P)


def over(ap, axis, n):
    a = ap.unsqueeze(axis)
    shape = list(a.shape)
    shape[axis] = n
    return a.to_broadcast(shape)


def modulation(core, dram, tables):
    with Room(core) as sb:
        T, V, A = core.T, core.V, core.A
        c = sb("mod_c", [P, 3, KD])
        cs = sb("mod_silu", [P, KD, 3])
        w = [sb(f"mod_w{b}", [P, KD, 512]) for b in range(2)]
        bias = [sb(f"mod_b{b}", [2, 512]) for b in range(2)]
        out = [sb(f"mod_o{b}", [2, 512]) for b in range(2)]
        got = None
        for j, name in enumerate(("c", "c_ctx", "c_2")):
            got = core.load[10](lambda e: e.dma_start(c[:, j, :], dram[name].rearrange("(p k) -> p k", k=KD)))
        silu = A(lambda e: e.activation(cs[:].rearrange("p k j -> p j k"), c[:], ACT.Silu), after=[got])
        T.wait(silu)
        for w_name, b_name, o_name, j0, m, n in (("w_ada", "b_ada", "mods", 0, 2, 6), ("ada_w_2", "ada_b_2", "mod2", 2, 1, 12)):
            wv = dram[w_name].rearrange("(p k) n -> p k n", k=KD)

            def body(i, marks):
                for b in range(2):
                    at = bass.ds(i * 1024 + 512 * b, 512)
                    prev = lambda x: [marks[x].last_round()] if x in marks else []
                    lw = core.load[b](lambda e: e.dma_start(w[b][:], wv[:, :, at]), after=prev(f"mm{b}"))
                    lb = core.load[2 + b](lambda e: e.dma_start(bias[b][0:m, :], dram[b_name][at].partition_broadcast(m)),
                                          after=prev(f"add{b}"))
                    t = core.mm(core.bank[0:m, b, :], [(lambda k=k: cs[:, k, j0:j0 + m], lambda k=k: w[b][:, k, :])
                                                       for k in range(KD)], after=[lw] + prev(f"add{b}"))
                    v = V(lambda e: e.tensor_tensor(out[b][0:m, :], core.bank[0:m, b, :], bias[b][0:m, :], ALU.add),
                          after=[t, lb] + prev(f"st{b}"))
                    marks[f"mm{b}"], marks[f"add{b}"] = t, v
                    marks[f"st{b}"] = core.store[b](lambda e: e.dma_start(dram[o_name][0:m, at], out[b][0:m, :]), after=[v])
            core.loop(n // 2, body)


class Norm:
    def __init__(self, core, sb, name):
        self.core = core
        self.sq = sb(name + "_sq", [P, D])
        self.ss = sb(name + "_ss", [P, 1])
        self.sd = sb(name + "_sd", [P, 1])
        self.rs = sb(name + "_rs", [P, 1])

    def rstd(self, x, eps, after):
        core = self.core
        core.A(lambda e: e.activation(self.sq[:], x, ACT.Square, accum_out=self.ss[:]), after=after)
        a = core.A(lambda e: e.activation(self.sd[:], self.ss[:], ACT.Sqrt, bias=eps, scale=1.0 / D), own=True)
        return core.V(lambda e: e.reciprocal(self.rs[:], self.sd[:]), after=[a])

    def apply(self, out, x, gain, shift=None, after=()):
        v = self.core.V(lambda e: e.scalar_tensor_tensor(out=out, in0=x, scalar=self.rs[:, 0:1], in1=gain,
                                                         op0=ALU.mult, op1=ALU.mult), after=after, own=True)
        if shift is not None:
            v = self.core.V(lambda e: e.tensor_tensor(out, out, shift, ALU.add), own=True)
        return v


def gain_rows(core, gain, w_row, scale_row, shift, shift_row, tmp):
    core.load[0](lambda e: e.dma_start(gain, row(w_row)))
    core.load[0](lambda e: e.dma_start(tmp, row(scale_row)))
    got = core.load[0](lambda e: e.dma_start(shift, row(shift_row)))
    core.V(lambda e: e.scalar_tensor_tensor(out=gain, in0=tmp, scalar=1.0, in1=gain, op0=ALU.add, op1=ALU.mult), after=[got])
    return core.V.last()


def project_first(core, dram, tables):
    T, V, A, G = core.T, core.V, core.A, core.G
    ident = tables["mats"][:, C_ID, :]
    with Room(core) as sb:
        TOK = SEQ + CTX
        hT = sb("hT", [P, KD, TOK])
        with Room(core) as sb1:
            norm = Norm(core, sb1, "n1")
            gain, shift, tmp = (sb1(f"n1_{n}", [P, D]) for n in ("gain", "shift", "tmp"))
            x = [sb1(f"n1_x{b}", [P, D]) for b in range(2)]
            h = [sb1(f"n1_h{b}", [P, D]) for b in range(2)]
            for src, mod, n, at0 in ((dram["x"], 0, NT, 0), (dram["ctx"], 1, NC, SEQ)):
                mrow = dram["mods"][mod, :]
                rows_in = gain_rows(core, gain[:], dram["norm_w"], mrow[D:2 * D], shift[:], mrow[0:D], tmp[:])

                def body(i, marks):
                    prev = lambda k: [marks[k].last_round()] if k in marks else []
                    for b in range(2):
                        ld = core.load[1 + b](lambda e: e.dma_start(x[b][:], src[bass.ds(i * 256 + 128 * b, 128), :]),
                                              after=prev(f"h{b}"))
                        V.wait(norm.rstd(x[b][:], tables["eps"][:, 0:1], [ld]))
                        v = norm.apply(h[b][:], x[b][:], gain[:], shift[:], after=prev(f"t{b}") + [rows_in])
                        marks[f"h{b}"] = v
                        t = core.tr([(lambda k=k: core.bank[:, 2 * b + k // 4, 128 * (k % 4):128 * (k % 4) + 128],
                                      lambda k=k: h[b][:, 128 * k:128 * k + 128]) for k in range(KD)], ident,
                                    after=[v] + prev(f"ev{b}"))
                        marks[f"t{b}"] = t
                        for half in range(2):
                            A(lambda e: e.activation(hT[:, 4 * half:4 * half + 4, bass.ds(i * 256 + 128 * b + at0, 128)],
                                                     core.bank[:, 2 * b + half, :].rearrange("p (k n) -> p k n", k=4),
                                                     ACT.Copy), after=[t])
                        marks[f"ev{b}"] = A.last()
                core.loop(n // 2, body)
                core.V.wait(T.last(), A.last())
                core.nc.sync.wait_ge(V.sem, V.n)

        NCT = CONV // P
        taps = sb("taps", [P, NCT, 10])
        with Room(core) as sb1:
            flat = sb1("taps_flat", [10, CONV])
            core.load[0](lambda e: e.dma_start(flat[0:9, :], dram["conv_w"].rearrange("a b c -> (a b) c")))
            got = core.load[0](lambda e: e.dma_start(flat[9:10, :], dram["conv_b"].rearrange("(a c) -> a c", a=1)))
            t = core.tr([(lambda k=k: core.bank[:, 0, 10 * k:10 * k + 10], lambda k=k: flat[:, 128 * k:128 * k + 128])
                         for k in range(NCT)], tables["mats"][0:10, C_ID, 0:10], after=[got])
            V(lambda e: e.tensor_copy(taps[:].rearrange("p t j -> p (t j)"), core.bank[:, 0, 0:10 * NCT]), after=[t])

        w = [sb(f"w1_{b}", [P, KD, 256]) for b in range(2)]
        img = [sb(f"img{b}", [P, GRID_H + 2, GRID_W + 2]) for b in range(2)]
        line = [sb(f"line{b}", [P, CTX + 2]) for b in range(2)]
        acc = [sb(f"acc{b}", [P, TOK]) for b in range(2)]
        tap = [sb(f"tap{b}", [P, 10]) for b in range(2)]
        res = [sb(f"res{b}", [P, TOK]) for b in range(2)]
        for b in range(2):
            G(lambda e: e.memset(img[b][:], 0.0))
            G(lambda e: e.memset(line[b][:], 0.0))
        zeroed = G.last()
        win = dram["w_in"].rearrange("(k p) n -> p k n", p=P)

        def products(s, b, wap, lw, wait, ctx_too):
            T.wait(lw, *wait)
            for half, n0, n in ((0, 0, 512), (1, 512, 512)) + (((2, 1024, 256),) if ctx_too else ()):
                core.mm(core.bank[:, 3 * b + half, 0:n], [(lambda k=k: wap[:, k, 128 * s:128 * s + 128],
                                                          lambda k=k: hT[:, k, n0:n0 + n]) for k in range(KD)])
            return T.last()

        for slab in range(2):
            lw = core.load[1 + slab](lambda e: e.dma_start(w[slab][:], win[:, :, 256 * slab:256 * slab + 256]))
            for s in range(2):
                u_tile = 2 * slab + s
                t = products(s, s, w[slab], lw, [A.last()] if u_tile > 1 else [], False)
                a = A(lambda e: e.activation(res[s][:, 0:SEQ], core.bank[:, 3 * s:3 * s + 2, :].rearrange("p a n -> p (a n)"),
                                             ACT.Copy), after=[t] + ([core.store[s].last()] if u_tile > 1 else []))
                core.store[s](lambda e: e.dma_start(dram["uT"][128 * u_tile:128 * u_tile + 128, :], res[s][:, 0:SEQ]), after=[a])
        before = [T.last(), A.last(), zeroed, core.store[0].last(), core.store[1].last()]
        for q in (T, V, A, core.load[1], core.load[2]):
            q.wait(*before)

        def body(i, marks):
            prev = lambda k: [marks[k].last_round()] if k in marks else []
            for slab in range(2):
                lw = core.load[1 + slab](lambda e: e.dma_start(w[slab][:], win[:, :, bass.ds(i * 512 + COL_XBC + 256 * slab, 256)]),
                                         after=prev(f"mm{slab}"))
                for s in range(2):
                    first = slab == 0
                    j = 2 * slab + s
                    before = (lambda k: prev(k + str(2 + s))) if first else (lambda k: [marks[k + str(s)]] if k + str(s) in marks else [])
                    t = products(s, s, w[slab], lw, before("ev"), True)
                    marks[f"mm{slab}"] = t
                    A(lambda e: e.activation(img[s][:, 1:1 + GRID_H, 1:1 + GRID_W],
                                             core.bank[:, 3 * s:3 * s + 2, :].rearrange("p a (r c) -> p (a r) c", c=GRID_W),
                                             ACT.Copy), after=[t] + before("conv"))
                    A(lambda e: e.activation(line[s][:, 1:1 + CTX], core.bank[:, 3 * s + 2, 0:CTX], ACT.Copy))
                    a = A(lambda e: e.activation(tap[s][:], taps[:, bass.ds(i * 4 + j, 1), :].rearrange("p a n -> p (a n)"),
                                                 ACT.Copy))
                    marks[f"ev{j}"] = a
                    V.wait(a, *before("silu"))
                    grid = acc[s][:, 0:SEQ].rearrange("p (r c) -> p r c", c=GRID_W)
                    for dy in range(3):
                        for dx in range(3):
                            src = img[s][:, dy:dy + GRID_H, dx:dx + GRID_W]
                            wt = tap[s][:, 3 * dy + dx:3 * dy + dx + 1]
                            if dy == dx == 0:
                                V(lambda e: e.tensor_scalar(grid, src, wt, None, ALU.mult))
                            else:
                                V(lambda e: e.scalar_tensor_tensor(out=grid, in0=src, scalar=wt, in1=grid,
                                                                   op0=ALU.mult, op1=ALU.add), own=True)
                    for dx in range(3):
                        wt = tap[s][:, 3 + dx:4 + dx]
                        if dx == 0:
                            V(lambda e: e.tensor_scalar(acc[s][:, SEQ:TOK], line[s][:, 0:CTX], wt, None, ALU.mult))
                        else:
                            V(lambda e: e.scalar_tensor_tensor(out=acc[s][:, SEQ:TOK], in0=line[s][:, dx:dx + CTX], scalar=wt,
                                                               in1=acc[s][:, SEQ:TOK], op0=ALU.mult, op1=ALU.add), own=True)
                    marks[f"conv{j}"] = V.last()
                    marks[f"silu{j}"] = A(lambda e: e.activation(res[s][:], acc[s][:], ACT.Silu, bias=tap[s][:, 9:10]),
                                          after=[V.last()] + before("st"))
                    marks[f"st{j}"] = core.store[s](
                        lambda e: e.dma_start(dram["xbcT"][bass.ds(i * 512 + 128 * j, 128), :], res[s][:]), after=[A.last()])
        core.loop(NCT // 4, body)
        core.settle()

        zw = [sb(f"zw{b}", [P, KD, 512]) for b in range(2)]
        zo = [sb(f"zo{b}", [P, 512]) for b in range(4)]

        def body(i, marks):
            prev = lambda k: [marks[k].last_round()] if k in marks else []
            for b in range(2):
                lw = core.load[1 + b](lambda e: e.dma_start(zw[b][:], win[:, :, bass.ds(i * 1024 + COL_Z + 512 * b, 512)]),
                                      after=prev(f"mm{b}"))
                T.wait(lw)
                for m in range(NT):
                    n = NT * b + m
                    s = n % 4
                    old = lambda k: [marks[f"{k}{n - 4}"]] if n >= 4 else prev(f"{k}{n + 12}")
                    t = core.mm(core.bank[:, s, :], [(lambda k=k: hT[:, k, 128 * m:128 * m + 128], lambda k=k: zw[b][:, k, :])
                                                     for k in range(KD)], after=old("ev"))
                    marks[f"mm{b}"] = t
                    marks[f"ev{n}"] = A(lambda e: e.activation(zo[s][:], core.bank[:, s, :], ACT.Silu), after=[t] + old("st"))
                    marks[f"st{n}"] = core.store[s](lambda e: e.dma_start(
                        dram["z"][128 * m:128 * m + 128, bass.ds(i * 1024 + 512 * b, 512)], zo[s][:]), after=[A.last()])
        core.loop(2, body)
        core.settle()
        wd = sb("wd", [P, KD, 2 * NH])
        lw = core.load[0](lambda e: e.dma_start(wd[:], win[:, :, COL_DT:COL_DT + 2 * NH]))
        T.wait(lw)
        for m in range(NT + NC):
            t = core.mm(core.bank[:, 0, 48 * m:48 * m + 48], [(lambda k=k: hT[:, k, 128 * m:128 * m + 128], lambda k=k: wd[:, k, :])
                                                             for k in range(KD)])
        V(lambda e: e.tensor_copy(tables["dt"][:].rearrange("p t h -> p (t h)"), core.bank[:, 0, 0:480]), after=[t])


def fourier(core, dram, tables):
    T, V, A, G = core.T, core.V, core.A, core.G
    with Room(core) as sb:
        groups = sb("f_groups", [P, 256])
        uc = [sb(f"f_u{b}", [P, 4, P]) for b in range(2)]
        AC = sb("f_AC", [P, NT, 2, DF])
        CS = sb("f_CS", [P, 2, KD, SEQ])
        lhs = [sb(f"f_lhs{b}", [P, NT, 2, P]) for b in range(2)]
        mT = sb("f_mT", [P, 4, SEQ])
        g = core.load[0](lambda e: e.dma_start(groups[:], dram["dft_groups"]))
        big = [core.load[3 + j](lambda e: e.dma_start(CS[:, j, :, :], dram["dft_seq"][j].rearrange("(k p) n -> p k n", p=P)))
               for j in range(2)]
        uv = dram["uT"].rearrange("(c p) n -> p c n", p=P)
        T.wait(g)

        def body(i, marks):
            prev = lambda k: [marks[k].last_round()] if k in marks else []
            for b in range(2):
                ld = core.load[1 + b](lambda e: e.dma_start(uc[b][:], uv[:, :, bass.ds(i * 256 + 128 * b, 128)]), after=prev(f"t{b}"))
                T.wait(ld, *prev(f"ev{b}"))
                for ct in range(4):
                    t = T(lambda e: e.matmul(core.bank[:, 2 * b + ct // 2, 256 * (ct % 2):256 * (ct % 2) + 256], uc[b][:, ct, :],
                                             groups[:], start=True, stop=True), inc=ct == 3)
                marks[f"t{b}"] = T.last()
                for half in range(2):
                    for cs in range(2):
                        V(lambda e: e.tensor_copy(
                            AC[:, bass.ds(i * 2 + b, 1), cs, 256 * half:256 * half + 256].rearrange("p a (c n) -> p (a c) n", c=2),
                            core.bank[:, 2 * b + half, :].rearrange("p (c s n) -> p c s n", c=2, s=2)[:, :, cs, :]),
                          after=[T.last()])
                marks[f"ev{b}"] = V.last()
        core.loop(NT // 2, body)
        T.wait(*big)
        G.wait(V.last())

        def body(i, marks):
            prev = lambda k: [marks[k].last_round()] if k in marks else []
            for b in range(2):
                g = G(lambda e: e.tensor_copy(lhs[b][:].rearrange("p t s n -> p (t s) n"),
                                              AC[:, :, :, bass.ds(i * 256 + 128 * b, 128)].rearrange("p t s n -> p (t s) n")),
                      after=prev(f"t{b}"))
                T.wait(g, *prev(f"ev{b}"))
                for half in range(2):
                    core.mm(core.bank[:, 4 + 2 * b + half, :],
                            [(lambda k=k, s=s: lhs[b][:, k, s, :], lambda k=k, s=s: CS[:, s, k, 512 * half:512 * half + 512])
                             for k in range(KD) for s in range(2)])
                marks[f"t{b}"] = T.last()
                marks[f"ev{b}"] = A(lambda e: e.activation(mT[:, bass.ds(i * 2 + b, 1), :].rearrange("p a n -> p (a n)"),
                                                           core.bank[:, 4 + 2 * b:6 + 2 * b, :].rearrange("p a n -> p (a n)"),
                                                           ACT.Copy), after=[T.last()])
        core.loop(2, body)
        wf = sb("f_w", [P, 4, DF])
        bf = sb("f_b", [P, DF])
        z = [sb(f"f_z{b}", [P, DF]) for b in range(2)]
        o = [sb(f"f_o{b}", [P, DF]) for b in range(2)]
        l4 = [sb(f"f_l{b}", [P, 4, P]) for b in range(2)]
        core.load[0](lambda e: e.dma_start(wf[:], dram["w_fourier"].rearrange("(k p) n -> p k n", p=P)))
        got = core.load[0](lambda e: e.dma_start(bf[:], row(dram["b_fourier"])))
        T.wait(got)
        V.wait(got)
        G.wait(A.last())

        def body(i, marks):
            prev = lambda k: [marks[k].last_round()] if k in marks else []
            for b in range(2):
                lz = core.load[1 + b](lambda e: e.dma_start(z[b][:], dram["z"][bass.ds(i * 256 + 128 * b, 128), 0:DF]), after=prev(f"v{b}"))
                g = G(lambda e: e.tensor_copy(l4[b][:], mT[:, :, bass.ds(i * 256 + 128 * b, 128)]), after=prev(f"t{b}"))
                t = core.mm(core.bank[:, b, :], [(lambda k=k: l4[b][:, k, :], lambda k=k: wf[:, k, :]) for k in range(4)],
                            after=[g] + prev(f"v{b}"))
                marks[f"t{b}"] = t
                V(lambda e: e.tensor_tensor(o[b][:], core.bank[:, b, :], bf[:], ALU.add), after=[t] + prev(f"st{b}"))
                marks[f"v{b}"] = V(lambda e: e.tensor_tensor(o[b][:], o[b][:], z[b][:], ALU.mult), after=[lz], own=True)
                marks[f"st{b}"] = core.store[b](lambda e: e.dma_start(dram["mix"][bass.ds(i * 256 + 128 * b, 128), 0:DF], o[b][:]),
                                                after=[V.last()])
        core.loop(NT // 2, body)


def constants():
    k = np.arange(P)
    mats = np.stack([k[:, None] == k, k[:, None] <= k, k[:, None] >= k, k[:, None] > k, k[:, None] < k,
                     np.ones((P, P), bool)]).astype(np.float32)
    n = np.arange(SEQ)
    ang = 2 * np.pi * ((n[:, None] * n) % SEQ) / SEQ
    scale = 1.0 / np.sqrt(SEQ * 64.0)
    g = np.arange(64)
    small = 2 * np.pi * ((g[:, None] * g) % 64) / 64
    groups = np.zeros((P, 2, P))
    for b in range(2):
        groups[64 * b:64 * b + 64, 0, 64 * b:64 * b + 64] = np.cos(small)
        groups[64 * b:64 * b + 64, 1, 64 * b:64 * b + 64] = np.sin(small)
    return {"mats": mats, "dft_seq": np.stack([np.cos(ang) * scale, -np.sin(ang) * scale]).astype(np.float32),
            "dft_groups": groups.reshape(P, 256).astype(np.float32),
            "counts": np.concatenate([np.arange(4, 0, -1), np.arange(32, 0, -1), 128 * np.arange(8),
                                      np.arange(48)]).astype(np.float32),
            "rope_inv": (10000.0 ** (-np.arange(32, dtype=np.float64) / 32)).astype(np.float32),
            "far": np.stack([np.where(k[None, :] <= k[:, None], 0.0, FAR),
                             np.where(k[None, :] // 64 <= k[:, None] // 64, 0.0, FAR)]).astype(np.float32)}


def load_tables(core, sb, dram):
    t = {"mats": sb("mats", [P, 6, P]), "eps": sb("eps", [P, 1]), "dt": sb("dt", [P, NT + NC, 2 * NH]),
         "logits": sb("logits", [P, NT, 36]), "weight": sb("weight", [P, 2, NT]), "slot": sb("slot", [P, 2, NT], I32),
         "expert": sb("expert", [P, 48], I32)}
    core.V(lambda e: e.memset(t["eps"][:], EPS))
    core.load[0](lambda e: e.dma_start(t["mats"][:], dram["mats"].rearrange("m p n -> p m n")))
    core.settle()
    return t


def decays(core, dram, tables, sb):
    T, V, A = core.T, core.V, core.A
    n = NT + NC
    t = {k: sb("s_" + k, [P, n, 2 * NH]) for k in ("dt", "a", "ec", "dec", "et")}
    with Room(core) as s1:
        bias, an = s1("s_bias", [P, 2 * NH]), s1("s_an", [P, 2 * NH])
        p, q = s1("s_p", [P, n, 2 * NH]), s1("s_q", [P, n, 2 * NH])
        core.load[0](lambda e: e.dma_start(bias[:], row(dram["dt_bias"].rearrange("a h -> (a h)"))))
        got = core.load[0](lambda e: e.dma_start(an[:], row(dram["a_log"].rearrange("a h -> (a h)"))))
        a = A(lambda e: e.activation(an[:], an[:], ACT.Exp), after=[got])
        V(lambda e: e.tensor_tensor(p[:], tables["dt"][:], over(bias[:], 1, n), ALU.add), after=[got])
        V(lambda e: e.tensor_scalar(q[:], p[:], -1.0, None, ALU.mult), own=True)
        V(lambda e: e.tensor_tensor(q[:], q[:], p[:], ALU.min), own=True)
        A(lambda e: e.activation(q[:], q[:], ACT.Exp), after=[V.last()])
        A(lambda e: e.activation(q[:], q[:], ACT.Ln, bias=1.0), own=True)
        V(lambda e: e.scalar_tensor_tensor(out=t["dt"][:], in0=p[:], scalar=0.0, in1=q[:], op0=ALU.max, op1=ALU.add),
          after=[A.last()])
        V(lambda e: e.scalar_tensor_tensor(out=t["a"][:], in0=t["dt"][:], scalar=-1.0, in1=over(an[:], 1, n),
                                           op0=ALU.mult, op1=ALU.mult), own=True, after=[a])
        T.wait(V.last())
        mats = tables["mats"]
        T(lambda e: e.matmul(core.bank[:, 0, 0:480], mats[:, C_LE, :], t["a"][:].rearrange("p t h -> p (t h)"), start=True, stop=True), inc=False)
        T(lambda e: e.matmul(core.bank[:, 1, 0:480], mats[:, C_GE, :], t["a"][:].rearrange("p t h -> p (t h)"), start=True, stop=True), inc=False)
        T(lambda e: e.matmul(core.bank[:, 2, 0:480], mats[:, C_ONE, :], t["a"][:].rearrange("p t h -> p (t h)"), start=True, stop=True))
        for half in range(2):
            cols = slice(NH * half, NH * half + NH)
            cum = core.bank[:, half, 0:480].rearrange("p (t h) -> p t h", h=2 * NH)[:, :, cols]
            tot = core.bank[:, 2, 0:480].rearrange("p (t h) -> p t h", h=2 * NH)[:, :, cols]
            A(lambda e: e.activation(t["ec"][:, :, cols], cum, ACT.Exp), after=[T.last()])
            A(lambda e: e.activation(t["et"][:, :, cols], tot, ACT.Exp))
            V(lambda e: e.tensor_copy(p[:, :, cols], cum), own=True, after=[A.last()])
            V(lambda e: e.tensor_tensor(q[:, :, cols], tot, p[:, :, cols], ALU.subtract), own=True)
            A(lambda e: e.activation(q[:, :, cols], q[:, :, cols], ACT.Exp), after=[V.last()])
            V(lambda e: e.tensor_tensor(t["dec"][:, :, cols], q[:, :, cols], t["dt"][:, :, cols], ALU.mult), after=[A.last()])
    return t


def heads(ap):
    return ap.rearrange("p (h d) -> p h d", d=HP)


def state_space(core, dram, tables):
    T, V, A, G = core.T, core.V, core.A, core.G
    ident = tables["mats"][:, C_ID, :]
    with Room(core) as sb:
        t = decays(core, dram, tables, sb)
        xb = [sb(f"s_xb{b}", [P, CONV // P, P]) for b in range(2)]
        X = sb("s_X", [P, DS + NBC * NST])
        xd = sb("s_xd", [P, DS])
        H = sb("s_H", [P, DS])
        HB = sb("s_HB", [P, NT, DS])
        xv = dram["xbcT"].rearrange("(t p) n -> p t n", p=P)

        def load_chunk(b, tile, after):
            return core.load[1 + b](lambda e: e.dma_start(xb[b][:], xv[:, :, bass.ds(tile * P, P)]), after=after)

        def turn(b, got, free):
            for q in range(4):
                bank = 6 + q % 2
                core.tr([(lambda j=j: core.bank[:, bank, 128 * j:128 * j + 128], lambda j=j: xb[b][:, 4 * q + j, :])
                         for j in range(4)], ident, after=[got] + (free if q == 0 else []) + ([evac[q % 2]] if q > 1 else []))
                if q == 0:
                    evac = {}
                if q % 2 == 0:
                    evac[0] = A(lambda e: e.activation(X[:, 512 * q:512 * q + 512], core.bank[:, bank, :], ACT.Copy), after=[T.last()] + (free if q == 0 else []))
                else:
                    evac[1] = V(lambda e: e.tensor_copy(X[:, 512 * q:512 * q + 512], core.bank[:, bank, :]), after=[T.last()] + (free if q == 1 else []))
            return [evac[0], evac[1]]

        def state_step(tile, way, ready):
            cols = slice(NH * way, NH * way + NH)
            v = V(lambda e: e.tensor_tensor(heads(xd[:]), heads(X[:, 0:DS]),
                                            over(t["dec"][:, bass.ds(tile, 1), cols].rearrange("p a h -> p (a h)"), 2, HP), ALU.mult),
                  after=ready)
            for g in range(NBC):
                core.mm(core.bank[:, 2 + g, 0:384], [(lambda: X[:, DS + NST * g:DS + NST * g + NST],
                                                      lambda: xd[:, 384 * g:384 * g + 384])], after=[v])
            V(lambda e: e.tensor_tensor(heads(H[:]), heads(H[:]),
                                        over(t["et"][:, bass.ds(tile, 1), cols].rearrange("p a h -> p (a h)"), 2, HP), ALU.mult), own=True)
            return V(lambda e: e.tensor_tensor(H[:].rearrange("p (g n) -> p g n", g=NBC), H[:].rearrange("p (g n) -> p g n", g=NBC),
                                               core.bank[:, 2:6, 0:384], ALU.add), own=True, after=[T.last()])

        V(lambda e: e.memset(H[:], 0.0))
        done = [V.last()]
        for tile in (9, 8):
            got = load_chunk(tile % 2, tile, [])
            done = [state_step(tile, 1, turn(tile % 2, got, done + [T.last()]))]

        if "hb" in dram:
            core.store[7](lambda e: e.dma_start(dram["hb"], H[:]), after=done)
            core.settle()
        T.wait(*done)
        A.wait(*done)
        core.load[1].wait(*done)

        def body(i, marks):
            prev = lambda k: [marks[k].last_round()] if k in marks else []
            for b in range(2):
                tile = i * -2 + (NT - 1 - b)
                got = load_chunk(b, tile, prev(f"turn{b}"))
                free = ([marks["step0"]] if b and "step0" in marks else prev("step1"))
                ready = turn(b, got, free + ([T.last()] if b else prev("mm")))
                marks[f"turn{b}"] = T.last()
                G(lambda e: e.tensor_copy(HB[:, bass.ds(tile, 1), :].rearrange("p a n -> p (a n)"), H[:]), after=free)
                marks[f"step{b}"] = state_step(tile, 1, ready + [G.last()])
                marks["mm"] = T.last()
        core.loop(NT // 2, body)
        core.settle()

        V(lambda e: e.memset(H[:], 0.0))
        done = [V.last()]
        for tile in (8, 9):
            got = load_chunk(tile % 2, tile, [])
            done = [state_step(tile, 0, turn(tile % 2, got, done + [T.last()]))]
        if "hf" in dram:
            core.store[7](lambda e: e.dma_start(dram["hf"], H[:]), after=done)
            core.settle()

        LE, GE = tables["mats"][:, C_LE, :], tables["mats"][:, C_GE, :]
        cb = sb("s_cb", [P, 2, NBC, P])
        xf = [sb(f"s_xf{w}", [P, DS]) for w in range(2)]
        R = [sb(f"s_R{w}", [P, HG, P]) for w in range(2)]
        E = [sb(f"s_E{b}", [P, HG, P]) for b in range(2)]
        M = [[sb(f"s_M{b}{w}", [P, HG, P]) for w in range(2)] for b in range(2)]
        yt = sb("s_y", [P, DS])
        y2 = sb("s_y2", [P, 384])
        skip = sb("s_skip", [P, NH])
        nw = sb("s_nw", [P, DS])
        zt = [sb(f"s_z{b}", [P, DS]) for b in range(2)]
        ss, sd, rs = (sb(f"s_{k}", [P, NBC]) for k in ("ss", "sd", "rs"))
        core.load[0](lambda e: e.dma_start(skip[:], row(dram["d_skip"])))
        got = core.load[0](lambda e: e.dma_start(nw[:], row(dram["ssd_norm_w"])))
        for e in core.engines:
            e.wait_ge(core.load[0].sem, core.load[0].n)
            for x in (T, V, A):
                e.wait_ge(x.sem, x.n)

        def chunk(i, b, marks):
            prev = lambda k: [marks[k].last_round()] if k in marks else []
            before = lambda k: ([marks[k + "0"]] if k + "0" in marks else []) if b else prev(k + "1")
            tile = i * 2 + b
            got = load_chunk(b, tile, prev(f"off{b}"))
            lz = core.load[3 + b](lambda e: e.dma_start(zt[b][:], dram["z"][bass.ds(tile * P, P), DF:DF + DS]), after=prev(f"gate{b}"))
            ready = turn(b, got, before("step") + before("ytoff") + before("skip") + [x for x in before("state_mm")])
            dcol = lambda name, w: t[name][:, bass.ds(tile, 1), NH * w:NH * w + NH].rearrange("p a h -> p (a h)")
            for g in range(NBC):
                core.mm(core.bank[:, 5, 128 * g:128 * g + 128], [(lambda: xb[b][:, 12 + g, :], lambda: xb[b][:, 16 + g, :])],
                        after=before("step") if g == 0 else [])
            cbt = T.last()
            for w, mask in ((0, LE), (1, GE)):
                V(lambda e: e.tensor_tensor(cb[:, w, :, :], core.bank[:, 5, :].rearrange("p (g n) -> p g n", g=NBC),
                                            over(mask, 1, NBC), ALU.mult), after=[cbt] + before("M"))
            cbv = V.last()
            xfs = [V(lambda e: e.tensor_tensor(heads(xf[0][:]), heads(X[:, 0:DS]), over(dcol("dt", 0), 2, HP), ALU.mult), after=ready),
                   G(lambda e: e.tensor_tensor(heads(xf[1][:]), heads(X[:, 0:DS]), over(dcol("dt", 1), 2, HP), ALU.mult), after=ready + before("off"))]
            G(lambda e: e.tensor_tensor(heads(yt[:]), heads(X[:, 0:DS]), over(skip[:], 2, HP), ALU.mult), after=before("st"))
            skipped = G.last()
            marks[f"skip{b}"] = skipped
            mask_of = (LE, GE)
            evE, dT, mE, offs = {}, {}, {}, {}

            def differences(g):
                rs_ = []
                for w, Q in ((0, V), (1, G)):
                    a = t["a"][:, bass.ds(tile, 1), NH * w + HG * g:NH * w + HG * g + HG].rearrange("p a h -> p (a h)")
                    rs_.append(Q(lambda e: e.tensor_tensor(R[w][:], over(mask_of[w], 1, HG), over(a, 2, P), ALU.mult),
                                 after=[dT[g - 1]] if g else before("lastD")))
                T.wait(*rs_, *([evE[g - 1]] if g else before("lastE")))
                for half in range(2):
                    for w, m in ((0, C_GT), (1, C_LT)):
                        T(lambda e: e.matmul(core.bank[:, half, 0:384], tables["mats"][:, m, :],
                                             R[w][:, 3 * half:3 * half + 3, :].rearrange("p h n -> p (h n)"),
                                             start=w == 0, stop=w == 1), inc=half == 1 and w == 1)
                dT[g] = T.last()
                s = g % 2
                evE[g] = A(lambda e: e.activation(E[s][:].rearrange("p (a h) n -> p a (h n)", a=2), core.bank[:, 0:2, 0:384], ACT.Exp),
                           after=[dT[g]] + ([mE[g - 2]] if g > 1 else before("M")) + ([mG[g - 2]] if g > 1 else before("MG")))

            mG, yT = {}, {}

            def weights(g):
                s = g % 2
                free = [yT[g - 2]] if g > 1 else before("off")
                mE[g] = V(lambda e: e.tensor_tensor(M[s][0][:], E[s][:], over(cb[:, 0, g, :], 1, HG), ALU.mult), after=[evE[g], cbv] + free)
                mG[g] = G(lambda e: e.tensor_tensor(M[s][1][:], E[s][:], over(cb[:, 1, g, :], 1, HG), ALU.mult), after=[evE[g], cbv] + free)

            def outputs(g):
                s = g % 2
                T.wait(mE[g], mG[g], *xfs, *([offs[g - 1]] if g else before("ytoff")))
                for h in range(HG):
                    c0 = HP * (HG * g + h)
                    for w in range(2):
                        T(lambda e: e.matmul(core.bank[:, 2, HP * h:HP * h + HP], M[s][w][:, h, :], xf[w][:, c0:c0 + HP],
                                             start=w == 0, stop=w == 1), inc=False)
                T(lambda e: e.matmul(core.bank[:, 3, 0:384], xb[b][:, 16 + g, :], H[:, 384 * g:384 * g + 384], start=True, stop=True), inc=False)
                T(lambda e: e.matmul(core.bank[:, 4, 0:384], xb[b][:, 16 + g, :],
                                     HB[:, bass.ds(tile, 1), 384 * g:384 * g + 384].rearrange("p a n -> p (a n)"), start=True, stop=True))
                yT[g] = T.last()
                ec = lambda w: over(t["ec"][:, bass.ds(tile, 1), NH * w + HG * g:NH * w + HG * g + HG].rearrange("p a h -> p (a h)"), 2, HP)
                y = yt[:, 384 * g:384 * g + 384]
                V(lambda e: e.tensor_tensor(y, y, core.bank[:, 2, 0:384], ALU.add), after=[yT[g], skipped])
                for w in range(2):
                    V(lambda e: e.tensor_tensor(heads(y2[:]), heads(core.bank[:, 3 + w, 0:384]), ec(w), ALU.mult), own=True)
                    V(lambda e: e.tensor_tensor(y, y, y2[:], ALU.add), own=True)
                offs[g] = V.last()

            differences(0)
            for g in range(NBC):
                weights(g)
                if g + 1 < NBC:
                    differences(g + 1)
                outputs(g)
            marks[f"M{b}"], marks[f"MG{b}"], marks[f"lastD{b}"], marks[f"lastE{b}"] = mE[3], mG[3], dT[3], evE[3]
            marks[f"off{b}"], marks[f"ytoff{b}"] = yT[3], offs[3]
            marks[f"step{b}"] = state_step(tile, 0, ready + [yT[3]])
            marks[f"state_mm{b}"] = T.last()
            V(lambda e: e.tensor_tensor(yt[:], yt[:], zt[b][:], ALU.mult), own=True, after=[lz])
            marks[f"gate{b}"] = V.last()
            for g in range(NBC):
                A(lambda e: e.activation(y2[:], yt[:, 384 * g:384 * g + 384], ACT.Square, accum_out=ss[:, g:g + 1]), after=[V.last()], own=True)
            a = A(lambda e: e.activation(sd[:], ss[:], ACT.Sqrt, bias=tables["eps"][:, 0:1], scale=1.0 / 384), own=True)
            V(lambda e: e.reciprocal(rs[:], sd[:]), after=[a])
            V(lambda e: e.tensor_tensor(yt[:].rearrange("p (g n) -> p g n", g=NBC), yt[:].rearrange("p (g n) -> p g n", g=NBC),
                                        over(rs[:], 2, 384), ALU.mult), own=True)
            V(lambda e: e.tensor_tensor(yt[:], yt[:], nw[:], ALU.mult), own=True)
            marks[f"st{b}"] = core.store[b](lambda e: e.dma_start(dram["mix"][bass.ds(tile * P, P), DF:DF + DS], yt[:]), after=[V.last()])

        def body(i, marks):
            for b in range(2):
                chunk(i, b, marks)
        core.loop(NT // 2, body)


def prev_of(marks):
    return lambda k: [marks[k].last_round()] if k in marks else []


def turn_rows(core, out, src, n, ident, banks, after, free):
    for q in range((n + 3) // 4):
        m = min(4, n - 4 * q)
        bank = banks[q % len(banks)]
        wait = ([] if q else list(after)) + (free[q % len(banks)] if q < len(banks) else [evs[q - len(banks)]])
        if q == 0:
            evs = []
        t = core.tr([(lambda j=j: core.bank[:, bank, 128 * j:128 * j + 128],
                      lambda j=j: src[:, 128 * (4 * q + j):128 * (4 * q + j) + 128]) for j in range(m)], ident, after=wait)
        evs.append(core.A(lambda e: e.activation(out[:, 4 * q:4 * q + m, :],
                                                 core.bank[:, bank, 0:128 * m].rearrange("p (j n) -> p j n", j=m), ACT.Copy), after=[t]))
    return t, evs[-1]


def close_first(core, dram, tables):
    T, V, A = core.T, core.V, core.A
    ident = tables["mats"][:, C_ID, :]
    with Room(core) as sb:
        KM = 2 * D // P
        w = sb("c_w", [P, KM, D])
        gate, fin, gain, shift = (sb("c_" + k, [P, D]) for k in ("gate", "fin", "gain", "shift"))
        x, y, x1, h = (sb("c_" + k, [P, D]) for k in ("x", "y", "x1", "h"))
        mix = [sb(f"c_mix{b}", [P, 2 * D]) for b in range(2)]
        mT = sb("c_mT", [P, KM, P])
        norm = Norm(core, sb, "c_n")
        wl = [core.load[5 + j](lambda e: e.dma_start(w[:, 4 * j:4 * j + 4, :], dram["w_out"].rearrange("(k p) n -> p k n", p=P)[:, 4 * j:4 * j + 4, :]))
              for j in range(4)]
        core.load[9](lambda e: e.dma_start(gate[:], row(dram["mods"][0, 2 * D:3 * D])))
        gl = core.load[9](lambda e: e.dma_start(fin[:], row(dram["final_norm_w"])))
        m2 = dram["mod2"][0, :]
        gain_rows(core, gain[:], dram["norm1_g_2"], m2[D:2 * D], shift[:], m2[0:D], y[:])
        V.wait(gl)
        T.wait(*wl)

        def body(i, marks):
            for b in range(2):
                before = lambda k: ([marks[k + "0"]] if k + "0" in marks else []) if b else prev_of(marks)(k + "1")
                at = bass.ds(i * 256 + 128 * b, 128)
                lm = core.load[1 + b](lambda e: e.dma_start(mix[b][:], dram["mix"][at, :]), after=prev_of(marks)(f"t{b}"))
                lx = core.load[3](lambda e: e.dma_start(x[:], dram["x"][at, :]), after=before("x"))
                t, ev = turn_rows(core, mT, mix[b][:], KM, ident, (4, 5), [lm], [before("evt"), before("evt")])
                marks[f"t{b}"], marks[f"evt{b}"] = t, ev
                T.wait(ev, *before("mul"))
                for half in range(2):
                    core.mm(core.bank[:, half, :], [(lambda k=k: mT[:, k, :], lambda k=k: w[:, k, 512 * half:512 * half + 512]) for k in range(KM)])
                marks[f"mm{b}"] = T.last()
                marks[f"mul{b}"] = V(lambda e: e.tensor_tensor(y[:], core.bank[:, 0:2, :].rearrange("p a n -> p (a n)"), gate[:], ALU.mult),
                                     after=[T.last()], own=True)
                marks[f"x{b}"] = V(lambda e: e.tensor_tensor(y[:], y[:], x[:], ALU.add), after=[lx], own=True)
                V.wait(norm.rstd(y[:], tables["eps"][:, 0:1], [V.last()]))
                norm.apply(x1[:], y[:], fin[:], after=before("stx"))
                marks[f"stx{b}"] = core.store[0](lambda e: e.dma_start(dram["x1"][at, :], x1[:]), after=[V.last()])
                V.wait(norm.rstd(x1[:], tables["eps"][:, 0:1], [V.last()]))
                norm.apply(h[:], x1[:], gain[:], shift[:], after=before("sth"))
                marks[f"sth{b}"] = core.store[1](lambda e: e.dma_start(dram["h1"][at, :], h[:]), after=[V.last()])
        core.loop(NT // 2, body)


COLS2 = 4816
C_FQ, C_FK, C_FV, C_FL, C_DQ, C_DK, C_DV, C_IQ, C_IK, C_IW, C_GF = 0, 512, 1024, 1536, 1544, 2056, 2120, 2184, 2696, 2760, 2768


def project_second(core, dram, tables):
    T, V, A = core.T, core.V, core.A
    ident = tables["mats"][:, C_ID, :]
    with Room(core) as sb:
        hT = sb("p_hT", [P, KD, SEQ])
        h = [sb(f"p_h{b}", [P, D]) for b in range(2)]
        w = [sb(f"p_w{b}", [P, KD, 512]) for b in range(2)]
        o = [sb(f"p_o{b}", [P, 512]) for b in range(4)]
        wv = dram["w_in_2"].rearrange("(k p) n -> p k n", p=P)

        def body(i, marks):
            prev = prev_of(marks)
            for b in range(2):
                ld = core.load[1 + b](lambda e: e.dma_start(h[b][:], dram["h1"][bass.ds(i * 256 + 128 * b, 128), :]), after=prev(f"t{b}"))
                for half in range(2):
                    t = core.tr([(lambda k=k: core.bank[:, 2 * b + half, 128 * k:128 * k + 128],
                                  lambda k=k: h[b][:, 512 * half + 128 * k:512 * half + 128 * k + 128]) for k in range(4)], ident,
                                after=[ld] + prev(f"ev{b}"))
                    marks[f"t{b}"] = t
                    marks[f"ev{b}"] = A(lambda e: e.activation(hT[:, 4 * half:4 * half + 4, bass.ds(i * 256 + 128 * b, 128)],
                                                               core.bank[:, 2 * b + half, :].rearrange("p (k n) -> p k n", k=4),
                                                               ACT.Copy), after=[t])
        core.loop(NT // 2, body)
        core.settle()

        def chunk(b, at, n, marks, prev):
            lw = core.load[3 + b](lambda e: e.dma_start(w[b][:, :, 0:n], wv[:, :, at]), after=prev(f"mm{b}"))
            T.wait(lw)
            for m in range(NT):
                j = NT * b + m
                s = j % 4
                old = lambda k: ([marks[f"{k}{j - 4}"]] if f"{k}{j - 4}" in marks else []) if j >= 4 else prev(f"{k}{j + 12}")
                t = core.mm(core.bank[:, s, 0:n], [(lambda k=k: hT[:, k, 128 * m:128 * m + 128], lambda k=k: w[b][:, k, 0:n])
                                                   for k in range(KD)], after=old("ev"))
                marks[f"mm{b}"] = t
                Q, f = (A, lambda e: e.activation(o[s][:, 0:n], core.bank[:, s, 0:n], ACT.Copy)) if s % 2 else \
                       (V, lambda e: e.tensor_copy(o[s][:, 0:n], core.bank[:, s, 0:n]))
                marks[f"ev{j}"] = Q(f, after=[t] + old("st"))
                marks[f"st{j}"] = core.store[s](lambda e: e.dma_start(dram["proj"][128 * m:128 * m + 128, at], o[s][:, 0:n]), after=[Q.last()])

        def body(i, marks):
            for b in range(2):
                chunk(b, bass.ds(i * 1024 + 512 * b, 512), 512, marks, prev_of(marks))
        core.loop(4, body)
        core.settle()
        marks = {}
        chunk(0, slice(4096, 4608), 512, marks, lambda k: [])
        for s in range(4):
            marks[f"ev{NT - 4 + s}"], marks[f"st{NT - 4 + s}"] = marks[f"ev{NT - 4 + s}"], marks[f"st{NT - 4 + s}"]
        chunk(1, slice(4608, COLS2), COLS2 - 4608, marks, lambda k: [])


ROPE_C1, ROPE_C2, ROPE_C3 = 6.28125, 0.0019353071693331003, 1.0253131677018246e-11
MAGIC = 1.5 * 2 ** 23


def prepare_heads(core, dram, tables):
    T, V, A, G = core.T, core.V, core.A, core.G
    ident = tables["mats"][:, C_ID, :]
    with Room(core) as sb:
        ld = core.load
        gq, gk, dgq, dgk = (sb("h_" + k, [P, 64]) for k in ("gq", "gk", "dgq", "dgk"))
        bf = sb("h_bf", [P, 8])
        inv = sb("h_inv", [P, 32])
        posi, pos = sb("h_posi", [P, NT], I32), sb("h_pos", [P, NT])
        for t, k in ((gq, "qn_fox_2"), (gk, "kn_fox_2"), (dgq, "qn_dsa_2"), (dgk, "kn_dsa_2"), (bf, "b_fgt_2"), (inv, "rope_inv")):
            ld[0](lambda e: e.dma_start(t[:], row(dram[k])))
        with core.nc.allow_non_contiguous_dma(reason="one position a partition"):
            got = ld[0](lambda e: e.dma_start(posi[:], dram["positions_2"].rearrange("(t p) -> p t", p=P)))
        ang, red, kk = (sb("h_" + k, [P, NT, 32]) for k in ("ang", "red", "kk"))
        cos, sin = sb("h_cos", [P, NT, 32]), sb("h_sin", [P, NT, 32])
        V(lambda e: e.tensor_copy(pos[:], posi[:]), after=[got])
        V(lambda e: e.tensor_tensor(ang[:], over(pos[:], 2, 32), over(inv[:], 1, NT), ALU.mult), own=True)
        for table, turn in ((sin, 0.0), (cos, 0.25)):
            V(lambda e: e.tensor_scalar(kk[:], ang[:], 1.0 / (2 * np.pi), turn, ALU.mult, ALU.add), own=True)
            V(lambda e: e.tensor_scalar(kk[:], kk[:], MAGIC, None, ALU.add), own=True)
            V(lambda e: e.tensor_scalar(kk[:], kk[:], -MAGIC, None, ALU.add), own=True)
            V(lambda e: e.scalar_tensor_tensor(out=red[:], in0=kk[:], scalar=-ROPE_C1, in1=ang[:], op0=ALU.mult, op1=ALU.add), own=True, after=[A.last()])
            V(lambda e: e.scalar_tensor_tensor(out=red[:], in0=kk[:], scalar=-ROPE_C2, in1=red[:], op0=ALU.mult, op1=ALU.add), own=True)
            V(lambda e: e.scalar_tensor_tensor(out=red[:], in0=kk[:], scalar=-ROPE_C3, in1=red[:], op0=ALU.mult, op1=ALU.add), own=True)
            if turn:
                V(lambda e: e.tensor_scalar(red[:], red[:], 2 * np.pi * turn, None, ALU.add), own=True)
            V(lambda e: e.tensor_scalar(red[:], red[:], 3.1415925, -3.1415925, ALU.min, ALU.max), own=True)
            A(lambda e: e.activation(table[:], red[:], ACT.Sin), after=[V.last()])
        V.wait(A.last())
        core.settle()

        x = [sb(f"h_x{b}", [P, C_GF]) for b in range(2)]
        sq = sb("h_sq", [P, 2 * 512])
        ss, sd, rs = (sb("h_" + k, [P, 26]) for k in ("ss", "sd", "rs"))
        r1, r2, r3 = (sb("h_" + k, [P, 8, 32]) for k in ("r1", "r2", "r3"))
        lf, l2, ft, carry = (sb("h_" + k, [P, 8]) for k in ("lf", "l2", "ft", "carry"))
        qT = sb("h_qT", [P, 17, P])
        V(lambda e: e.memset(carry[:], 0.0))
        V.wait(V.last())

        h3 = lambda ap, n=64: ap.rearrange("p (h d) -> p h d", d=n)

        def tile(b, i, marks):
            before = lambda k: ([marks[k + "0"]] if k + "0" in marks else []) if b else prev_of(marks)(k + "1")
            at = bass.ds(i * 256 + 128 * b, 128)
            ti = i * 2 + b
            X = x[b]
            got = ld[1 + b](lambda e: e.dma_start(X[:], dram["proj"][at, 0:C_GF]), after=prev_of(marks)(f"t{b}"))
            A(lambda e: e.activation(sq[:], X[:, C_FQ:C_FV], ACT.Square), after=[got] + before("sq2"))
            V(lambda e: e.tensor_reduce(ss[:, 0:16], h3(sq[:]), AX.X, ALU.add), after=[A.last()])
            A(lambda e: e.activation(sq[:, 0:576], X[:, C_DQ:C_DV], ACT.Square), after=[V.last()])
            v = V(lambda e: e.tensor_reduce(ss[:, 16:25], h3(sq[:, 0:576]), AX.X, ALU.add), after=[A.last()], own=True)
            marks[f"sq2{b}"] = v
            A(lambda e: e.activation(sd[:, 0:25], ss[:, 0:25], ACT.Sqrt, bias=tables["eps"][:, 0:1], scale=1.0 / 64), after=[v])
            V(lambda e: e.reciprocal(rs[:, 0:25], sd[:, 0:25]), after=[A.last()])
            for c, r0, nh, gain, scale in ((C_FQ, 0, 8, gq, 0.125), (C_FK, 8, 8, gk, 1.0), (C_DQ, 16, 8, dgq, 0.125), (C_DK, 24, 1, dgk, 1.0)):
                blk = h3(X[:, c:c + 64 * nh])
                V(lambda e: e.tensor_tensor(blk, blk, over(rs[:, r0:r0 + nh], 2, 64), ALU.mult), own=True)
                V(lambda e: e.scalar_tensor_tensor(out=blk, in0=blk, scalar=scale, in1=over(gain[:], 1, nh), op0=ALU.mult, op1=ALU.mult), own=True)
            for c, nh in ((C_DQ, 8), (C_DK, 1), (C_IQ, 8), (C_IK, 1)):
                blk = h3(X[:, c:c + 64 * nh])
                a, bb = blk[:, :, 0:32], blk[:, :, 32:64]
                cs = over(cos[:, bass.ds(ti, 1), :].rearrange("p a n -> p (a n)"), 1, nh)
                sn = over(sin[:, bass.ds(ti, 1), :].rearrange("p a n -> p (a n)"), 1, nh)
                V(lambda e: e.tensor_tensor(r1[:, 0:nh, :], a, sn, ALU.mult), own=True)
                V(lambda e: e.tensor_tensor(r2[:, 0:nh, :], bb, sn, ALU.mult), own=True)
                V(lambda e: e.tensor_tensor(r3[:, 0:nh, :], a, cs, ALU.mult), own=True)
                V(lambda e: e.tensor_tensor(bb, bb, cs, ALU.mult), own=True)
                V(lambda e: e.tensor_tensor(a, r3[:, 0:nh, :], r2[:, 0:nh, :], ALU.subtract), own=True)
                V(lambda e: e.tensor_tensor(bb, bb, r1[:, 0:nh, :], ALU.add), own=True)
            ready = V.last()
            V(lambda e: e.tensor_tensor(lf[:], X[:, C_FL:C_FL + 8], bf[:], ALU.add), own=True, after=before("ft"))
            V(lambda e: e.tensor_scalar(l2[:], lf[:], -1.0, None, ALU.mult), own=True)
            V(lambda e: e.tensor_tensor(l2[:], l2[:], lf[:], ALU.min), own=True)
            A(lambda e: e.activation(l2[:], l2[:], ACT.Exp), after=[V.last()])
            A(lambda e: e.activation(l2[:], l2[:], ACT.Ln, bias=1.0), own=True)
            V(lambda e: e.tensor_scalar(lf[:], lf[:], 0.0, None, ALU.min), own=True)
            V(lambda e: e.tensor_tensor(lf[:], lf[:], l2[:], ALU.subtract), own=True, after=[A.last()])
            T.wait(V.last(), *before("carry"))
            T(lambda e: e.matmul(core.bank[:, 0, 0:8], tables["mats"][:, C_LE, :], lf[:], start=True, stop=True), inc=False)
            T(lambda e: e.matmul(core.bank[:, 0, 8:16], tables["mats"][:, C_ONE, :], lf[:], start=True, stop=True))
            V(lambda e: e.scalar_tensor_tensor(out=ft[:], in0=core.bank[:, 0, 0:8], scalar=-1.0, in1=carry[:], op0=ALU.mult, op1=ALU.subtract), after=[T.last()])
            V(lambda e: e.tensor_tensor(carry[:], carry[:], core.bank[:, 0, 8:16], ALU.add), own=True)
            marks[f"carry{b}"] = V.last()
            blocks = [X[:, C_FQ + 128 * j:C_FQ + 128 * j + 128] for j in range(8)] + [X[:, C_DQ + 128 * j:C_DQ + 128 * j + 128] for j in range(4)] \
                + [X[:, C_IQ + 128 * j:C_IQ + 128 * j + 128] for j in range(4)]
            T.wait(ready)
            evs = []
            for q in range(4):
                bank = 1 + q
                t = core.tr([(lambda j=j: core.bank[:, bank, 128 * j:128 * j + 128], lambda j=j: blocks[4 * q + j]) for j in range(4)],
                            ident, after=before(f"ev{q}"))
                marks[f"ev{q}{b}"] = A(lambda e: e.activation(qT[:, 4 * q:4 * q + 4, :], core.bank[:, bank, :].rearrange("p (j n) -> p j n", j=4),
                                                              ACT.Copy), after=[t] + (before("st") if q == 0 else []))
            core.tr([(lambda: core.bank[0:8, 5, 256:384], lambda: ft[:]),
                     (lambda: core.bank[0:64, 5, 0:128], lambda: X[:, C_DK:C_DK + 64]),
                     (lambda: core.bank[0:64, 5, 128:256], lambda: X[:, C_IK:C_IK + 64])], ident, after=before("ev4") + [V.last()])
            marks[f"t{b}"] = T.last()
            marks[f"ft{b}"] = T.last()
            A(lambda e: e.activation(kx[0:64, :], core.bank[0:64, 5, 0:256], ACT.Copy), after=[T.last()] + before("st2"))
            marks[f"ev4{b}"] = A(lambda e: e.activation(fx[0:8, :], core.bank[0:8, 5, 256:384], ACT.Copy))
            for hh in range(2):
                half = slice(64 * hh, 64 * hh + 64)
                for name, j0 in (("fqT", 0), ("fkT", 4), ("dqT", 8), ("iqT", 12)):
                    core.store[0](lambda e: e.dma_start(dram[name][hh::2, 0:64, at].rearrange("h d n -> d h n"), qT[half, j0:j0 + 4, :]),
                                  after=[marks[f"ev3{b}"]])
            marks[f"st{b}"] = core.store[0].last()
            core.store[1](lambda e: e.dma_start(dram["dkT"][:, at], kx[0:64, 0:128]), after=[A.last()])
            core.store[1](lambda e: e.dma_start(dram["ikT"][:, at], kx[0:64, 128:256]))
            marks[f"st2{b}"] = core.store[1](lambda e: e.dma_start(dram["fkT"][:, 64, at], fx[0:8, :]))

        kx, fx = sb("h_kx", [64, 256]), sb("h_fx", [8, P])

        def body(i, marks):
            for b in range(2):
                tile(b, i, marks)
        core.loop(NT // 2, body)


TOPK, NAH, HD = 256, 8, 64
DONE = -3e38


def attend(core, dram, tables):
    T, V, A = core.T, core.V, core.A
    ident = tables["mats"][:, C_ID, :]
    with Room(core) as sb:
        far = sb("a_far", [P, 2, SEQ])
        fkT, dkT, ikT = sb("a_fkT", [HD + 1, NAH, SEQ]), sb("a_dkT", [HD, SEQ]), sb("a_ikT", [HD, SEQ])
        fv, dv, iw = sb("a_fv", [P, NT, 512]), sb("a_dv", [P, NT, HD]), sb("a_iw", [P, NT, NAH])
        qt = {k: [sb(f"a_{k}{b}", [HD + 1, NAH, P]) for b in range(2)] for k in ("fox", "dsa", "idx")}
        Sm, Pb, R = ([sb(f"a_{k}{b}", [P, SEQ]) for b in range(2)] for k in ("Sm", "Pb", "R"))
        PT = [sb(f"a_PT{b}", [P, NT, P]) for b in range(2)]
        score = [sb(f"a_score{b}", [P, SEQ]) for b in range(3)]
        best = sb("a_best", [P, 8])
        mx, nm, sm, rc = ([sb(f"a_{k}{b}", [P, 1]) for b in range(4)] for k in ("mx", "nm", "sm", "rc"))
        ob = {k: [sb(f"a_o{k}{b}", [P, 512]) for b in range(2)] for k in ("fox", "dsa")}

        V(lambda e: e.memset(far[:], 0.0))
        for b in range(2):
            V(lambda e: e.memset(qt["fox"][b][HD:HD + 1, :, :], 1.0))
        ld = core.load
        ld[0](lambda e: e.dma_start(fkT[:], dram["fkT"].rearrange("h d n -> d h n")), after=[V.last()])
        ld[0](lambda e: e.dma_start(dkT[:], dram["dkT"]))
        ld[0](lambda e: e.dma_start(ikT[:], dram["ikT"]))
        pv = dram["proj"].rearrange("(t p) n -> p t n", p=P)
        ld[0](lambda e: e.dma_start(fv[:], pv[:, :, C_FV:C_FV + 512]))
        ld[0](lambda e: e.dma_start(dv[:], pv[:, :, C_DV:C_DV + HD]))
        ld[0](lambda e: e.dma_start(iw[:], pv[:, :, C_IW:C_IW + NAH]))
        got = ld[0](lambda e: e.dma_start(far[:, :, SEQ - P:SEQ], dram["far"].rearrange("m p n -> p m n")))
        T.wait(got)
        V.wait(got)

        order = [("idx", 2), ("fox", 0), ("fox", 1), ("fox", 2), ("dsa", 0), ("dsa", 1), ("fox", 3), ("idx", 3), ("fox", 4), ("dsa", 2), ("idx", 4),
                 ("fox", 5), ("dsa", 3), ("idx", 5), ("fox", 6), ("idx", 6), ("dsa", 4), ("fox", 7), ("idx", 7), ("dsa", 5),
                 ("dsa", 6), ("dsa", 7)]
        units = [(kind, j, h) for kind, j in order for h in range(NAH)]
        qload, qfree, count = {}, {}, {}
        done = {k: {} for k in "SEXNO"}
        done["N"] = {}
        scored, biased, bias_read, stored = {}, {}, {}, {}
        pending = []

        def load_queries(kind, j):
            n = count[kind] = count.get(kind, -1) + 1
            src = dram[{"fox": "fqT", "dsa": "dqT", "idx": "iqT"}[kind]]
            stream = ld[1 + 2 * ("fox", "dsa", "idx").index(kind) + n % 2]
            buf = qt[kind][n % 2]
            qload[kind, j] = (buf, stream(lambda e: e.dma_start(buf[0:HD, :, :], src[:, :, P * j:P * j + P].rearrange("h d n -> d h n")),
                                          after=[qfree[kind, n - 2]] if n > 1 else [V.last()]))
            qfree[kind, j, "n"] = n

        def round_of(j):
            s = score[j % 3][:, 0:P * (j + 1)]
            def go(last):
                V(lambda e: e.max(best[:], s), own=True, after=scored[j])
                V(lambda e: e.match_replace(s, best[:], s, DONE), own=True)
                if last:
                    biased[j] = V(lambda e: e.tensor_scalar(s, s, DONE, FAR, ALU.is_gt, ALU.mult), own=True)
            return go

        def fill(n=None, until=None):
            while pending and (n is None or n > 0) and (until is None or until not in biased):
                j, go, last = pending.pop(0)
                go(last)
                n = None if n is None else n - 1

        def step_s(n):
            kind, j, h = units[n]
            L = P * (j + 1)
            if h == 0 and (kind, j) not in qload:
                load_queries(kind, j)
            buf, got = qload[kind, j]
            T.wait(got, *done["E"].get(n - 2, []))
            depth = HD + 1 if kind == "fox" else HD
            for c in range(0, L, 512):
                m = min(512, L - c)
                keys = {"fox": lambda: fkT[:, h, c:c + m], "dsa": lambda: dkT[:, c:c + m], "idx": lambda: ikT[:, c:c + m]}[kind]
                core.mm(core.bank[:, 2 * (n % 2) + c // 512, 0:m], [(lambda: buf[0:depth, h, :], keys)])
            done["S"][n] = T.last()
            if h == NAH - 1:
                qfree[kind, qfree[kind, j, "n"]] = T.last()
                later = [u for u in order[order.index((kind, j)) + 1:] if u[0] == kind]
                if later:
                    load_queries(kind, later[0][1])

        def step_e(n):
            kind, j, h = units[n]
            L = P * (j + 1)
            b = n % 2
            S = core.bank[:, 2 * b:2 * b + 2, :].rearrange("p a n -> p (a n)")[:, 0:L]
            if kind == "idx":
                s = score[j % 3][:, 0:L]
                a = A(lambda e: e.activation(R[b][:, 0:L], S, ACT.Relu), after=[done["S"][n]] + done["N"].get(b, []))
                w = iw[:, j, h:h + 1]
                if h == 0:
                    v = V(lambda e: e.tensor_scalar(s, R[b][:, 0:L], w, None, ALU.mult), after=[a] + bias_read.get(j - 3, []), own=True)
                else:
                    v = V(lambda e: e.scalar_tensor_tensor(out=s, in0=R[b][:, 0:L], scalar=w, in1=s, op0=ALU.mult, op1=ALU.add),
                          after=[a], own=True)
                done["N"][b] = [v]
                if h == NAH - 1:
                    d = s[:, L - P:L]
                    scored[j] = [V(lambda e: e.tensor_tensor(d, d, far[:, 1, SEQ - P:SEQ], ALU.add), own=True)]
                    pending.extend((j, round_of(j), r == TOPK // 8 - 1) for r in range(TOPK // 8))
                done["E"][n] = [a]
                return
            if kind == "fox":
                mask, more = far[:, 0, SEQ - L:SEQ], []
            elif j < TOPK // P:
                mask, more = far[:, 1, SEQ - L:SEQ], []
            else:
                fill(until=j)
                mask, more = score[j % 3][:, 0:L], [biased[j]]
            m4 = n % 4
            v = V(lambda e: e.tensor_tensor_reduce(out=Sm[b][:, 0:L], in0=S, in1=mask, scale=1.0, scalar=-3.4e38, op0=ALU.add,
                                                   op1=ALU.max, accum_out=mx[m4][:]), after=[done["S"][n]] + more + done["X"].get(n - 2, []) )
            if kind == "dsa" and h == NAH - 1:
                bias_read[j] = [v]
            v2 = V(lambda e: e.tensor_scalar(nm[m4][:], mx[m4][:], -1.0, None, ALU.mult), own=True)
            a = A(lambda e: e.activation(Pb[b][:, 0:L], Sm[b][:, 0:L], ACT.Exp, bias=nm[m4][:, 0:1], accum_out=sm[m4][:]),
                  after=[v2] + done["X"].get(n - 2, []))
            done["E"][n] = [v]
            done["P", n] = a

        def step_x(n):
            kind, j, h = units[n]
            if kind == "idx":
                return
            b = n % 2
            T.wait(done["P", n])
            evs = []
            for q in range((j + 4) // 4):
                m = min(4, j + 1 - 4 * q)
                t = core.tr([(lambda c=c: core.bank[:, 4 + q, 128 * c:128 * c + 128],
                              lambda c=c: Pb[b][:, 128 * (4 * q + c):128 * (4 * q + c) + 128]) for c in range(m)], ident,
                            after=bank_free.get(q, []))
                Q = (A, V)[q]
                o_, i_ = PT[b][:, 4 * q:4 * q + m, :], core.bank[:, 4 + q, 0:128 * m].rearrange("p (c n) -> p c n", c=m)
                ev = Q((lambda e: e.activation(o_, i_, ACT.Copy)) if q == 0 else (lambda e: e.tensor_copy(o_, i_)), after=[t] + pt_free.get(b, []))
                bank_free[q] = [ev]
                evs.append(ev)
            done["X"][n] = [T.last()]
            done["T", n] = evs
            m4 = n % 4
            done["R", n] = V(lambda e: e.reciprocal(rc[m4][:], sm[m4][:]), after=[done["P", n]])

        bank_free, pt_free = {}, {}

        def step_o(n):
            kind, j, h = units[n]
            if kind == "idx":
                return
            b, m4, slot = n % 2, n % 4, n % 2
            out = core.bank[:, 6 + slot, 0:HD]
            vals = (lambda k: fv[:, k, HD * h:HD * h + HD]) if kind == "fox" else (lambda k: dv[:, k, :])
            core.mm(out, [(lambda k=k: PT[b][:, k, :], lambda k=k: vals(k)) for k in range(j + 1)],
                    after=done["T", n] + done["O"].get(slot, []))
            pt_free[b] = [T.last()]
            o = ob[kind][j % 2]
            a = A(lambda e: e.activation(o[:, HD * h:HD * h + HD], out, ACT.Copy, scale=rc[m4][:, 0:1]),
                  after=[T.last(), done["R", n]] + (stored.get((kind, j - 2), []) if h == 0 else []))
            done["O"][slot] = [a]
            if h == NAH - 1:
                stored[kind, j] = [core.store[(kind == "dsa") * 2 + j % 2](
                    lambda e: e.dma_start(dram["o" + kind][P * j:P * j + P, :], o[:]), after=[a])]

        N = len(units)
        for n in range(-2, N + 1):
            if n + 2 < N:
                step_s(n + 2)
            if 0 <= n + 1 < N:
                step_e(n + 1)
                fill(2)
            if 0 <= n < N:
                step_x(n)
            if 0 <= n - 1:
                step_o(n - 1)


NE, NG, EG, DE = 32, 4, 8, 512
SLOT_TILES = NE + 2 * SEQ // P


def merge(core, dram, tables):
    T, V, A, G = core.T, core.V, core.A, core.G
    ident = tables["mats"][:, C_ID, :]
    with Room(core) as sb:
        ld = core.load
        wp = [sb(f"m_wp{j}", [P, 4, D]) for j in range(2)]
        wo = sb("m_wo", [P, KD, D])
        wr = sb("m_wr", [P, KD, NG + NE])
        gate, gain, shift = (sb("m_" + k, [P, D]) for k in ("gate", "gain", "shift"))
        bg = sb("m_bg", [P, 2 * D])
        o = [sb(f"m_o{b}", [P, D]) for b in range(2)]
        gs = [sb(f"m_gs{b}", [P, 2 * D]) for b in range(2)]
        x = sb("m_x", [P, D])
        oT, mT = sb("m_oT", [P, KD, P]), sb("m_mT", [P, KD, P])
        m1, m2, x2, h = (sb("m_" + k, [P, D]) for k in ("m1", "m2", "x2", "h"))
        norm = Norm(core, sb, "m_n")
        ld[9](lambda e: e.dma_start(wp[0][:], dram["w_proj_fox_2"].rearrange("(k p) n -> p k n", p=P)))
        ld[9](lambda e: e.dma_start(wp[1][:], dram["w_proj_dsa_2"].rearrange("(k p) n -> p k n", p=P)))
        ld[9](lambda e: e.dma_start(wo[:], dram["w_out_2"].rearrange("(k p) n -> p k n", p=P)))
        ld[9](lambda e: e.dma_start(wr[:, :, 0:NG], dram["router_w_grp_2"].rearrange("(k p) n -> p k n", p=P)))
        ld[9](lambda e: e.dma_start(wr[:, :, NG:NG + NE], dram["router_w_exp_2"].rearrange("(k p) n -> p k n", p=P)))
        ld[9](lambda e: e.dma_start(bg[:], row(dram["b_gate_2"])))
        mod = dram["mod2"][0, :]
        wl = ld[9](lambda e: e.dma_start(gate[:], row(mod[2 * D:3 * D])))
        gain_rows(core, gain[:], dram["norm2_g_2"], mod[4 * D:5 * D], shift[:], mod[3 * D:4 * D], m1[:])
        T.wait(wl)
        V.wait(wl)

        def tile(b, i, marks):
            prev = prev_of(marks)
            before = lambda k: ([marks[k + "0"]] if k + "0" in marks else []) if b else prev(k + "1")
            at = bass.ds(i * 256 + 128 * b, 128)
            l1 = ld[1 + b](lambda e: e.dma_start(o[b][:, 0:512], dram["ofox"][at, :]), after=prev(f"to{b}"))
            l1 = ld[1 + b](lambda e: e.dma_start(o[b][:, 512:1024], dram["odsa"][at, :]))
            l2 = ld[3 + b](lambda e: e.dma_start(gs[b][:], dram["proj"][at, C_GF:C_GF + 2 * D]), after=prev(f"gs{b}"))
            l3 = ld[5](lambda e: e.dma_start(x[:], dram["x1"][at, :]), after=before("x"))
            V(lambda e: e.tensor_tensor(gs[b][:], gs[b][:], bg[:], ALU.add), after=[l2])
            sg = A(lambda e: e.activation(gs[b][:], gs[b][:], ACT.Sigmoid), after=[V.last()])
            t, ev = turn_rows(core, oT, o[b][:], KD, ident, (6, 7), [l1], [before("ev6"), before("ev7")])
            marks[f"to{b}"] = t
            T.wait(ev, *before("v2"))
            for j in range(2):
                for half in range(2):
                    core.mm(core.bank[:, 2 * j + half, :], [(lambda k=k: oT[:, 4 * j + k, :], lambda k=k: wp[j][:, k, 512 * half:512 * half + 512])
                                                            for k in range(4)])
            p = T.last()
            flat = lambda j: core.bank[:, 2 * j:2 * j + 2, :].rearrange("p a n -> p (a n)")
            V(lambda e: e.tensor_tensor(m1[:], flat(0), gs[b][:, 0:D], ALU.mult), after=[p, sg] + before("tm"))
            V(lambda e: e.tensor_tensor(m2[:], flat(1), gs[b][:, D:2 * D], ALU.mult))
            marks[f"gs{b}"] = V.last()
            v = V(lambda e: e.tensor_tensor(m1[:], m1[:], m2[:], ALU.add), own=True)
            t, ev = turn_rows(core, mT, m1[:], KD, ident, (6, 7), [v], [[A.last()], [A.last()]])
            marks[f"tm{b}"] = t
            T.wait(ev)
            for half in range(2):
                core.mm(core.bank[:, 4 + half, :], [(lambda k=k: mT[:, k, :], lambda k=k: wo[:, k, 512 * half:512 * half + 512]) for k in range(KD)],
                        after=before("v2"))
            V(lambda e: e.tensor_tensor(x2[:], flat(2), gate[:], ALU.mult), after=[T.last()] + before("stx") + before("nx"))
            marks[f"x{b}"] = V(lambda e: e.tensor_tensor(x2[:], x2[:], x[:], ALU.add), own=True, after=[l3])
            marks[f"v2{b}"] = V.last()
            marks[f"stx{b}"] = core.store[0](lambda e: e.dma_start(dram["x2"][at, :], x2[:]), after=[V.last()])
            V.wait(norm.rstd(x2[:], tables["eps"][:, 0:1], [V.last()]))
            v = norm.apply(h[:], x2[:], gain[:], shift[:], after=before("sth") + before("th"))
            marks[f"nx{b}"] = v
            marks[f"sth{b}"] = core.store[1](lambda e: e.dma_start(dram["h2"][at, :], h[:]), after=[v])
            t, ev = turn_rows(core, oT, h[:], KD, ident, (6, 7), [v], [[A.last()], [A.last()]])
            marks[f"th{b}"] = t
            core.mm(core.bank[:, 0, 0:NG + NE], [(lambda k=k: oT[:, k, :], lambda k=k: wr[:, k, :]) for k in range(KD)], after=[ev])
            marks[f"ev6{b}"] = marks[f"ev7{b}"] = T.last()
            V(lambda e: e.tensor_copy(tables["logits"][:, bass.ds(i * 2 + b, 1), :].rearrange("p a n -> p (a n)"), core.bank[:, 0, 0:NG + NE]),
              after=[T.last()])
            marks[f"v2{b}"] = V.last()

        def body(i, marks):
            for b in range(2):
                tile(b, i, marks)
        core.loop(NT // 2, body)


def route(core, dram, tables):
    T, V, A, G = core.T, core.V, core.A, core.G
    with Room(core) as sb:
        ld = core.load
        v = lambda f: V(f, own=True)
        new = lambda name, *shape: sb("r_" + name, [P, *shape])
        bgr, bex = new("bgr", NG), new("bex", NE)
        cst = new("cst", NG + NE + 8 + SLOT_TILES)
        ld[0](lambda e: e.dma_start(bgr[:], row(dram["router_b_grp_2"])))
        ld[0](lambda e: e.dma_start(bex[:], row(dram["router_b_exp_2"])))
        got = ld[0](lambda e: e.dma_start(cst[:], row(dram["counts"])))
        down4, down32 = cst[:, 0:NG], cst[:, NG:NG + NE]
        steps, tile_no = cst[:, NG + NE:NG + NE + 8], cst[:, NG + NE + 8:]
        V.wait(got)
        gl, eq, oh = new("gl", NT, NG), new("eq", NT, NG), new("oh", NT, NG)
        gm, gs, gw, t1, t2 = (new(k, NT) for k in ("gm", "gs", "gw", "t1", "t2"))
        el, q32, w32 = new("el", NT, NE), new("q32", NT, NE), new("w32", NT, NE)
        E = [new(f"E{j}", NT, NE) for j in range(2)]
        m = [new(f"m{j}", NT) for j in range(2)]
        lg = tables["logits"]
        W = tables["weight"]
        v(lambda e: e.tensor_tensor(gl[:], lg[:, :, 0:NG], over(bgr[:], 1, NT), ALU.add))
        v(lambda e: e.tensor_reduce(gm[:], gl[:], AX.X, ALU.max))
        v(lambda e: e.tensor_tensor(eq[:], gl[:], over(gm[:], 2, NG), ALU.is_equal))
        v(lambda e: e.tensor_tensor(eq[:], eq[:], over(down4, 1, NT), ALU.mult))
        v(lambda e: e.tensor_reduce(t1[:], eq[:], AX.X, ALU.max))
        v(lambda e: e.tensor_tensor(oh[:], eq[:], over(t1[:], 2, NG), ALU.is_equal))
        v(lambda e: e.tensor_tensor(gl[:], gl[:], over(gm[:], 2, NG), ALU.subtract))
        a = A(lambda e: e.activation(gl[:], gl[:], ACT.Exp), after=[V.last()])
        V.wait(a)
        v(lambda e: e.tensor_reduce(gs[:], gl[:], AX.X, ALU.add))
        v(lambda e: e.reciprocal(gw[:], gs[:]))
        v(lambda e: e.tensor_scalar(oh[:], oh[:], -1.0, -FAR, ALU.add, ALU.mult))
        v(lambda e: e.tensor_tensor(el[:], lg[:, :, NG:NG + NE], over(bex[:], 1, NT), ALU.add))
        el4 = el[:].rearrange("p t (g k) -> p (t g) k", k=EG)
        v(lambda e: e.tensor_tensor(el4, el4, over(oh[:].rearrange("p t g -> p (t g)"), 2, EG), ALU.add))
        for j in range(2):
            v(lambda e: e.tensor_reduce(m[j][:], el[:], AX.X, ALU.max))
            v(lambda e: e.tensor_tensor(q32[:], el[:], over(m[j][:], 2, NE), ALU.is_equal))
            v(lambda e: e.tensor_tensor(q32[:], q32[:], over(down32, 1, NT), ALU.mult))
            v(lambda e: e.tensor_reduce(t1[:], q32[:], AX.X, ALU.max))
            v(lambda e: e.tensor_tensor(E[j][:], q32[:], over(t1[:], 2, NE), ALU.is_equal))
            if j == 0:
                v(lambda e: e.scalar_tensor_tensor(out=el[:], in0=E[0][:], scalar=2 * FAR, in1=el[:], op0=ALU.mult, op1=ALU.add))
        v(lambda e: e.tensor_tensor(t2[:], m[1][:], m[0][:], ALU.subtract))
        a = A(lambda e: e.activation(t2[:], t2[:], ACT.Exp), after=[V.last()])
        V.wait(a)
        v(lambda e: e.tensor_scalar(t1[:], t2[:], 1.0, None, ALU.add))
        v(lambda e: e.reciprocal(t1[:], t1[:]))
        v(lambda e: e.tensor_tensor(W[:, 0, :], t1[:], gw[:], ALU.mult))
        v(lambda e: e.tensor_tensor(W[:, 1, :], W[:, 0, :], t2[:], ALU.mult))
        v(lambda e: e.tensor_tensor(w32[:], E[0][:], E[1][:], ALU.add))
        for j, c in ((0, C_LT), (1, C_ONE)):
            T(lambda e: e.matmul(core.bank[:, j, 0:NT * NE], tables["mats"][:, c, :], w32[:].rearrange("p t n -> p (t n)"), start=True, stop=True),
              after=[V.last()])
        rank, run, total = new("rank", NT, NE), new("run", NE), new("total", NT, NE)
        V.wait(T.last())
        v(lambda e: e.memset(run[:], 0.0))
        v(lambda e: e.tensor_copy(total[:].rearrange("p t n -> p (t n)"), core.bank[:, 1, 0:NT * NE]))
        for t in range(NT):
            v(lambda e: e.tensor_tensor(rank[:, t, :], core.bank[:, 0, NE * t:NE * t + NE], run[:], ALU.add))
            v(lambda e: e.tensor_tensor(run[:], run[:], total[:, t, :], ALU.add))
        cmp, inc = new("cmp", NE, 8), [new(f"inc{j}", NE) for j in range(2)]
        tiles = new("tiles", NE)
        v(lambda e: e.tensor_tensor(cmp[:], over(run[:], 2, 8), over(steps, 1, NE), ALU.is_gt))
        v(lambda e: e.tensor_reduce(tiles[:], cmp[:], AX.X, ALU.add))
        v(lambda e: e.tensor_copy(inc[0][:], tiles[:]))
        src = 0
        for d in (1, 2, 4, 8, 16):
            v(lambda e: e.tensor_copy(inc[1 - src][:, 0:d], inc[src][:, 0:d]))
            v(lambda e: e.tensor_tensor(inc[1 - src][:, d:NE], inc[src][:, d:NE], inc[src][:, 0:NE - d], ALU.add))
            src = 1 - src
        ends = inc[src]
        base = new("base", NE)
        v(lambda e: e.tensor_tensor(base[:], ends[:], tiles[:], ALU.subtract))
        v(lambda e: e.tensor_scalar(base[:], base[:], float(P), None, ALU.mult))
        v(lambda e: e.tensor_tensor(rank[:], rank[:], over(base[:], 1, NT), ALU.add))
        for j in range(2):
            v(lambda e: e.tensor_tensor(q32[:], E[j][:], rank[:], ALU.mult))
            v(lambda e: e.tensor_reduce(t1[:], q32[:], AX.X, ALU.add))
            v(lambda e: e.tensor_copy(tables["slot"][:, j, :], t1[:]))
        ge, te = new("ge", SLOT_TILES, NE), new("te", SLOT_TILES)
        v(lambda e: e.tensor_tensor(ge[:], over(tile_no, 2, NE), over(ends[:], 1, SLOT_TILES), ALU.is_ge))
        v(lambda e: e.tensor_reduce(te[:], ge[:], AX.X, ALU.add))
        v(lambda e: e.tensor_scalar(te[:], te[:], float(NE - 1), None, ALU.min))
        v(lambda e: e.tensor_copy(tables["expert"][:], te[:]))
        zero, tok = sb("r_zero", [P, SLOT_TILES], I32), sb("r_tok", [P, NT], I32)
        G(lambda e: e.memset(zero[:], 0))
        G(lambda e: e.iota(tok[:], [[P, NT]], base=0, channel_multiplier=1))
        z = core.store[0](lambda e: e.dma_start(dram["slot_token"].rearrange("(p m) a -> p (m a)", p=P), zero[:]), after=[G.last()])
        G.wait(z, V.last(), G.last())
        for t in range(NT):
            for j in range(2):
                core.scatter(lambda e: e.indirect_dma_start(out=dram["slot_token"], out_offset=bass.IndirectOffsetOnAxis(
                    ap=tables["slot"][:, j, t:t + 1].bitcast(U32), axis=0), in_=tok[:, t:t + 1], in_offset=None))


def experts(core, dram, tables):
    T, V, A, G = core.T, core.V, core.A, core.G
    ident = tables["mats"][:, C_ID, :]
    with Room(core) as sb:
        ld = core.load
        w1, w3 = ([sb(f"e_{k}{b}", [P, KD, DE]) for b in range(2)] for k in ("w1", "w3"))
        w2 = [sb(f"e_w2{b}", [P, DE // P, D]) for b in range(2)]
        ids = sb("e_ids", [P, SLOT_TILES], I32)
        idb = [sb(f"e_idb{b}", [P, 1], I32) for b in range(2)]
        x = [sb(f"e_x{b}", [P, D]) for b in range(2)]
        xT = [sb(f"e_xT{b}", [P, KD, P]) for b in range(2)]
        g = [sb(f"e_g{b}", [P, DE]) for b in range(2)]
        gT = [sb(f"e_gT{b}", [P, DE // P, P]) for b in range(2)]
        y = [sb(f"e_y{b}", [P, D]) for b in range(2)]
        with core.nc.allow_non_contiguous_dma(reason="a slot's token on the slot's partition"):
            got = ld[0](lambda e: e.dma_start(ids[:], dram["slot_token"].rearrange("(m p) a -> p (m a)", p=P)))
        idle = sb("e_idle", [P, 1])
        G(lambda e: e.memset(idle[:], 0.0))
        G.wait(got)

        def fetch(b, i, marks):
            prev = prev_of(marks)
            m = i * 2 + b
            if ld[1].counting:
                ex = 0
            else:
                ex = core.nc.sync.value_load(tables["expert"][0:1, bass.ds(m, 1)], min_val=0, max_val=NE - 1)
            out = []
            for j, (buf, name, kk) in enumerate(((w1, "exp_w1_2", KD), (w3, "exp_w3_2", KD), (w2, "exp_w2_2", DE // P))):
                n = 1 + 3 * b + j
                out.append(ld[n](lambda e: e.dma_start(buf[b][:], dram[name][bass.ds(ex, 1), :, :].rearrange("a (k p) n -> p (a k) n", p=P)),
                                 after=prev(f"w{j}{b}")))
            G(lambda e: e.tensor_copy(idb[b][:], ids[:, bass.ds(m, 1)]), after=prev(f"tx{b}"))
            G.wait(G.last())
            G(lambda e: e.tensor_tensor(idle[:], idle[:], idle[:], ALU.add))
            gather = core.gather[b](lambda e: e.indirect_dma_start(out=x[b][:], out_offset=None, in_=dram["h2"],
                                                                   in_offset=bass.IndirectOffsetOnAxis(ap=idb[b][:, 0:1].bitcast(U32), axis=0)),
                                    )
            return out, gather

        def turn_x(b, gather, marks):
            before = prev_of(marks)
            T.wait(gather, *before(f"down{b}"))
            for q in range(2):
                t = core.tr([(lambda c=c: core.bank[:, 4 + q, 128 * c:128 * c + 128], lambda c=c: x[b][:, 512 * q + 128 * c:512 * q + 128 * c + 128])
                             for c in range(4)], ident, after=[last[f"x{q}"]] if f"x{q}" in last else prev_of(marks)(f"lx{q}"))
                o_, i_ = xT[b][:, 4 * q:4 * q + 4, :], core.bank[:, 4 + q, :].rearrange("p (c n) -> p c n", c=4)
                Q = (A, V)[q]
                last[f"x{q}"] = Q((lambda e: e.activation(o_, i_, ACT.Copy)) if q == 0 else (lambda e: e.tensor_copy(o_, i_)),
                                  after=[t] + before(f"up{b}"))
                marks[f"lx{q}"] = last[f"x{q}"]
            marks[f"tx{b}"] = T.last()
            return [last["x0"], last["x1"]]

        def up(b, w, ready, marks, i):
            T.wait(*ready)
            for j, buf in ((0, w1), (1, w3)):
                core.mm(core.bank[:, j, :], [(lambda k=k: xT[b][:, k, :], lambda k=k: buf[b][:, k, :]) for k in range(KD)],
                        after=[w[j]] + ([last["mul"]] if "mul" in last else prev_of(marks)("lmul")))
                marks[f"w{j}{b}"] = T.last()
            marks[f"up{b}"] = T.last()
            a = A(lambda e: e.activation(g[b][:], core.bank[:, 0, :], ACT.Silu), after=[T.last()] + prev_of(marks)(f"tg{b}"))
            last["mul"] = V(lambda e: e.tensor_tensor(g[b][:], g[b][:], core.bank[:, 1, :], ALU.mult), after=[a])
            marks["lmul"] = last["mul"]

        def down(b, w, mul, marks):
            t = core.tr([(lambda c=c: core.bank[:, 6, 128 * c:128 * c + 128], lambda c=c: g[b][:, 128 * c:128 * c + 128]) for c in range(4)],
                        ident, after=[mul] + ([last["g"]] if "g" in last else prev_of(marks)("lg")))
            marks[f"tg{b}"] = t
            last["g"] = marks["lg"] = A(lambda e: e.activation(gT[b][:].rearrange("p c n -> p (c n)"), core.bank[:, 6, :], ACT.Copy),
                                        after=[t] + prev_of(marks)(f"down{b}"))
            T.wait(last["g"], w[2], *([last["y"]] if "y" in last else prev_of(marks)("ly")))
            for half in range(2):
                core.mm(core.bank[:, 2 + half, :], [(lambda k=k: gT[b][:, k, :], lambda k=k: w2[b][:, k, 512 * half:512 * half + 512])
                                                    for k in range(DE // P)])
            marks[f"down{b}"] = marks[f"w2{b}"] = T.last()
            last["y"] = marks["ly"] = V(lambda e: e.tensor_copy(y[b][:], core.bank[:, 2:4, :].rearrange("p a n -> p (a n)")),
                                        after=[T.last()] + prev_of(marks)(f"st{b}"))

        last = {}

        def body(i, marks):
            last.clear()
            w, x_ = zip(*(fetch(b, i, marks) for b in range(2)))
            r0 = turn_x(0, x_[0], marks)
            up(0, w[0], r0, marks, i)
            mul0 = last["mul"]
            r1 = turn_x(1, x_[1], marks)
            down(0, w[0], mul0, marks)
            up(1, w[1], r1, marks, i)
            marks["st0"] = core.store[0](lambda e: e.dma_start(dram["y"][bass.ds(i * 256, 128), :], y[0][:]), after=[last["y"]])
            down(1, w[1], last["mul"], marks)
            marks["st1"] = core.store[1](lambda e: e.dma_start(dram["y"][bass.ds(i * 256 + 128, 128), :], y[1][:]), after=[last["y"]])
        core.loop(SLOT_TILES // 2, body)


def combine(core, dram, tables):
    V, G = core.V, core.G
    with Room(core) as sb:
        gate = sb("o_gate", [P, D])
        y = [[sb(f"o_y{j}{b}", [P, D]) for b in range(2)] for j in range(2)]
        x2 = [sb(f"o_x{b}", [P, D]) for b in range(2)]
        V.wait(core.load[0](lambda e: e.dma_start(gate[:], row(dram["mod2"][0, 5 * D:6 * D]))))
        read, stored = {}, {}
        for t in range(NT):
            b = t % 2
            lx = core.load[1 + b](lambda e: e.dma_start(x2[b][:], dram["x2"][P * t:P * t + P, :]), after=stored.get(t - 2, []))
            got = [core.gather[2 * b + j](lambda e: e.indirect_dma_start(
                out=y[j][b][:], out_offset=None, in_=dram["y"],
                in_offset=bass.IndirectOffsetOnAxis(ap=tables["slot"][:, j, t:t + 1].bitcast(U32), axis=0)), after=read.get(t - 2, [])) for j in range(2)]
            V(lambda e: e.tensor_scalar(y[0][b][:], y[0][b][:], tables["weight"][:, 0, t:t + 1], None, ALU.mult), after=got[:1])
            V(lambda e: e.scalar_tensor_tensor(out=y[0][b][:], in0=y[1][b][:], scalar=tables["weight"][:, 1, t:t + 1], in1=y[0][b][:],
                                               op0=ALU.mult, op1=ALU.add), after=got[1:], own=True)
            V(lambda e: e.tensor_tensor(y[0][b][:], y[0][b][:], gate[:], ALU.mult), own=True)
            read[t] = [V(lambda e: e.tensor_tensor(x2[b][:], x2[b][:], y[0][b][:], ALU.add), own=True, after=[lx])]
            stored[t] = [core.store[b](lambda e: e.dma_start(dram["result"][P * t:P * t + P, :], x2[b][:]), after=[V.last()])]


SCRATCH = {"mods": (2, 3 * D), "mod2": (1, 6 * D), "uT": (DF, SEQ), "z": (SEQ, 2 * D), "xbcT": (CONV, SEQ + CTX), "mix": (SEQ, 2 * D),
           "x1": (SEQ, D), "h1": (SEQ, D), "proj": (SEQ, COLS2), "fqT": (NAH, HD, SEQ), "fkT": (NAH, HD + 1, SEQ), "dqT": (NAH, HD, SEQ),
           "iqT": (NAH, HD, SEQ), "dkT": (HD, SEQ), "ikT": (HD, SEQ), "ofox": (SEQ, 512), "odsa": (SEQ, 512), "x2": (SEQ, D), "h2": (SEQ, D),
           "y": (SLOT_TILES * P, D)}
STAGES = (modulation, project_first, fourier, state_space, close_first, project_second, prepare_heads, attend, merge, route, experts, combine)


def program(nc, dram):
    for name, shape in SCRATCH.items():
        dram[name] = nc.dram_tensor(name, shape, F32).ap()
    dram["slot_token"] = nc.dram_tensor("slot_token", (SLOT_TILES * P, 1), I32).ap()
    with ExitStack() as ctx:
        core = Core(nc, ctx)
        with Room(core) as sb:
            tables = load_tables(core, sb, dram)
            for stage in STAGES:
                stage(core, dram, tables)


def kernel(**inputs):
    import concourse.bacc as bacc
    from concourse.bass_utils import run_bass_kernel_spmd

    nc = bacc.Bacc("TRN2", target_bir_lowering=False, num_devices=1)
    arrays, dram = {}, {}
    for name, a in {**inputs, **constants()}.items():
        a = np.asarray(a)
        if name in inputs and a.ndim > 1:
            a = a[0]
        arrays["in_" + name] = np.ascontiguousarray(a)
        dram[name] = nc.dram_tensor("in_" + name, a.shape, mybir.dt.from_np(a.dtype), kind="ExternalInput").ap()
    dram["result"] = nc.dram_tensor("result", (SEQ, D), F32, kind="ExternalOutput").ap()
    program(nc, dram)
    out = run_bass_kernel_spmd(nc, [arrays], core_ids=[0]).results[0]["result"]
    return out.reshape(1, SEQ, D)
```

```python
import numpy as np
import concourse.bass as bass
from concourse import mybir
from contextlib import ExitStack

F32, BF16, I32 = mybir.dt.float32, mybir.dt.bfloat16, mybir.dt.int32
U32 = mybir.dt.uint32
ALU, ACT, AX = mybir.AluOpType, mybir.ActivationFunctionType, mybir.AxisListType
START = 4096


class Ticket:
    def __init__(self, queue, base, step, loop):
        self.queue, self.base, self.step, self.loop = queue, base, step, loop

    def last_round(self, back=1):
        return Ticket(self.queue, self.base - back * self.step, self.step, self.loop)

    def value(self):
        return self.base if self.loop is None else self.loop * self.step + self.base


class Queue:
    def __init__(self, nc, eng, name, unit=1, start=START):
        self.eng, self.unit, self.sem = eng, unit, nc.alloc_semaphore(name)
        self.n, self.step, self.loop, self.counting = start, 0, None, False
        self.bump = start > 0
        if start:
            eng.sem_inc(self.sem, start)

    def __call__(self, f, after=(), own=False, inc=True):
        self.wait(*after, *([self.last()] if own else []))
        if not self.counting:
            ins = f(self.eng)
            if inc:
                ins.then_inc(self.sem, self.unit)
        if inc:
            self.n += self.unit
        return self.last()

    def last(self):
        return Ticket(self, self.n, self.step, self.loop)

    def wait(self, *tickets):
        if self.counting:
            return
        latest = {}
        for t in tickets:
            k = (t.queue, t.step, t.loop is None)
            if k not in latest or latest[k].base < t.base:
                latest[k] = t
        for t in latest.values():
            self.eng.wait_ge(t.queue.sem, t.value())


def run_loop(nc, queues, trips, body, live=None, rest=None):
    before, marks = {q: q.n for q in queues}, {}
    for q in queues:
        q.counting = True
    body(0, marks)
    steps = {q: q.n - before[q] for q in queues}
    for t in marks.values():
        t.step = steps[t.queue]
    for q in queues:
        q.n, q.counting, q.step = before[q], False, steps[q]
    with nc.Fori(0, trips) as i:
        for q in queues:
            q.loop = i
        for t in marks.values():
            t.loop = i
        if live is None:
            body(i, dict(marks))
        else:
            with nc.If(i < live):
                body(i, dict(marks))
            with nc.Else():
                at = {q: q.n for q in queues}
                for q in queues:
                    q.n = before[q]
                rest(i)
                for q in queues:
                    q.n, moved = at[q], q.n > before[q]
                    if steps[q] and q.bump and not moved:
                        q.wait(Ticket(q, before[q], steps[q], i))
                        q.eng.sem_inc(q.sem, steps[q])
    for q in queues:
        q.n, q.step, q.loop = before[q] + trips * steps[q], 0, None
D, SEQ, CTX, P, KD = 1024, 1024, 256, 128, 8
NT, NC = SEQ // P, CTX // P
DF, DS, NBC, NST = 512, 1536, 4, 128
NH, HP, HG = 24, 64, 6
CONV, GRID_H, GRID_W = 2560, 16, 64
COL_Z, COL_XBC, COL_DT = 512, 2560, 5120
EPS, FAR = 1e-6, -1e30
C_ID, C_LE, C_GE, C_GT, C_LT, C_ONE = range(6)


class Core:
    def __init__(self, nc, ctx):
        self.nc, self.ctx = nc, ctx
        self.T, self.V, self.A, self.G = (Queue(nc, e, n) for e, n in (
            (nc.tensor, "pe_done"), (nc.vector, "dve_done"), (nc.scalar, "act_done"), (nc.gpsimd, "pool_done")))
        self.load = [Queue(nc, nc.sync, f"load{j}_done", 16) for j in range(12)]
        self.store = [Queue(nc, nc.scalar, f"store{j}_done", 16) for j in range(8)]
        self.gather = [Queue(nc, nc.gpsimd, f"gather{j}_done", 16, 0) for j in range(4)]
        self.scatter = Queue(nc, nc.gpsimd, "scatter_done", 16, 0)
        self.queues = [self.T, self.V, self.A, self.G] + self.load + self.store + self.gather + [self.scatter]
        self.engines = [nc.tensor, nc.vector, nc.scalar, nc.gpsimd, nc.sync]
        self.bank = ctx.enter_context(nc.psum_tensor("banks", [P, 8, 512], F32))

    def settle(self):
        for e in self.engines:
            for q in self.queues:
                if q.n:
                    e.wait_ge(q.sem, q.n)

    def loop(self, trips, body, more=(), live=None, rest=None):
        run_loop(self.nc, self.queues + list(more), trips, body, live, rest)

    def mm(self, out, pairs, after=(), inc=True, start=True, stop=True):
        self.T.wait(*after)
        for n, (a, b) in enumerate(pairs):
            last = n == len(pairs) - 1
            self.T(lambda e: e.matmul(out, a(), b(), start=start and n == 0, stop=stop and last), inc=inc and last)
        return self.T.last()

    def tr(self, outs, ident, after=()):
        self.T.wait(*after)
        for n, (o, a) in enumerate(outs):
            self.T(lambda e: e.transpose(o(), a(), ident), inc=n == len(outs) - 1)
        return self.T.last()


class Room:
    def __init__(self, core):
        self.core, self.stack = core, ExitStack()

    def __call__(self, name, shape, dt=F32):
        return self.stack.enter_context(self.core.nc.sbuf_tensor(name, shape, dt))

    def __enter__(self):
        self.stack.__enter__()
        return self

    def __exit__(self, *a):
        self.core.settle()
        return self.stack.__exit__(*a)


def row(ap):
    return ap.partition_broadcast(P)


def over(ap, axis, n):
    a = ap.unsqueeze(axis)
    shape = list(a.shape)
    shape[axis] = n
    return a.to_broadcast(shape)


def modulation(core, dram, tables):
    with Room(core) as sb:
        T, V, A = core.T, core.V, core.A
        c = sb("mod_c", [P, 3, KD])
        cs = sb("mod_silu", [P, KD, 3])
        w = [sb(f"mod_w{b}", [P, KD, 512]) for b in range(2)]
        bias = [sb(f"mod_b{b}", [2, 512]) for b in range(2)]
        out = [sb(f"mod_o{b}", [2, 512]) for b in range(2)]
        got = None
        for j, name in enumerate(("c", "c_ctx", "c_2")):
            got = core.load[10](lambda e: e.dma_start(c[:, j, :], dram[name].rearrange("(p k) -> p k", k=KD)))
        silu = A(lambda e: e.activation(cs[:].rearrange("p k j -> p j k"), c[:], ACT.Silu), after=[got])
        T.wait(silu)
        for w_name, b_name, o_name, j0, m, n in (("w_ada", "b_ada", "mods", 0, 2, 6), ("ada_w_2", "ada_b_2", "mod2", 2, 1, 12)):
            wv = dram[w_name].rearrange("(p k) n -> p k n", k=KD)

            def body(i, marks):
                for b in range(2):
                    at = bass.ds(i * 1024 + 512 * b, 512)
                    prev = lambda x: [marks[x].last_round()] if x in marks else []
                    lw = core.load[b](lambda e: e.dma_start(w[b][:], wv[:, :, at]), after=prev(f"mm{b}"))
                    lb = core.load[2 + b](lambda e: e.dma_start(bias[b][0:m, :], dram[b_name][at].partition_broadcast(m)),
                                          after=prev(f"add{b}"))
                    t = core.mm(core.bank[0:m, b, :], [(lambda k=k: cs[:, k, j0:j0 + m], lambda k=k: w[b][:, k, :])
                                                       for k in range(KD)], after=[lw] + prev(f"add{b}"))
                    v = V(lambda e: e.tensor_tensor(out[b][0:m, :], core.bank[0:m, b, :], bias[b][0:m, :], ALU.add),
                          after=[t, lb] + prev(f"st{b}"))
                    marks[f"mm{b}"], marks[f"add{b}"] = t, v
                    marks[f"st{b}"] = core.store[b](lambda e: e.dma_start(dram[o_name][0:m, at], out[b][0:m, :]), after=[v])
            core.loop(n // 2, body)


class Norm:
    def __init__(self, core, sb, name):
        self.core = core
        self.sq = sb(name + "_sq", [P, D])
        self.ss = sb(name + "_ss", [P, 1])
        self.sd = sb(name + "_sd", [P, 1])
        self.rs = sb(name + "_rs", [P, 1])

    def rstd(self, x, eps, after):
        core = self.core
        core.A(lambda e: e.activation(self.sq[:], x, ACT.Square, accum_out=self.ss[:]), after=after)
        a = core.A(lambda e: e.activation(self.sd[:], self.ss[:], ACT.Sqrt, bias=eps, scale=1.0 / D), own=True)
        return core.V(lambda e: e.reciprocal(self.rs[:], self.sd[:]), after=[a])

    def apply(self, out, x, gain, shift=None, after=()):
        v = self.core.V(lambda e: e.scalar_tensor_tensor(out=out, in0=x, scalar=self.rs[:, 0:1], in1=gain,
                                                         op0=ALU.mult, op1=ALU.mult), after=after, own=True)
        if shift is not None:
            v = self.core.V(lambda e: e.tensor_tensor(out, out, shift, ALU.add), own=True)
        return v


def gain_rows(core, gain, w_row, scale_row, shift, shift_row, tmp):
    core.load[0](lambda e: e.dma_start(gain, row(w_row)))
    core.load[0](lambda e: e.dma_start(tmp, row(scale_row)))
    got = core.load[0](lambda e: e.dma_start(shift, row(shift_row)))
    core.V(lambda e: e.scalar_tensor_tensor(out=gain, in0=tmp, scalar=1.0, in1=gain, op0=ALU.add, op1=ALU.mult), after=[got])
    return core.V.last()


def project_first(core, dram, tables):
    T, V, A, G = core.T, core.V, core.A, core.G
    ident = tables["mats"][:, C_ID, :]
    with Room(core) as sb:
        TOK = SEQ + CTX
        hT = sb("hT", [P, KD, TOK])
        with Room(core) as sb1:
            norm = Norm(core, sb1, "n1")
            gain, shift, tmp = (sb1(f"n1_{n}", [P, D]) for n in ("gain", "shift", "tmp"))
            x = [sb1(f"n1_x{b}", [P, D]) for b in range(2)]
            h = [sb1(f"n1_h{b}", [P, D]) for b in range(2)]
            for src, mod, n, at0 in ((dram["x"], 0, NT, 0), (dram["ctx"], 1, NC, SEQ)):
                mrow = dram["mods"][mod, :]
                rows_in = gain_rows(core, gain[:], dram["norm_w"], mrow[D:2 * D], shift[:], mrow[0:D], tmp[:])

                def body(i, marks):
                    prev = lambda k: [marks[k].last_round()] if k in marks else []
                    for b in range(2):
                        ld = core.load[1 + b](lambda e: e.dma_start(x[b][:], src[bass.ds(i * 256 + 128 * b, 128), :]),
                                              after=prev(f"h{b}"))
                        V.wait(norm.rstd(x[b][:], tables["eps"][:, 0:1], [ld]))
                        v = norm.apply(h[b][:], x[b][:], gain[:], shift[:], after=prev(f"t{b}") + [rows_in])
                        marks[f"h{b}"] = v
                        t = core.tr([(lambda k=k: core.bank[:, 2 * b + k // 4, 128 * (k % 4):128 * (k % 4) + 128],
                                      lambda k=k: h[b][:, 128 * k:128 * k + 128]) for k in range(KD)], ident,
                                    after=[v] + prev(f"ev{b}"))
                        marks[f"t{b}"] = t
                        for half in range(2):
                            A(lambda e: e.activation(hT[:, 4 * half:4 * half + 4, bass.ds(i * 256 + 128 * b + at0, 128)],
                                                     core.bank[:, 2 * b + half, :].rearrange("p (k n) -> p k n", k=4),
                                                     ACT.Copy), after=[t])
                        marks[f"ev{b}"] = A.last()
                core.loop(n // 2, body)
                core.V.wait(T.last(), A.last())
                core.nc.sync.wait_ge(V.sem, V.n)

        NCT = CONV // P
        taps = sb("taps", [P, NCT, 10])
        with Room(core) as sb1:
            flat = sb1("taps_flat", [10, CONV])
            core.load[0](lambda e: e.dma_start(flat[0:9, :], dram["conv_w"].rearrange("a b c -> (a b) c")))
            got = core.load[0](lambda e: e.dma_start(flat[9:10, :], dram["conv_b"].rearrange("(a c) -> a c", a=1)))
            t = core.tr([(lambda k=k: core.bank[:, 0, 10 * k:10 * k + 10], lambda k=k: flat[:, 128 * k:128 * k + 128])
                         for k in range(NCT)], tables["mats"][0:10, C_ID, 0:10], after=[got])
            V(lambda e: e.tensor_copy(taps[:].rearrange("p t j -> p (t j)"), core.bank[:, 0, 0:10 * NCT]), after=[t])

        w = [sb(f"w1_{b}", [P, KD, 256]) for b in range(2)]
        img = [sb(f"img{b}", [P, GRID_H + 2, GRID_W + 2]) for b in range(2)]
        line = [sb(f"line{b}", [P, CTX + 2]) for b in range(2)]
        acc = [sb(f"acc{b}", [P, TOK]) for b in range(2)]
        tap = [sb(f"tap{b}", [P, 10]) for b in range(2)]
        res = [sb(f"res{b}", [P, TOK]) for b in range(2)]
        for b in range(2):
            G(lambda e: e.memset(img[b][:], 0.0))
            G(lambda e: e.memset(line[b][:], 0.0))
        zeroed = G.last()
        win = dram["w_in"].rearrange("(k p) n -> p k n", p=P)

        def products(s, b, wap, lw, wait, ctx_too):
            T.wait(lw, *wait)
            for half, n0, n in ((0, 0, 512), (1, 512, 512)) + (((2, 1024, 256),) if ctx_too else ()):
                core.mm(core.bank[:, 3 * b + half, 0:n], [(lambda k=k: wap[:, k, 128 * s:128 * s + 128],
                                                          lambda k=k: hT[:, k, n0:n0 + n]) for k in range(KD)])
            return T.last()

        for slab in range(2):
            lw = core.load[1 + slab](lambda e: e.dma_start(w[slab][:], win[:, :, 256 * slab:256 * slab + 256]))
            for s in range(2):
                u_tile = 2 * slab + s
                t = products(s, s, w[slab], lw, [A.last()] if u_tile > 1 else [], False)
                a = A(lambda e: e.activation(res[s][:, 0:SEQ], core.bank[:, 3 * s:3 * s + 2, :].rearrange("p a n -> p (a n)"),
                                             ACT.Copy), after=[t] + ([core.store[s].last()] if u_tile > 1 else []))
                core.store[s](lambda e: e.dma_start(dram["uT"][128 * u_tile:128 * u_tile + 128, :], res[s][:, 0:SEQ]), after=[a])
        xt = [sb(f"xt{b}", [P, NT + NC, P]) for b in range(2)]
        V(lambda e: e.memset(res[1][:], 0.0), after=[core.store[1].last()])
        before = [T.last(), A.last(), V.last(), zeroed, core.store[0].last(), core.store[1].last()]
        for q in (T, V, A, core.load[1], core.load[2]):
            q.wait(*before)

        def turn(s, i, j, done, before, marks):
            T.wait(*done)
            for q, m in ((0, 4), (1, 4), (2, 2)):
                bank = 6 + q % 2
                t = core.tr([(lambda c=c: core.bank[:, bank, 128 * c:128 * c + 128], lambda c=c: res[s][:, 512 * q + 128 * c:512 * q + 128 * c + 128])
                             for c in range(m)], ident, after=before(f"xe{q % 2}") if q < 2 else [first_ev])
                ev = A(lambda e: e.activation(xt[s][:, 4 * q:4 * q + m, :], core.bank[:, bank, 0:128 * m].rearrange("p (c n) -> p c n", c=m),
                                              ACT.Copy), after=[t] + (before("xst") if q == 0 else []))
                if q == 0:
                    first_ev = ev
                marks[f"xe{q % 2}_{j}"] = ev
            marks[f"xturn_{j}"] = T.last()
            marks[f"xst_{j}"] = core.store[2 + s](lambda e: e.dma_start(
                dram["xtok"].rearrange("(t p) n -> p t n", p=P)[:, :, bass.ds(i * 512 + 128 * j, 128)], xt[s][:]), after=[ev])

        def body(i, marks):
            prev = lambda k: [marks[k].last_round()] if k in marks else []
            turned = lambda j: [marks[f"xturn_{j - 1}"]] if j else prev("xturn_3")
            for slab in range(2):
                lw = core.load[1 + slab](lambda e: e.dma_start(w[slab][:], win[:, :, bass.ds(i * 512 + COL_XBC + 256 * slab, 256)]),
                                         after=prev(f"mm{slab}"))
                for s in range(2):
                    first = slab == 0
                    j = 2 * slab + s
                    before = (lambda k: prev(k + str(2 + s))) if first else (lambda k: [marks[k + str(s)]] if k + str(s) in marks else [])
                    t = products(s, s, w[slab], lw, before("ev"), True)
                    marks[f"mm{slab}"] = t
                    same = {"xe0": 1, "xe1": 1, "xst": 2}
                    turn(1 - s, i, j, [marks[f"silu{j - 1}"]] if j else prev("silu3"),
                         lambda k: [marks[f"{k}_{j - same[k]}"]] if j >= same[k] and f"{k}_{j - same[k]}" in marks else prev(f"{k}_{j - same[k] + 4}"), marks)
                    A(lambda e: e.activation(img[s][:, 1:1 + GRID_H, 1:1 + GRID_W],
                                             core.bank[:, 3 * s:3 * s + 2, :].rearrange("p a (r c) -> p (a r) c", c=GRID_W),
                                             ACT.Copy), after=[t] + before("conv"))
                    A(lambda e: e.activation(line[s][:, 1:1 + CTX], core.bank[:, 3 * s + 2, 0:CTX], ACT.Copy))
                    a = A(lambda e: e.activation(tap[s][:], taps[:, bass.ds(i * 4 + j, 1), :].rearrange("p a n -> p (a n)"),
                                                 ACT.Copy))
                    marks[f"ev{j}"] = a
                    V.wait(a, *before("silu"))
                    grid = acc[s][:, 0:SEQ].rearrange("p (r c) -> p r c", c=GRID_W)
                    for dy in range(3):
                        for dx in range(3):
                            src = img[s][:, dy:dy + GRID_H, dx:dx + GRID_W]
                            wt = tap[s][:, 3 * dy + dx:3 * dy + dx + 1]
                            if dy == dx == 0:
                                V(lambda e: e.tensor_scalar(grid, src, wt, None, ALU.mult))
                            else:
                                V(lambda e: e.scalar_tensor_tensor(out=grid, in0=src, scalar=wt, in1=grid,
                                                                   op0=ALU.mult, op1=ALU.add), own=True)
                    for dx in range(3):
                        wt = tap[s][:, 3 + dx:4 + dx]
                        if dx == 0:
                            V(lambda e: e.tensor_scalar(acc[s][:, SEQ:TOK], line[s][:, 0:CTX], wt, None, ALU.mult))
                        else:
                            V(lambda e: e.scalar_tensor_tensor(out=acc[s][:, SEQ:TOK], in0=line[s][:, dx:dx + CTX], scalar=wt,
                                                               in1=acc[s][:, SEQ:TOK], op0=ALU.mult, op1=ALU.add), own=True)
                    marks[f"conv{j}"] = V.last()
                    marks[f"silu{j}"] = A(lambda e: e.activation(res[s][:], acc[s][:], ACT.Silu, bias=tap[s][:, 9:10]),
                                          after=[V.last()] + before("st") + turned(j))
                    marks[f"st{j}"] = core.store[s](
                        lambda e: e.dma_start(dram["xbcT"][bass.ds(i * 512 + 128 * j, 128), :], res[s][:]), after=[A.last()])
        core.loop(NCT // 4, body)
        turn(1, NCT // 4, 0, [A.last()], lambda k: [A.last(), core.store[3].last()], {})
        core.settle()

        zw = [sb(f"zw{b}", [P, KD, 512]) for b in range(2)]
        zo = [sb(f"zo{b}", [P, 512]) for b in range(4)]

        def body(i, marks):
            prev = lambda k: [marks[k].last_round()] if k in marks else []
            for b in range(2):
                lw = core.load[1 + b](lambda e: e.dma_start(zw[b][:], win[:, :, bass.ds(i * 1024 + COL_Z + 512 * b, 512)]),
                                      after=prev(f"mm{b}"))
                T.wait(lw)
                for m in range(NT):
                    n = NT * b + m
                    s = n % 4
                    old = lambda k: [marks[f"{k}{n - 4}"]] if n >= 4 else prev(f"{k}{n + 12}")
                    t = core.mm(core.bank[:, s, :], [(lambda k=k: hT[:, k, 128 * m:128 * m + 128], lambda k=k: zw[b][:, k, :])
                                                     for k in range(KD)], after=old("ev"))
                    marks[f"mm{b}"] = t
                    marks[f"ev{n}"] = A(lambda e: e.activation(zo[s][:], core.bank[:, s, :], ACT.Silu), after=[t] + old("st"))
                    marks[f"st{n}"] = core.store[s](lambda e: e.dma_start(
                        dram["z"][128 * m:128 * m + 128, bass.ds(i * 1024 + 512 * b, 512)], zo[s][:]), after=[A.last()])
        core.loop(2, body)
        core.settle()
        wd = sb("wd", [P, KD, 2 * NH])
        lw = core.load[0](lambda e: e.dma_start(wd[:], win[:, :, COL_DT:COL_DT + 2 * NH]))
        T.wait(lw)
        for m in range(NT + NC):
            t = core.mm(core.bank[:, 0, 48 * m:48 * m + 48], [(lambda k=k: hT[:, k, 128 * m:128 * m + 128], lambda k=k: wd[:, k, :])
                                                             for k in range(KD)])
        V(lambda e: e.tensor_copy(tables["dt"][:].rearrange("p t h -> p (t h)"), core.bank[:, 0, 0:480]), after=[t])


def fourier(core, dram, tables):
    T, V, A, G = core.T, core.V, core.A, core.G
    with Room(core) as sb:
        groups = sb("f_groups", [P, 256])
        uc = [sb(f"f_u{b}", [P, 4, P]) for b in range(2)]
        AC = sb("f_AC", [P, NT, 2, DF])
        CS = sb("f_CS", [P, 2, KD, SEQ])
        lhs = [sb(f"f_lhs{b}", [P, NT, 2, P]) for b in range(2)]
        mT = sb("f_mT", [P, 4, SEQ])
        g = core.load[0](lambda e: e.dma_start(groups[:], dram["dft_groups"]))
        big = [core.load[3 + j](lambda e: e.dma_start(CS[:, j, :, :], dram["dft_seq"][j].rearrange("(k p) n -> p k n", p=P)))
               for j in range(2)]
        uv = dram["uT"].rearrange("(c p) n -> p c n", p=P)
        T.wait(g)

        def body(i, marks):
            prev = lambda k: [marks[k].last_round()] if k in marks else []
            for b in range(2):
                ld = core.load[1 + b](lambda e: e.dma_start(uc[b][:], uv[:, :, bass.ds(i * 256 + 128 * b, 128)]), after=prev(f"t{b}"))
                T.wait(ld, *prev(f"ev{b}"))
                for ct in range(4):
                    t = T(lambda e: e.matmul(core.bank[:, 2 * b + ct // 2, 256 * (ct % 2):256 * (ct % 2) + 256], uc[b][:, ct, :],
                                             groups[:], start=True, stop=True), inc=ct == 3)
                marks[f"t{b}"] = T.last()
                for half in range(2):
                    for cs in range(2):
                        V(lambda e: e.tensor_copy(
                            AC[:, bass.ds(i * 2 + b, 1), cs, 256 * half:256 * half + 256].rearrange("p a (c n) -> p (a c) n", c=2),
                            core.bank[:, 2 * b + half, :].rearrange("p (c s n) -> p c s n", c=2, s=2)[:, :, cs, :]),
                          after=[T.last()])
                marks[f"ev{b}"] = V.last()
        core.loop(NT // 2, body)
        T.wait(*big)
        G.wait(V.last())

        def body(i, marks):
            prev = lambda k: [marks[k].last_round()] if k in marks else []
            for b in range(2):
                g = G(lambda e: e.tensor_copy(lhs[b][:].rearrange("p t s n -> p (t s) n"),
                                              AC[:, :, :, bass.ds(i * 256 + 128 * b, 128)].rearrange("p t s n -> p (t s) n")),
                      after=prev(f"t{b}"))
                T.wait(g, *prev(f"ev{b}"))
                for half in range(2):
                    core.mm(core.bank[:, 4 + 2 * b + half, :],
                            [(lambda k=k, s=s: lhs[b][:, k, s, :], lambda k=k, s=s: CS[:, s, k, 512 * half:512 * half + 512])
                             for k in range(KD) for s in range(2)])
                marks[f"t{b}"] = T.last()
                marks[f"ev{b}"] = A(lambda e: e.activation(mT[:, bass.ds(i * 2 + b, 1), :].rearrange("p a n -> p (a n)"),
                                                           core.bank[:, 4 + 2 * b:6 + 2 * b, :].rearrange("p a n -> p (a n)"),
                                                           ACT.Copy), after=[T.last()])
        core.loop(2, body)
        wf = sb("f_w", [P, 4, DF])
        bf = sb("f_b", [P, DF])
        z = [sb(f"f_z{b}", [P, DF]) for b in range(2)]
        o = [sb(f"f_o{b}", [P, DF]) for b in range(2)]
        l4 = [sb(f"f_l{b}", [P, 4, P]) for b in range(2)]
        core.load[0](lambda e: e.dma_start(wf[:], dram["w_fourier"].rearrange("(k p) n -> p k n", p=P)))
        got = core.load[0](lambda e: e.dma_start(bf[:], row(dram["b_fourier"])))
        T.wait(got)
        V.wait(got)
        G.wait(A.last())

        def body(i, marks):
            prev = lambda k: [marks[k].last_round()] if k in marks else []
            for b in range(2):
                lz = core.load[1 + b](lambda e: e.dma_start(z[b][:], dram["z"][bass.ds(i * 256 + 128 * b, 128), 0:DF]), after=prev(f"v{b}"))
                g = G(lambda e: e.tensor_copy(l4[b][:], mT[:, :, bass.ds(i * 256 + 128 * b, 128)]), after=prev(f"t{b}"))
                t = core.mm(core.bank[:, b, :], [(lambda k=k: l4[b][:, k, :], lambda k=k: wf[:, k, :]) for k in range(4)],
                            after=[g] + prev(f"v{b}"))
                marks[f"t{b}"] = t
                V(lambda e: e.tensor_tensor(o[b][:], core.bank[:, b, :], bf[:], ALU.add), after=[t] + prev(f"st{b}"))
                marks[f"v{b}"] = V(lambda e: e.tensor_tensor(o[b][:], o[b][:], z[b][:], ALU.mult), after=[lz], own=True)
                marks[f"st{b}"] = core.store[b](lambda e: e.dma_start(dram["mix"][bass.ds(i * 256 + 128 * b, 128), 0:DF], o[b][:]),
                                                after=[V.last()])
        core.loop(NT // 2, body)


def constants():
    k = np.arange(P)
    mats = np.stack([k[:, None] == k, k[:, None] <= k, k[:, None] >= k, k[:, None] > k, k[:, None] < k,
                     np.ones((P, P), bool)]).astype(np.float32)
    n = np.arange(SEQ)
    ang = 2 * np.pi * ((n[:, None] * n) % SEQ) / SEQ
    scale = 1.0 / np.sqrt(SEQ * 64.0)
    g = np.arange(64)
    small = 2 * np.pi * ((g[:, None] * g) % 64) / 64
    groups = np.zeros((P, 2, P))
    for b in range(2):
        groups[64 * b:64 * b + 64, 0, 64 * b:64 * b + 64] = np.cos(small)
        groups[64 * b:64 * b + 64, 1, 64 * b:64 * b + 64] = np.sin(small)
    return {"mats": mats, "dft_seq": np.stack([np.cos(ang) * scale, -np.sin(ang) * scale]).astype(np.float32),
            "dft_groups": groups.reshape(P, 256).astype(np.float32),
            "counts": np.concatenate([np.arange(4, 0, -1), np.arange(32, 0, -1), 128 * np.arange(8),
                                      np.arange(48)]).astype(np.float32),
            "rope_inv": (10000.0 ** (-np.arange(32, dtype=np.float64) / 32)).astype(np.float32),
            "far": np.stack([np.where(k[None, :] <= k[:, None], 0.0, FAR),
                             np.where(k[None, :] // 64 <= k[:, None] // 64, 0.0, FAR)]).astype(np.float32)}


def load_tables(core, sb, dram):
    t = {"mats": sb("mats", [P, 6, P]), "eps": sb("eps", [P, 1]), "dt": sb("dt", [P, NT + NC, 2 * NH]),
         "logits": sb("logits", [P, NT, 36]), "weight": sb("weight", [P, 2, NT]), "slot": sb("slot", [P, 2, NT], I32),
         "expert": sb("expert", [P, 48], I32), "live": sb("live", [P, 1], I32)}
    core.V(lambda e: e.memset(t["eps"][:], EPS))
    core.load[0](lambda e: e.dma_start(t["mats"][:], dram["mats"].rearrange("m p n -> p m n")))
    core.settle()
    return t


def decays(core, dram, tables, sb):
    T, V, A = core.T, core.V, core.A
    n = NT + NC
    t = {k: sb("s_" + k, [P, n, 2 * NH]) for k in ("dt", "a", "ec", "dec", "et")}
    with Room(core) as s1:
        bias, an = s1("s_bias", [P, 2 * NH]), s1("s_an", [P, 2 * NH])
        p, q = s1("s_p", [P, n, 2 * NH]), s1("s_q", [P, n, 2 * NH])
        core.load[0](lambda e: e.dma_start(bias[:], row(dram["dt_bias"].rearrange("a h -> (a h)"))))
        got = core.load[0](lambda e: e.dma_start(an[:], row(dram["a_log"].rearrange("a h -> (a h)"))))
        a = A(lambda e: e.activation(an[:], an[:], ACT.Exp), after=[got])
        V(lambda e: e.tensor_tensor(p[:], tables["dt"][:], over(bias[:], 1, n), ALU.add), after=[got])
        V(lambda e: e.tensor_scalar(q[:], p[:], -1.0, None, ALU.mult), own=True)
        V(lambda e: e.tensor_tensor(q[:], q[:], p[:], ALU.min), own=True)
        A(lambda e: e.activation(q[:], q[:], ACT.Exp), after=[V.last()])
        A(lambda e: e.activation(q[:], q[:], ACT.Ln, bias=1.0), own=True)
        V(lambda e: e.scalar_tensor_tensor(out=t["dt"][:], in0=p[:], scalar=0.0, in1=q[:], op0=ALU.max, op1=ALU.add),
          after=[A.last()])
        V(lambda e: e.scalar_tensor_tensor(out=t["a"][:], in0=t["dt"][:], scalar=-1.0, in1=over(an[:], 1, n),
                                           op0=ALU.mult, op1=ALU.mult), own=True, after=[a])
        T.wait(V.last())
        mats = tables["mats"]
        T(lambda e: e.matmul(core.bank[:, 0, 0:480], mats[:, C_LE, :], t["a"][:].rearrange("p t h -> p (t h)"), start=True, stop=True), inc=False)
        T(lambda e: e.matmul(core.bank[:, 1, 0:480], mats[:, C_GE, :], t["a"][:].rearrange("p t h -> p (t h)"), start=True, stop=True), inc=False)
        T(lambda e: e.matmul(core.bank[:, 2, 0:480], mats[:, C_ONE, :], t["a"][:].rearrange("p t h -> p (t h)"), start=True, stop=True))
        for half in range(2):
            cols = slice(NH * half, NH * half + NH)
            cum = core.bank[:, half, 0:480].rearrange("p (t h) -> p t h", h=2 * NH)[:, :, cols]
            tot = core.bank[:, 2, 0:480].rearrange("p (t h) -> p t h", h=2 * NH)[:, :, cols]
            A(lambda e: e.activation(t["ec"][:, :, cols], cum, ACT.Exp), after=[T.last()])
            A(lambda e: e.activation(t["et"][:, :, cols], tot, ACT.Exp))
            V(lambda e: e.tensor_copy(p[:, :, cols], cum), own=True, after=[A.last()])
            V(lambda e: e.tensor_tensor(q[:, :, cols], tot, p[:, :, cols], ALU.subtract), own=True)
            A(lambda e: e.activation(q[:, :, cols], q[:, :, cols], ACT.Exp), after=[V.last()])
            V(lambda e: e.tensor_tensor(t["dec"][:, :, cols], q[:, :, cols], t["dt"][:, :, cols], ALU.mult), after=[A.last()])
    return t


def heads(ap):
    return ap.rearrange("p (h d) -> p h d", d=HP)


def state_space(core, dram, tables):
    T, V, A, G = core.T, core.V, core.A, core.G
    ident = tables["mats"][:, C_ID, :]
    with Room(core) as sb:
        t = decays(core, dram, tables, sb)
        xb = [sb(f"s_xb{b}", [P, 2 * NBC, P]) for b in range(2)]
        Xs = [sb(f"s_X{b}", [P, DS + NBC * NST]) for b in range(2)]
        xd = sb("s_xd", [P, DS])
        H = sb("s_H", [P, DS])
        HB = sb("s_HB", [P, NT, DS])
        xv = dram["xbcT"].rearrange("(t p) n -> p t n", p=P)

        def load_chunk(b, tile, after, free):
            return [core.load[1 + b](lambda e: e.dma_start(xb[b][:], xv[:, DS // P:, bass.ds(tile * P, P)]), after=after),
                    core.load[5 + b](lambda e: e.dma_start(Xs[b][:], dram["xtok"][bass.ds(tile * P, P), P:P + DS + NBC * NST]), after=free)]

        def weigh(tile, b, way, ready):
            return V(lambda e: e.tensor_tensor(heads(xd[:]), heads(Xs[b][:, 0:DS]),
                                               over(t["dec"][:, bass.ds(tile, 1), NH * way:NH * way + NH].rearrange("p a h -> p (a h)"), 2, HP),
                                               ALU.mult), after=ready)

        def state_step(tile, b, way, ready, weighed, free=((),) * 4):
            X = Xs[b]
            T.wait(weighed)
            cols = slice(NH * way, NH * way + NH)
            for g in range(NBC):
                core.mm(core.bank[:, 2 + g, 0:384], [(lambda: X[:, DS + NST * g:DS + NST * g + NST],
                                                      lambda: xd[:, 384 * g:384 * g + 384])], after=free[g])
            V(lambda e: e.tensor_tensor(heads(H[:]), heads(H[:]),
                                        over(t["et"][:, bass.ds(tile, 1), cols].rearrange("p a h -> p (a h)"), 2, HP), ALU.mult), own=True, after=ready)
            return V(lambda e: e.tensor_tensor(H[:].rearrange("p (g n) -> p g n", g=NBC), H[:].rearrange("p (g n) -> p g n", g=NBC),
                                               core.bank[:, 2:6, 0:384], ALU.add), own=True, after=[T.last()])

        V(lambda e: e.memset(H[:], 0.0))
        done = [V.last()]
        for tile in (9, 8):
            got = load_chunk(tile % 2, tile, [], [])
            done = [state_step(tile, tile % 2, 1, done, weigh(tile, tile % 2, 1, got + done))]

        T.wait(*done)
        A.wait(*done)
        core.load[1].wait(*done)

        def body(i, marks):
            prev = lambda k: [marks[k].last_round()] if k in marks else []
            for b in range(2):
                tile = i * -2 + (NT - 1 - b)
                free = ([marks["step0"]] if b and "step0" in marks else prev("step1"))
                ready = load_chunk(b, tile, prev(f"step{b}"), [])
                G(lambda e: e.tensor_copy(HB[:, bass.ds(tile, 1), :].rearrange("p a n -> p (a n)"), H[:]), after=free)
                marks[f"step{b}"] = state_step(tile, b, 1, [G.last()], weigh(tile, b, 1, ready + free))
        core.loop(NT // 2, body)
        core.settle()

        V(lambda e: e.memset(H[:], 0.0))
        done = [V.last()]
        for tile in (8, 9):
            got = load_chunk(tile % 2, tile, [], [])
            done = [state_step(tile, tile % 2, 0, done, weigh(tile, tile % 2, 0, got + done))]

        LE, GE = tables["mats"][:, C_LE, :], tables["mats"][:, C_GE, :]
        cbs = [sb(f"s_cb{b}", [P, 2, NBC, P]) for b in range(2)]
        xfs2 = [[sb(f"s_xf{b}{w}", [P, DS]) for w in range(2)] for b in range(2)]
        R = [sb(f"s_R{w}", [P, HG, P]) for w in range(2)]
        E = [sb(f"s_E{b}", [P, HG, P]) for b in range(2)]
        M = [[sb(f"s_M{b}{w}", [P, HG, P]) for w in range(2)] for b in range(2)]
        yts = [sb(f"s_y{b}", [P, DS]) for b in range(2)]
        y2 = [sb(f"s_y2{w}", [P, 384]) for w in range(2)]
        sq = sb("s_sq", [P, 384])
        skip = sb("s_skip", [P, NH])
        nw = sb("s_nw", [P, DS])
        zt = [sb(f"s_z{b}", [P, DS]) for b in range(2)]
        ss, sd, rs = (sb(f"s_{k}", [P, NBC]) for k in ("ss", "sd", "rs"))
        core.load[0](lambda e: e.dma_start(skip[:], row(dram["d_skip"])))
        got = core.load[0](lambda e: e.dma_start(nw[:], row(dram["ssd_norm_w"])))
        for e in core.engines:
            e.wait_ge(core.load[0].sem, core.load[0].n)
            for x in (T, V, A):
                e.wait_ge(x.sem, x.n)

        ROUND = 4

        class Chunk:

            def __init__(self, i, j, marks):
                self.tile, self.j, self.b, self.marks = i * ROUND + j, j, j % 2, marks
                self.X, self.yt, self.cb, self.xf = Xs[self.b], yts[self.b], cbs[self.b], xfs2[self.b]
                self.dT, self.evE, self.mE, self.mG, self.yT, self.offs = {}, {}, {}, {}, {}, {}

            def ago(self, k, n):
                if self.j >= n:
                    return [self.marks[f"{k}{self.j - n}"]] if f"{k}{self.j - n}" in self.marks else []
                k = f"{k}{self.j - n + ROUND}"
                return [self.marks[k].last_round()] if k in self.marks else []

            def mark(self, k, t):
                self.marks[f"{k}{self.j}"] = t

            def col(self, name, a, n):
                return t[name][:, bass.ds(self.tile, 1), a:a + n].rearrange("p a h -> p (a h)")

            def head(self):
                b, tile, X = self.b, self.tile, self.X
                got, gx = load_chunk(b, tile, self.ago("products", 2), self.ago("step", 2))
                self.lz = core.load[3 + b](lambda e: e.dma_start(zt[b][:], dram["z"][bass.ds(tile * P, P), DF:DF + DS]), after=self.ago("gate", 2))
                self.gx = gx
                for g in range(NBC):
                    core.mm(core.bank[:, 1, 128 * g:128 * g + 128], [(lambda: xb[b][:, g, :], lambda: xb[b][:, NBC + g, :])],
                            after=self.ago("lastE", 1) + [got] if g == 0 else [])
                cbt = T.last()
                for w, mask in ((0, LE), (1, GE)):
                    V(lambda e: e.tensor_tensor(self.cb[:, w, :, :], core.bank[:, 1, :].rearrange("p (g n) -> p g n", g=NBC),
                                                over(mask, 1, NBC), ALU.mult), after=[cbt] + self.ago("MG", 2) + self.ago("M", 2))
                self.cbv = V.last()
                self.differences(0)
                wait = [gx] + self.ago("products", 2)
                self.xfs = [Q(lambda e: e.tensor_tensor(heads(self.xf[w][:]), heads(X[:, 0:DS]), over(self.col("dt", NH * w, NH), 2, HP), ALU.mult),
                              after=wait) for w, Q in ((0, V), (1, G))]
                self.mark("xf", G.last())
                self.weights(0)
                self.differences(1)
                self.skipped = G(lambda e: e.tensor_tensor(heads(self.yt[:]), heads(X[:, 0:DS]), over(skip[:], 2, HP), ALU.mult),
                                 after=[gx] + self.ago("st", 2))
                self.mark("skip", G.last())

            def differences(self, g):
                rs_ = [Q(lambda e: e.tensor_tensor(R[w][:], over(mask, 1, HG), over(self.col("a", NH * w + HG * g, HG), 2, P), ALU.mult),
                         after=[self.dT[g - 1]] if g else self.ago("lastD", 1)) for w, Q, mask in ((0, V, LE), (1, G, GE))]
                T.wait(*rs_, *([self.evE[g - 1]] if g else self.ago("lastE", 1) + [self.cbv]))
                for half in range(2):
                    for w, m in ((0, C_GT), (1, C_LT)):
                        T(lambda e: e.matmul(core.bank[:, half, 0:384], tables["mats"][:, m, :],
                                             R[w][:, 3 * half:3 * half + 3, :].rearrange("p h n -> p (h n)"),
                                             start=w == 0, stop=w == 1), inc=half == 1 and w == 1)
                self.dT[g] = T.last()
                s = g % 2
                self.evE[g] = A(lambda e: e.activation(E[s][:].rearrange("p (a h) n -> p a (h n)", a=2), core.bank[:, 0:2, 0:384], ACT.Exp),
                                after=[self.dT[g]] + ([self.mE[g - 2], self.mG[g - 2]] if g > 1 else self.ago("M", 1) + self.ago("MG", 1)))

            def weights(self, g):
                s = g % 2
                wait = [self.evE[g], self.cbv] + ([self.yT[g - 2]] if g > 1 else self.ago(f"products_{g}_", 1))
                for w, Q, m in ((0, V, self.mE), (1, G, self.mG)):
                    m[g] = Q(lambda e: e.tensor_tensor(M[s][w][:], E[s][:], over(self.cb[:, w, g, :], 1, HG), ALU.mult), after=wait)

            def products(self, g):
                s, y0, b = g % 2, 2 + 3 * (g % 2), self.b
                T.wait(self.mE[g], self.mG[g], *self.xfs, *([self.offs[g - 2]] if g > 1 else self.ago("step", 1) + self.ago("gathered", 1)))
                for h in range(HG):
                    c0 = HP * (HG * g + h)
                    for w in range(2):
                        T(lambda e: e.matmul(core.bank[:, y0, HP * h:HP * h + HP], M[s][w][:, h, :], self.xf[w][:, c0:c0 + HP],
                                             start=w == 0, stop=w == 1), inc=False)
                T(lambda e: e.matmul(core.bank[:, y0 + 1, 0:384], xb[b][:, NBC + g, :], H[:, 384 * g:384 * g + 384], start=True, stop=True), inc=False)
                T(lambda e: e.matmul(core.bank[:, y0 + 2, 0:384], xb[b][:, NBC + g, :],
                                     HB[:, bass.ds(self.tile, 1), 384 * g:384 * g + 384].rearrange("p a n -> p (a n)"), start=True, stop=True))
                self.yT[g] = T.last()
                if g > 1:
                    self.mark(f"products_{g - 2}_", T.last())
                self.mark("products", T.last())

            def gather(self, g):
                y0 = 2 + 3 * (g % 2)
                y = self.yt[:, 384 * g:384 * g + 384]
                for w in range(2):
                    V(lambda e: e.tensor_tensor(heads(y2[w][:]), heads(core.bank[:, y0 + 1 + w, 0:384]),
                                                over(self.col("ec", NH * w + HG * g, HG), 2, HP), ALU.mult),
                      after=[self.yT[g]] + ([self.offs[g - 1]] if g else self.ago("gathered", 1)))
                V(lambda e: e.tensor_tensor(y, y, core.bank[:, y0, 0:384], ALU.add), after=[self.skipped])
                for w in range(2):
                    V(lambda e: e.tensor_tensor(y, y, y2[w][:], ALU.add), own=True)
                self.offs[g] = V.last()
                self.mark("gathered", V.last())

            def groups(self, ahead, between):
                for g in range(NBC):
                    if g + 1 < NBC:
                        self.weights(g + 1)
                    if g == 1:
                        weighed = weigh(self.tile, self.b, 0, [self.gx] + self.ago("step", 1))
                    self.products(g)
                    if g + 2 < NBC:
                        self.differences(g + 2)
                    if g == NBC - 1:
                        self.mark("M", self.mE[3]), self.mark("MG", self.mG[3]), self.mark("lastD", self.dT[3]), self.mark("lastE", self.evE[3])
                        ahead()
                    self.gather(g)
                    if g == 0:
                        between()
                even, odd = [self.offs[2]], [self.offs[3]]
                self.mark("step", state_step(self.tile, self.b, 0, [self.yT[3]], weighed, (even, even, even, odd)))

            def gate(self):
                yt = self.yt
                V(lambda e: e.tensor_tensor(yt[:], yt[:], zt[self.b][:], ALU.mult), own=True, after=[self.lz, self.offs[3]])
                self.mark("gate", V.last())
                for g in range(NBC):
                    y = yt[:, 384 * g:384 * g + 384]
                    V(lambda e: e.tensor_tensor_reduce(out=sq[:], in0=y, in1=y, scale=1.0 / 384, scalar=0.0, op0=ALU.mult, op1=ALU.add,
                                                       accum_out=ss[:, g:g + 1]), own=True)
                A(lambda e: e.activation(sd[:], ss[:], ACT.Sqrt, bias=tables["eps"][:, 0:1]), after=[V.last()])
                V(lambda e: e.reciprocal(rs[:], sd[:]), after=[A.last()])
                for g in range(NBC):
                    y = yt[:, 384 * g:384 * g + 384]
                    V(lambda e: e.scalar_tensor_tensor(out=y, in0=y, scalar=rs[:, g:g + 1], in1=nw[:, 384 * g:384 * g + 384],
                                                       op0=ALU.mult, op1=ALU.mult), own=g == 0)
                self.mark("st", core.store[self.b](lambda e: e.dma_start(dram["mix"][bass.ds(self.tile * P, P), DF:DF + DS], yt[:]), after=[V.last()]))

        def body(i, marks):
            chunks = [Chunk(i, j, marks) for j in range(ROUND)]
            chunks[0].head()
            for j, c in enumerate(chunks):
                more = j + 1 < ROUND
                c.groups(chunks[j + 1].head if more else lambda: None, chunks[j - 1].gate if j else lambda: None)
            chunks[-1].gate()
        core.loop(NT // ROUND, body)


def prev_of(marks):
    return lambda k: [marks[k].last_round()] if k in marks else []


def turn_rows(core, out, src, n, ident, banks, after, free):
    for q in range((n + 3) // 4):
        m = min(4, n - 4 * q)
        bank = banks[q % len(banks)]
        wait = ([] if q else list(after)) + (free[q % len(banks)] if q < len(banks) else [evs[q - len(banks)]])
        if q == 0:
            evs = []
        t = core.tr([(lambda j=j: core.bank[:, bank, 128 * j:128 * j + 128],
                      lambda j=j: src[:, 128 * (4 * q + j):128 * (4 * q + j) + 128]) for j in range(m)], ident, after=wait)
        evs.append(core.A(lambda e: e.activation(out[:, 4 * q:4 * q + m, :],
                                                 core.bank[:, bank, 0:128 * m].rearrange("p (j n) -> p j n", j=m), ACT.Copy), after=[t]))
    return t, evs[-1]


def close_first(core, dram, tables):
    T, V, A = core.T, core.V, core.A
    ident = tables["mats"][:, C_ID, :]
    with Room(core) as sb:
        KM = 2 * D // P
        w = sb("c_w", [P, KM, D])
        gate, fin, gain, shift = (sb("c_" + k, [P, D]) for k in ("gate", "fin", "gain", "shift"))
        x, y, x1, h = (sb("c_" + k, [P, D]) for k in ("x", "y", "x1", "h"))
        mix = [sb(f"c_mix{b}", [P, 2 * D]) for b in range(2)]
        mT = sb("c_mT", [P, KM, P])
        norm = Norm(core, sb, "c_n")
        wl = [core.load[5 + j](lambda e: e.dma_start(w[:, 4 * j:4 * j + 4, :], dram["w_out"].rearrange("(k p) n -> p k n", p=P)[:, 4 * j:4 * j + 4, :]))
              for j in range(4)]
        core.load[9](lambda e: e.dma_start(gate[:], row(dram["mods"][0, 2 * D:3 * D])))
        gl = core.load[9](lambda e: e.dma_start(fin[:], row(dram["final_norm_w"])))
        m2 = dram["mod2"][0, :]
        gain_rows(core, gain[:], dram["norm1_g_2"], m2[D:2 * D], shift[:], m2[0:D], y[:])
        V.wait(gl)
        T.wait(*wl)

        def body(i, marks):
            for b in range(2):
                before = lambda k: ([marks[k + "0"]] if k + "0" in marks else []) if b else prev_of(marks)(k + "1")
                at = bass.ds(i * 256 + 128 * b, 128)
                lm = core.load[1 + b](lambda e: e.dma_start(mix[b][:], dram["mix"][at, :]), after=prev_of(marks)(f"t{b}"))
                lx = core.load[3](lambda e: e.dma_start(x[:], dram["x"][at, :]), after=before("x"))
                t, ev = turn_rows(core, mT, mix[b][:], KM, ident, (4, 5), [lm], [before("evt"), before("evt")])
                marks[f"t{b}"], marks[f"evt{b}"] = t, ev
                T.wait(ev, *before("mul"))
                for half in range(2):
                    core.mm(core.bank[:, half, :], [(lambda k=k: mT[:, k, :], lambda k=k: w[:, k, 512 * half:512 * half + 512]) for k in range(KM)])
                marks[f"mm{b}"] = T.last()
                marks[f"mul{b}"] = V(lambda e: e.tensor_tensor(y[:], core.bank[:, 0:2, :].rearrange("p a n -> p (a n)"), gate[:], ALU.mult),
                                     after=[T.last()], own=True)
                marks[f"x{b}"] = V(lambda e: e.tensor_tensor(y[:], y[:], x[:], ALU.add), after=[lx], own=True)
                V.wait(norm.rstd(y[:], tables["eps"][:, 0:1], [V.last()]))
                norm.apply(x1[:], y[:], fin[:], after=before("stx"))
                marks[f"stx{b}"] = core.store[0](lambda e: e.dma_start(dram["x1"][at, :], x1[:]), after=[V.last()])
                V.wait(norm.rstd(x1[:], tables["eps"][:, 0:1], [V.last()]))
                norm.apply(h[:], x1[:], gain[:], shift[:], after=before("sth"))
                marks[f"sth{b}"] = core.store[1](lambda e: e.dma_start(dram["h1"][at, :], h[:]), after=[V.last()])
        core.loop(NT // 2, body)


COLS2 = 4816
C_FQ, C_FK, C_FV, C_FL, C_DQ, C_DK, C_DV, C_IQ, C_IK, C_IW, C_GF = 0, 512, 1024, 1536, 1544, 2056, 2120, 2184, 2696, 2760, 2768


def project_second(core, dram, tables):
    T, V, A = core.T, core.V, core.A
    ident = tables["mats"][:, C_ID, :]
    with Room(core) as sb:
        hT = sb("p_hT", [P, KD, SEQ])
        h = [sb(f"p_h{b}", [P, D]) for b in range(2)]
        w = [sb(f"p_w{b}", [P, KD, 512]) for b in range(2)]
        o = [sb(f"p_o{b}", [P, 512]) for b in range(4)]
        wv = dram["w_in_2"].rearrange("(k p) n -> p k n", p=P)

        def body(i, marks):
            prev = prev_of(marks)
            for b in range(2):
                ld = core.load[1 + b](lambda e: e.dma_start(h[b][:], dram["h1"][bass.ds(i * 256 + 128 * b, 128), :]), after=prev(f"t{b}"))
                for half in range(2):
                    t = core.tr([(lambda k=k: core.bank[:, 2 * b + half, 128 * k:128 * k + 128],
                                  lambda k=k: h[b][:, 512 * half + 128 * k:512 * half + 128 * k + 128]) for k in range(4)], ident,
                                after=[ld] + prev(f"ev{b}"))
                    marks[f"t{b}"] = t
                    marks[f"ev{b}"] = A(lambda e: e.activation(hT[:, 4 * half:4 * half + 4, bass.ds(i * 256 + 128 * b, 128)],
                                                               core.bank[:, 2 * b + half, :].rearrange("p (k n) -> p k n", k=4),
                                                               ACT.Copy), after=[t])
        core.loop(NT // 2, body)
        core.settle()

        def chunk(b, at, n, marks, prev):
            lw = core.load[3 + b](lambda e: e.dma_start(w[b][:, :, 0:n], wv[:, :, at]), after=prev(f"mm{b}"))
            T.wait(lw)
            for m in range(NT):
                j = NT * b + m
                s = j % 4
                old = lambda k: ([marks[f"{k}{j - 4}"]] if f"{k}{j - 4}" in marks else []) if j >= 4 else prev(f"{k}{j + 12}")
                t = core.mm(core.bank[:, s, 0:n], [(lambda k=k: hT[:, k, 128 * m:128 * m + 128], lambda k=k: w[b][:, k, 0:n])
                                                   for k in range(KD)], after=old("ev"))
                marks[f"mm{b}"] = t
                Q, f = (A, lambda e: e.activation(o[s][:, 0:n], core.bank[:, s, 0:n], ACT.Copy)) if s % 2 else \
                       (V, lambda e: e.tensor_copy(o[s][:, 0:n], core.bank[:, s, 0:n]))
                marks[f"ev{j}"] = Q(f, after=[t] + old("st"))
                marks[f"st{j}"] = core.store[s](lambda e: e.dma_start(dram["proj"][128 * m:128 * m + 128, at], o[s][:, 0:n]), after=[Q.last()])

        def body(i, marks):
            for b in range(2):
                chunk(b, bass.ds(i * 1024 + 512 * b, 512), 512, marks, prev_of(marks))
        core.loop(4, body)
        core.settle()
        marks = {}
        chunk(0, slice(4096, 4608), 512, marks, lambda k: [])
        for s in range(4):
            marks[f"ev{NT - 4 + s}"], marks[f"st{NT - 4 + s}"] = marks[f"ev{NT - 4 + s}"], marks[f"st{NT - 4 + s}"]
        chunk(1, slice(4608, COLS2), COLS2 - 4608, marks, lambda k: [])


ROPE_C1, ROPE_C2, ROPE_C3 = 6.28125, 0.0019353071693331003, 1.0253131677018246e-11
MAGIC = 1.5 * 2 ** 23


def prepare_heads(core, dram, tables):
    T, V, A, G = core.T, core.V, core.A, core.G
    ident = tables["mats"][:, C_ID, :]
    with Room(core) as sb:
        ld = core.load
        gq, gk, dgq, dgk = (sb("h_" + k, [P, 64]) for k in ("gq", "gk", "dgq", "dgk"))
        bf = sb("h_bf", [P, 8])
        inv = sb("h_inv", [P, 32])
        posi, pos = sb("h_posi", [P, NT], I32), sb("h_pos", [P, NT])
        for t, k in ((gq, "qn_fox_2"), (gk, "kn_fox_2"), (dgq, "qn_dsa_2"), (dgk, "kn_dsa_2"), (bf, "b_fgt_2"), (inv, "rope_inv")):
            ld[0](lambda e: e.dma_start(t[:], row(dram[k])))
        with core.nc.allow_non_contiguous_dma(reason="one position a partition"):
            got = ld[0](lambda e: e.dma_start(posi[:], dram["positions_2"].rearrange("(t p) -> p t", p=P)))
        ang, red, kk = (sb("h_" + k, [P, NT, 32]) for k in ("ang", "red", "kk"))
        cos, sin = sb("h_cos", [P, NT, 32]), sb("h_sin", [P, NT, 32])
        V(lambda e: e.tensor_copy(pos[:], posi[:]), after=[got])
        V(lambda e: e.tensor_tensor(ang[:], over(pos[:], 2, 32), over(inv[:], 1, NT), ALU.mult), own=True)
        for table, turn in ((sin, 0.0), (cos, 0.25)):
            V(lambda e: e.tensor_scalar(kk[:], ang[:], 1.0 / (2 * np.pi), turn, ALU.mult, ALU.add), own=True)
            V(lambda e: e.tensor_scalar(kk[:], kk[:], MAGIC, None, ALU.add), own=True)
            V(lambda e: e.tensor_scalar(kk[:], kk[:], -MAGIC, None, ALU.add), own=True)
            V(lambda e: e.scalar_tensor_tensor(out=red[:], in0=kk[:], scalar=-ROPE_C1, in1=ang[:], op0=ALU.mult, op1=ALU.add), own=True, after=[A.last()])
            V(lambda e: e.scalar_tensor_tensor(out=red[:], in0=kk[:], scalar=-ROPE_C2, in1=red[:], op0=ALU.mult, op1=ALU.add), own=True)
            V(lambda e: e.scalar_tensor_tensor(out=red[:], in0=kk[:], scalar=-ROPE_C3, in1=red[:], op0=ALU.mult, op1=ALU.add), own=True)
            if turn:
                V(lambda e: e.tensor_scalar(red[:], red[:], 2 * np.pi * turn, None, ALU.add), own=True)
            V(lambda e: e.tensor_scalar(red[:], red[:], 3.1415925, -3.1415925, ALU.min, ALU.max), own=True)
            A(lambda e: e.activation(table[:], red[:], ACT.Sin), after=[V.last()])
        V.wait(A.last())
        core.settle()

        x = [sb(f"h_x{b}", [P, C_GF]) for b in range(2)]
        sq = sb("h_sq", [P, 2 * 512])
        ss, sd, rs = (sb("h_" + k, [P, 26]) for k in ("ss", "sd", "rs"))
        r1, r2, r3 = (sb("h_" + k, [P, 8, 32]) for k in ("r1", "r2", "r3"))
        lf, l2, ft, carry = (sb("h_" + k, [P, 8]) for k in ("lf", "l2", "ft", "carry"))
        qT = sb("h_qT", [P, 17, P])
        V(lambda e: e.memset(carry[:], 0.0))
        V.wait(V.last())

        h3 = lambda ap, n=64: ap.rearrange("p (h d) -> p h d", d=n)

        def tile(b, i, marks):
            before = lambda k: ([marks[k + "0"]] if k + "0" in marks else []) if b else prev_of(marks)(k + "1")
            at = bass.ds(i * 256 + 128 * b, 128)
            ti = i * 2 + b
            X = x[b]
            got = ld[1 + b](lambda e: e.dma_start(X[:], dram["proj"][at, 0:C_GF]), after=prev_of(marks)(f"t{b}"))
            A(lambda e: e.activation(sq[:], X[:, C_FQ:C_FV], ACT.Square), after=[got] + before("sq2"))
            V(lambda e: e.tensor_reduce(ss[:, 0:16], h3(sq[:]), AX.X, ALU.add), after=[A.last()])
            A(lambda e: e.activation(sq[:, 0:576], X[:, C_DQ:C_DV], ACT.Square), after=[V.last()])
            v = V(lambda e: e.tensor_reduce(ss[:, 16:25], h3(sq[:, 0:576]), AX.X, ALU.add), after=[A.last()], own=True)
            marks[f"sq2{b}"] = v
            A(lambda e: e.activation(sd[:, 0:25], ss[:, 0:25], ACT.Sqrt, bias=tables["eps"][:, 0:1], scale=1.0 / 64), after=[v])
            V(lambda e: e.reciprocal(rs[:, 0:25], sd[:, 0:25]), after=[A.last()])
            for c, r0, nh, gain, scale in ((C_FQ, 0, 8, gq, 0.125), (C_FK, 8, 8, gk, 1.0), (C_DQ, 16, 8, dgq, 0.125), (C_DK, 24, 1, dgk, 1.0)):
                blk = h3(X[:, c:c + 64 * nh])
                V(lambda e: e.tensor_tensor(blk, blk, over(rs[:, r0:r0 + nh], 2, 64), ALU.mult), own=True)
                V(lambda e: e.scalar_tensor_tensor(out=blk, in0=blk, scalar=scale, in1=over(gain[:], 1, nh), op0=ALU.mult, op1=ALU.mult), own=True)
            for c, nh in ((C_DQ, 8), (C_DK, 1), (C_IQ, 8), (C_IK, 1)):
                blk = h3(X[:, c:c + 64 * nh])
                a, bb = blk[:, :, 0:32], blk[:, :, 32:64]
                cs = over(cos[:, bass.ds(ti, 1), :].rearrange("p a n -> p (a n)"), 1, nh)
                sn = over(sin[:, bass.ds(ti, 1), :].rearrange("p a n -> p (a n)"), 1, nh)
                V(lambda e: e.tensor_tensor(r1[:, 0:nh, :], a, sn, ALU.mult), own=True)
                V(lambda e: e.tensor_tensor(r2[:, 0:nh, :], bb, sn, ALU.mult), own=True)
                V(lambda e: e.tensor_tensor(r3[:, 0:nh, :], a, cs, ALU.mult), own=True)
                V(lambda e: e.tensor_tensor(bb, bb, cs, ALU.mult), own=True)
                V(lambda e: e.tensor_tensor(a, r3[:, 0:nh, :], r2[:, 0:nh, :], ALU.subtract), own=True)
                V(lambda e: e.tensor_tensor(bb, bb, r1[:, 0:nh, :], ALU.add), own=True)
            ready = V.last()
            V(lambda e: e.tensor_tensor(lf[:], X[:, C_FL:C_FL + 8], bf[:], ALU.add), own=True, after=before("ft"))
            V(lambda e: e.tensor_scalar(l2[:], lf[:], -1.0, None, ALU.mult), own=True)
            V(lambda e: e.tensor_tensor(l2[:], l2[:], lf[:], ALU.min), own=True)
            A(lambda e: e.activation(l2[:], l2[:], ACT.Exp), after=[V.last()])
            A(lambda e: e.activation(l2[:], l2[:], ACT.Ln, bias=1.0), own=True)
            V(lambda e: e.tensor_scalar(lf[:], lf[:], 0.0, None, ALU.min), own=True)
            V(lambda e: e.tensor_tensor(lf[:], lf[:], l2[:], ALU.subtract), own=True, after=[A.last()])
            T.wait(V.last(), *before("carry"))
            T(lambda e: e.matmul(core.bank[:, 0, 0:8], tables["mats"][:, C_LE, :], lf[:], start=True, stop=True), inc=False)
            T(lambda e: e.matmul(core.bank[:, 0, 8:16], tables["mats"][:, C_ONE, :], lf[:], start=True, stop=True))
            V(lambda e: e.scalar_tensor_tensor(out=ft[:], in0=core.bank[:, 0, 0:8], scalar=-1.0, in1=carry[:], op0=ALU.mult, op1=ALU.subtract), after=[T.last()])
            V(lambda e: e.tensor_tensor(carry[:], carry[:], core.bank[:, 0, 8:16], ALU.add), own=True)
            marks[f"carry{b}"] = V.last()
            blocks = [X[:, C_FQ + 128 * j:C_FQ + 128 * j + 128] for j in range(8)] + [X[:, C_DQ + 128 * j:C_DQ + 128 * j + 128] for j in range(4)] \
                + [X[:, C_IQ + 128 * j:C_IQ + 128 * j + 128] for j in range(4)]
            T.wait(ready)
            evs = []
            for q in range(4):
                bank = 1 + q
                t = core.tr([(lambda j=j: core.bank[:, bank, 128 * j:128 * j + 128], lambda j=j: blocks[4 * q + j]) for j in range(4)],
                            ident, after=before(f"ev{q}"))
                marks[f"ev{q}{b}"] = A(lambda e: e.activation(qT[:, 4 * q:4 * q + 4, :], core.bank[:, bank, :].rearrange("p (j n) -> p j n", j=4),
                                                              ACT.Copy), after=[t] + (before("st") if q == 0 else []))
            core.tr([(lambda: core.bank[0:8, 5, 256:384], lambda: ft[:]),
                     (lambda: core.bank[0:64, 5, 0:128], lambda: X[:, C_DK:C_DK + 64]),
                     (lambda: core.bank[0:64, 5, 128:256], lambda: X[:, C_IK:C_IK + 64])], ident, after=before("ev4") + [V.last()])
            marks[f"t{b}"] = T.last()
            marks[f"ft{b}"] = T.last()
            A(lambda e: e.activation(kx[0:64, :], core.bank[0:64, 5, 0:256], ACT.Copy), after=[T.last()] + before("st2"))
            marks[f"ev4{b}"] = A(lambda e: e.activation(fx[0:8, :], core.bank[0:8, 5, 256:384], ACT.Copy))
            for hh in range(2):
                half = slice(64 * hh, 64 * hh + 64)
                for name, j0 in (("fqT", 0), ("fkT", 4), ("dqT", 8), ("iqT", 12)):
                    core.store[0](lambda e: e.dma_start(dram[name][hh::2, 0:64, at].rearrange("h d n -> d h n"), qT[half, j0:j0 + 4, :]),
                                  after=[marks[f"ev3{b}"]])
            marks[f"st{b}"] = core.store[0].last()
            core.store[1](lambda e: e.dma_start(dram["dkT"][:, at], kx[0:64, 0:128]), after=[A.last()])
            core.store[1](lambda e: e.dma_start(dram["ikT"][:, at], kx[0:64, 128:256]))
            marks[f"st2{b}"] = core.store[1](lambda e: e.dma_start(dram["fkT"][:, 64, at], fx[0:8, :]))

        kx, fx = sb("h_kx", [64, 256]), sb("h_fx", [8, P])

        def body(i, marks):
            for b in range(2):
                tile(b, i, marks)
        core.loop(NT // 2, body)


TOPK, NAH, HD = 256, 8, 64
DONE = -3e38


def attend(core, dram, tables):
    T, V, A = core.T, core.V, core.A
    ident = tables["mats"][:, C_ID, :]
    with Room(core) as sb:
        far = sb("a_far", [P, 2, SEQ])
        fkT, dkT, ikT = sb("a_fkT", [HD + 1, NAH, SEQ]), sb("a_dkT", [HD, SEQ]), sb("a_ikT", [HD, SEQ])
        fv, dv, iw = sb("a_fv", [P, NT, 512]), sb("a_dv", [P, NT, HD]), sb("a_iw", [P, NT, NAH])
        qt = {k: [sb(f"a_{k}{b}", [HD + 1, NAH, P]) for b in range(2)] for k in ("fox", "dsa", "idx")}
        Sm, Pb, R = ([sb(f"a_{k}{b}", [P, SEQ]) for b in range(2)] for k in ("Sm", "Pb", "R"))
        PT = [sb(f"a_PT{b}", [P, NT, P]) for b in range(2)]
        score = [sb(f"a_score{b}", [P, SEQ]) for b in range(3)]
        best = sb("a_best", [P, 8])
        mx, nm, sm, rc = ([sb(f"a_{k}{b}", [P, 1]) for b in range(4)] for k in ("mx", "nm", "sm", "rc"))
        ob = {k: [sb(f"a_o{k}{b}", [P, 512]) for b in range(2)] for k in ("fox", "dsa")}

        V(lambda e: e.memset(far[:], 0.0))
        for b in range(2):
            V(lambda e: e.memset(qt["fox"][b][HD:HD + 1, :, :], 1.0))
        ld = core.load
        ld[0](lambda e: e.dma_start(fkT[:], dram["fkT"].rearrange("h d n -> d h n")), after=[V.last()])
        ld[0](lambda e: e.dma_start(dkT[:], dram["dkT"]))
        ld[0](lambda e: e.dma_start(ikT[:], dram["ikT"]))
        pv = dram["proj"].rearrange("(t p) n -> p t n", p=P)
        ld[0](lambda e: e.dma_start(fv[:], pv[:, :, C_FV:C_FV + 512]))
        ld[0](lambda e: e.dma_start(dv[:], pv[:, :, C_DV:C_DV + HD]))
        ld[0](lambda e: e.dma_start(iw[:], pv[:, :, C_IW:C_IW + NAH]))
        got = ld[0](lambda e: e.dma_start(far[:, :, SEQ - P:SEQ], dram["far"].rearrange("m p n -> p m n")))
        T.wait(got)
        V.wait(got)

        order = [("idx", 2), ("fox", 0), ("fox", 1), ("fox", 2), ("dsa", 0), ("dsa", 1), ("fox", 3), ("idx", 3), ("fox", 4), ("dsa", 2), ("idx", 4),
                 ("fox", 5), ("dsa", 3), ("idx", 5), ("fox", 6), ("idx", 6), ("dsa", 4), ("fox", 7), ("idx", 7), ("dsa", 5),
                 ("dsa", 6), ("dsa", 7)]
        units = [(kind, j, h) for kind, j in order for h in range(NAH)]
        qload, qfree, count = {}, {}, {}
        done = {k: {} for k in "SEXNO"}
        done["N"] = {}
        scored, biased, bias_read, stored = {}, {}, {}, {}
        pending = []

        def load_queries(kind, j):
            n = count[kind] = count.get(kind, -1) + 1
            src = dram[{"fox": "fqT", "dsa": "dqT", "idx": "iqT"}[kind]]
            stream = ld[1 + 2 * ("fox", "dsa", "idx").index(kind) + n % 2]
            buf = qt[kind][n % 2]
            qload[kind, j] = (buf, stream(lambda e: e.dma_start(buf[0:HD, :, :], src[:, :, P * j:P * j + P].rearrange("h d n -> d h n")),
                                          after=[qfree[kind, n - 2]] if n > 1 else [V.last()]))
            qfree[kind, j, "n"] = n

        def round_of(j):
            s = score[j % 3][:, 0:P * (j + 1)]
            def go(last):
                V(lambda e: e.max(best[:], s), own=True, after=scored[j])
                V(lambda e: e.match_replace(s, best[:], s, DONE), own=True)
                if last:
                    biased[j] = V(lambda e: e.tensor_scalar(s, s, DONE, FAR, ALU.is_gt, ALU.mult), own=True)
            return go

        def fill(n=None, until=None):
            while pending and (n is None or n > 0) and (until is None or until not in biased):
                j, go, last = pending.pop(0)
                go(last)
                n = None if n is None else n - 1

        def step_s(n):
            kind, j, h = units[n]
            L = P * (j + 1)
            if h == 0 and (kind, j) not in qload:
                load_queries(kind, j)
            buf, got = qload[kind, j]
            T.wait(got, *done["E"].get(n - 2, []))
            depth = HD + 1 if kind == "fox" else HD
            for c in range(0, L, 512):
                m = min(512, L - c)
                keys = {"fox": lambda: fkT[:, h, c:c + m], "dsa": lambda: dkT[:, c:c + m], "idx": lambda: ikT[:, c:c + m]}[kind]
                core.mm(core.bank[:, 2 * (n % 2) + c // 512, 0:m], [(lambda: buf[0:depth, h, :], keys)])
            done["S"][n] = T.last()
            if h == NAH - 1:
                qfree[kind, qfree[kind, j, "n"]] = T.last()
                later = [u for u in order[order.index((kind, j)) + 1:] if u[0] == kind]
                if later:
                    load_queries(kind, later[0][1])

        def step_e(n):
            kind, j, h = units[n]
            L = P * (j + 1)
            b = n % 2
            S = core.bank[:, 2 * b:2 * b + 2, :].rearrange("p a n -> p (a n)")[:, 0:L]
            if kind == "idx":
                s = score[j % 3][:, 0:L]
                a = A(lambda e: e.activation(R[b][:, 0:L], S, ACT.Relu), after=[done["S"][n]] + done["N"].get(b, []))
                w = iw[:, j, h:h + 1]
                if h == 0:
                    v = V(lambda e: e.tensor_scalar(s, R[b][:, 0:L], w, None, ALU.mult), after=[a] + bias_read.get(j - 3, []), own=True)
                else:
                    v = V(lambda e: e.scalar_tensor_tensor(out=s, in0=R[b][:, 0:L], scalar=w, in1=s, op0=ALU.mult, op1=ALU.add),
                          after=[a], own=True)
                done["N"][b] = [v]
                if h == NAH - 1:
                    d = s[:, L - P:L]
                    scored[j] = [V(lambda e: e.tensor_tensor(d, d, far[:, 1, SEQ - P:SEQ], ALU.add), own=True)]
                    pending.extend((j, round_of(j), r == TOPK // 8 - 1) for r in range(TOPK // 8))
                done["E"][n] = [a]
                return
            if kind == "fox":
                mask, more = far[:, 0, SEQ - L:SEQ], []
            elif j < TOPK // P:
                mask, more = far[:, 1, SEQ - L:SEQ], []
            else:
                fill(until=j)
                mask, more = score[j % 3][:, 0:L], [biased[j]]
            m4 = n % 4
            v = V(lambda e: e.tensor_tensor_reduce(out=Sm[b][:, 0:L], in0=S, in1=mask, scale=1.0, scalar=-3.4e38, op0=ALU.add,
                                                   op1=ALU.max, accum_out=mx[m4][:]), after=[done["S"][n]] + more + done["X"].get(n - 2, []) )
            if kind == "dsa" and h == NAH - 1:
                bias_read[j] = [v]
            v2 = V(lambda e: e.tensor_scalar(nm[m4][:], mx[m4][:], -1.0, None, ALU.mult), own=True)
            a = A(lambda e: e.activation(Pb[b][:, 0:L], Sm[b][:, 0:L], ACT.Exp, bias=nm[m4][:, 0:1], accum_out=sm[m4][:]),
                  after=[v2] + done["X"].get(n - 2, []))
            done["E"][n] = [v]
            done["P", n] = a

        def step_x(n):
            kind, j, h = units[n]
            if kind == "idx":
                return
            b = n % 2
            T.wait(done["P", n])
            evs = []
            for q in range((j + 4) // 4):
                m = min(4, j + 1 - 4 * q)
                t = core.tr([(lambda c=c: core.bank[:, 4 + q, 128 * c:128 * c + 128],
                              lambda c=c: Pb[b][:, 128 * (4 * q + c):128 * (4 * q + c) + 128]) for c in range(m)], ident,
                            after=bank_free.get(q, []))
                Q = (A, V)[q]
                o_, i_ = PT[b][:, 4 * q:4 * q + m, :], core.bank[:, 4 + q, 0:128 * m].rearrange("p (c n) -> p c n", c=m)
                ev = Q((lambda e: e.activation(o_, i_, ACT.Copy)) if q == 0 else (lambda e: e.tensor_copy(o_, i_)), after=[t] + pt_free.get(b, []))
                bank_free[q] = [ev]
                evs.append(ev)
            done["X"][n] = [T.last()]
            done["T", n] = evs
            m4 = n % 4
            done["R", n] = V(lambda e: e.reciprocal(rc[m4][:], sm[m4][:]), after=[done["P", n]])

        bank_free, pt_free = {}, {}

        def step_o(n):
            kind, j, h = units[n]
            if kind == "idx":
                return
            b, m4, slot = n % 2, n % 4, n % 2
            out = core.bank[:, 6 + slot, 0:HD]
            vals = (lambda k: fv[:, k, HD * h:HD * h + HD]) if kind == "fox" else (lambda k: dv[:, k, :])
            core.mm(out, [(lambda k=k: PT[b][:, k, :], lambda k=k: vals(k)) for k in range(j + 1)],
                    after=done["T", n] + done["O"].get(slot, []))
            pt_free[b] = [T.last()]
            o = ob[kind][j % 2]
            a = A(lambda e: e.activation(o[:, HD * h:HD * h + HD], out, ACT.Copy, scale=rc[m4][:, 0:1]),
                  after=[T.last(), done["R", n]] + (stored.get((kind, j - 2), []) if h == 0 else []))
            done["O"][slot] = [a]
            if h == NAH - 1:
                stored[kind, j] = [core.store[(kind == "dsa") * 2 + j % 2](
                    lambda e: e.dma_start(dram["o" + kind][P * j:P * j + P, :], o[:]), after=[a])]

        N = len(units)
        for n in range(-2, N + 1):
            if n + 2 < N:
                step_s(n + 2)
            if 0 <= n + 1 < N:
                step_e(n + 1)
                fill(2)
            if 0 <= n < N:
                step_x(n)
            if 0 <= n - 1:
                step_o(n - 1)


NE, NG, EG, DE = 32, 4, 8, 512
SLOT_TILES = NE + 2 * SEQ // P


def merge(core, dram, tables):
    T, V, A, G = core.T, core.V, core.A, core.G
    ident = tables["mats"][:, C_ID, :]
    with Room(core) as sb:
        ld = core.load
        wp = [sb(f"m_wp{j}", [P, 4, D]) for j in range(2)]
        wo = sb("m_wo", [P, KD, D])
        wr = sb("m_wr", [P, KD, NG + NE])
        gate, gain, shift = (sb("m_" + k, [P, D]) for k in ("gate", "gain", "shift"))
        bg = sb("m_bg", [P, 2 * D])
        o = [sb(f"m_o{b}", [P, D]) for b in range(2)]
        gs = [sb(f"m_gs{b}", [P, 2 * D]) for b in range(2)]
        x = sb("m_x", [P, D])
        oT, mT = sb("m_oT", [P, KD, P]), sb("m_mT", [P, KD, P])
        m1, m2, x2, h = (sb("m_" + k, [P, D]) for k in ("m1", "m2", "x2", "h"))
        norm = Norm(core, sb, "m_n")
        ld[9](lambda e: e.dma_start(wp[0][:], dram["w_proj_fox_2"].rearrange("(k p) n -> p k n", p=P)))
        ld[9](lambda e: e.dma_start(wp[1][:], dram["w_proj_dsa_2"].rearrange("(k p) n -> p k n", p=P)))
        ld[9](lambda e: e.dma_start(wo[:], dram["w_out_2"].rearrange("(k p) n -> p k n", p=P)))
        ld[9](lambda e: e.dma_start(wr[:, :, 0:NG], dram["router_w_grp_2"].rearrange("(k p) n -> p k n", p=P)))
        ld[9](lambda e: e.dma_start(wr[:, :, NG:NG + NE], dram["router_w_exp_2"].rearrange("(k p) n -> p k n", p=P)))
        ld[9](lambda e: e.dma_start(bg[:], row(dram["b_gate_2"])))
        mod = dram["mod2"][0, :]
        wl = ld[9](lambda e: e.dma_start(gate[:], row(mod[2 * D:3 * D])))
        gain_rows(core, gain[:], dram["norm2_g_2"], mod[4 * D:5 * D], shift[:], mod[3 * D:4 * D], m1[:])
        T.wait(wl)
        V.wait(wl)

        def tile(b, i, marks):
            prev = prev_of(marks)
            before = lambda k: ([marks[k + "0"]] if k + "0" in marks else []) if b else prev(k + "1")
            at = bass.ds(i * 256 + 128 * b, 128)
            l1 = ld[1 + b](lambda e: e.dma_start(o[b][:, 0:512], dram["ofox"][at, :]), after=prev(f"to{b}"))
            l1 = ld[1 + b](lambda e: e.dma_start(o[b][:, 512:1024], dram["odsa"][at, :]))
            l2 = ld[3 + b](lambda e: e.dma_start(gs[b][:], dram["proj"][at, C_GF:C_GF + 2 * D]), after=prev(f"gs{b}"))
            l3 = ld[5](lambda e: e.dma_start(x[:], dram["x1"][at, :]), after=before("x"))
            V(lambda e: e.tensor_tensor(gs[b][:], gs[b][:], bg[:], ALU.add), after=[l2])
            sg = A(lambda e: e.activation(gs[b][:], gs[b][:], ACT.Sigmoid), after=[V.last()])
            t, ev = turn_rows(core, oT, o[b][:], KD, ident, (6, 7), [l1], [before("ev6"), before("ev7")])
            marks[f"to{b}"] = t
            T.wait(ev, *before("v2"))
            for j in range(2):
                for half in range(2):
                    core.mm(core.bank[:, 2 * j + half, :], [(lambda k=k: oT[:, 4 * j + k, :], lambda k=k: wp[j][:, k, 512 * half:512 * half + 512])
                                                            for k in range(4)])
            p = T.last()
            flat = lambda j: core.bank[:, 2 * j:2 * j + 2, :].rearrange("p a n -> p (a n)")
            V(lambda e: e.tensor_tensor(m1[:], flat(0), gs[b][:, 0:D], ALU.mult), after=[p, sg] + before("tm"))
            V(lambda e: e.tensor_tensor(m2[:], flat(1), gs[b][:, D:2 * D], ALU.mult))
            marks[f"gs{b}"] = V.last()
            v = V(lambda e: e.tensor_tensor(m1[:], m1[:], m2[:], ALU.add), own=True)
            t, ev = turn_rows(core, mT, m1[:], KD, ident, (6, 7), [v], [[A.last()], [A.last()]])
            marks[f"tm{b}"] = t
            T.wait(ev)
            for half in range(2):
                core.mm(core.bank[:, 4 + half, :], [(lambda k=k: mT[:, k, :], lambda k=k: wo[:, k, 512 * half:512 * half + 512]) for k in range(KD)],
                        after=before("v2"))
            V(lambda e: e.tensor_tensor(x2[:], flat(2), gate[:], ALU.mult), after=[T.last()] + before("stx") + before("nx"))
            marks[f"x{b}"] = V(lambda e: e.tensor_tensor(x2[:], x2[:], x[:], ALU.add), own=True, after=[l3])
            marks[f"v2{b}"] = V.last()
            marks[f"stx{b}"] = core.store[0](lambda e: e.dma_start(dram["x2"][at, :], x2[:]), after=[V.last()])
            V.wait(norm.rstd(x2[:], tables["eps"][:, 0:1], [V.last()]))
            v = norm.apply(h[:], x2[:], gain[:], shift[:], after=before("sth") + before("th"))
            marks[f"nx{b}"] = v
            marks[f"sth{b}"] = core.store[1](lambda e: e.dma_start(dram["h2"][at, :], h[:]), after=[v])
            t, ev = turn_rows(core, oT, h[:], KD, ident, (6, 7), [v], [[A.last()], [A.last()]])
            marks[f"th{b}"] = t
            core.mm(core.bank[:, 0, 0:NG + NE], [(lambda k=k: oT[:, k, :], lambda k=k: wr[:, k, :]) for k in range(KD)], after=[ev])
            marks[f"ev6{b}"] = marks[f"ev7{b}"] = T.last()
            V(lambda e: e.tensor_copy(tables["logits"][:, bass.ds(i * 2 + b, 1), :].rearrange("p a n -> p (a n)"), core.bank[:, 0, 0:NG + NE]),
              after=[T.last()])
            marks[f"v2{b}"] = V.last()

        def body(i, marks):
            for b in range(2):
                tile(b, i, marks)
        core.loop(NT // 2, body)


def route(core, dram, tables):
    T, V, A, G = core.T, core.V, core.A, core.G
    with Room(core) as sb:
        ld = core.load
        v = lambda f: V(f, own=True)
        new = lambda name, *shape: sb("r_" + name, [P, *shape])
        bgr, bex = new("bgr", NG), new("bex", NE)
        cst = new("cst", NG + NE + 8 + SLOT_TILES)
        ld[0](lambda e: e.dma_start(bgr[:], row(dram["router_b_grp_2"])))
        ld[0](lambda e: e.dma_start(bex[:], row(dram["router_b_exp_2"])))
        got = ld[0](lambda e: e.dma_start(cst[:], row(dram["counts"])))
        down4, down32 = cst[:, 0:NG], cst[:, NG:NG + NE]
        steps, tile_no = cst[:, NG + NE:NG + NE + 8], cst[:, NG + NE + 8:]
        V.wait(got)
        gl, eq, oh = new("gl", NT, NG), new("eq", NT, NG), new("oh", NT, NG)
        gm, gs, gw, t1, t2 = (new(k, NT) for k in ("gm", "gs", "gw", "t1", "t2"))
        el, q32, w32 = new("el", NT, NE), new("q32", NT, NE), new("w32", NT, NE)
        E = [new(f"E{j}", NT, NE) for j in range(2)]
        m = [new(f"m{j}", NT) for j in range(2)]
        lg = tables["logits"]
        W = tables["weight"]
        v(lambda e: e.tensor_tensor(gl[:], lg[:, :, 0:NG], over(bgr[:], 1, NT), ALU.add))
        v(lambda e: e.tensor_reduce(gm[:], gl[:], AX.X, ALU.max))
        v(lambda e: e.tensor_tensor(eq[:], gl[:], over(gm[:], 2, NG), ALU.is_equal))
        v(lambda e: e.tensor_tensor(eq[:], eq[:], over(down4, 1, NT), ALU.mult))
        v(lambda e: e.tensor_reduce(t1[:], eq[:], AX.X, ALU.max))
        v(lambda e: e.tensor_tensor(oh[:], eq[:], over(t1[:], 2, NG), ALU.is_equal))
        v(lambda e: e.tensor_tensor(gl[:], gl[:], over(gm[:], 2, NG), ALU.subtract))
        a = A(lambda e: e.activation(gl[:], gl[:], ACT.Exp), after=[V.last()])
        V.wait(a)
        v(lambda e: e.tensor_reduce(gs[:], gl[:], AX.X, ALU.add))
        v(lambda e: e.reciprocal(gw[:], gs[:]))
        v(lambda e: e.tensor_scalar(oh[:], oh[:], -1.0, -FAR, ALU.add, ALU.mult))
        v(lambda e: e.tensor_tensor(el[:], lg[:, :, NG:NG + NE], over(bex[:], 1, NT), ALU.add))
        el4 = el[:].rearrange("p t (g k) -> p (t g) k", k=EG)
        v(lambda e: e.tensor_tensor(el4, el4, over(oh[:].rearrange("p t g -> p (t g)"), 2, EG), ALU.add))
        for j in range(2):
            v(lambda e: e.tensor_reduce(m[j][:], el[:], AX.X, ALU.max))
            v(lambda e: e.tensor_tensor(q32[:], el[:], over(m[j][:], 2, NE), ALU.is_equal))
            v(lambda e: e.tensor_tensor(q32[:], q32[:], over(down32, 1, NT), ALU.mult))
            v(lambda e: e.tensor_reduce(t1[:], q32[:], AX.X, ALU.max))
            v(lambda e: e.tensor_tensor(E[j][:], q32[:], over(t1[:], 2, NE), ALU.is_equal))
            if j == 0:
                v(lambda e: e.scalar_tensor_tensor(out=el[:], in0=E[0][:], scalar=2 * FAR, in1=el[:], op0=ALU.mult, op1=ALU.add))
        v(lambda e: e.tensor_tensor(t2[:], m[1][:], m[0][:], ALU.subtract))
        a = A(lambda e: e.activation(t2[:], t2[:], ACT.Exp), after=[V.last()])
        V.wait(a)
        v(lambda e: e.tensor_scalar(t1[:], t2[:], 1.0, None, ALU.add))
        v(lambda e: e.reciprocal(t1[:], t1[:]))
        v(lambda e: e.tensor_tensor(W[:, 0, :], t1[:], gw[:], ALU.mult))
        v(lambda e: e.tensor_tensor(W[:, 1, :], W[:, 0, :], t2[:], ALU.mult))
        v(lambda e: e.tensor_tensor(w32[:], E[0][:], E[1][:], ALU.add))
        for j, c in ((0, C_LT), (1, C_ONE)):
            T(lambda e: e.matmul(core.bank[:, j, 0:NT * NE], tables["mats"][:, c, :], w32[:].rearrange("p t n -> p (t n)"), start=True, stop=True),
              after=[V.last()])
        rank, run, total = new("rank", NT, NE), new("run", NE), new("total", NT, NE)
        V.wait(T.last())
        v(lambda e: e.memset(run[:], 0.0))
        v(lambda e: e.tensor_copy(total[:].rearrange("p t n -> p (t n)"), core.bank[:, 1, 0:NT * NE]))
        for t in range(NT):
            v(lambda e: e.tensor_tensor(rank[:, t, :], core.bank[:, 0, NE * t:NE * t + NE], run[:], ALU.add))
            v(lambda e: e.tensor_tensor(run[:], run[:], total[:, t, :], ALU.add))
        cmp, inc = new("cmp", NE, 8), [new(f"inc{j}", NE) for j in range(2)]
        tiles = new("tiles", NE)
        v(lambda e: e.tensor_tensor(cmp[:], over(run[:], 2, 8), over(steps, 1, NE), ALU.is_gt))
        v(lambda e: e.tensor_reduce(tiles[:], cmp[:], AX.X, ALU.add))
        v(lambda e: e.tensor_copy(inc[0][:], tiles[:]))
        src = 0
        for d in (1, 2, 4, 8, 16):
            v(lambda e: e.tensor_copy(inc[1 - src][:, 0:d], inc[src][:, 0:d]))
            v(lambda e: e.tensor_tensor(inc[1 - src][:, d:NE], inc[src][:, d:NE], inc[src][:, 0:NE - d], ALU.add))
            src = 1 - src
        ends = inc[src]
        base = new("base", NE)
        v(lambda e: e.tensor_tensor(base[:], ends[:], tiles[:], ALU.subtract))
        v(lambda e: e.tensor_scalar(base[:], base[:], float(P), None, ALU.mult))
        v(lambda e: e.tensor_tensor(rank[:], rank[:], over(base[:], 1, NT), ALU.add))
        for j in range(2):
            v(lambda e: e.tensor_tensor(q32[:], E[j][:], rank[:], ALU.mult))
            v(lambda e: e.tensor_reduce(t1[:], q32[:], AX.X, ALU.add))
            v(lambda e: e.tensor_copy(tables["slot"][:, j, :], t1[:]))
        ge, te = new("ge", SLOT_TILES, NE), new("te", SLOT_TILES)
        v(lambda e: e.tensor_tensor(ge[:], over(tile_no, 2, NE), over(ends[:], 1, SLOT_TILES), ALU.is_ge))
        v(lambda e: e.tensor_reduce(te[:], ge[:], AX.X, ALU.add))
        v(lambda e: e.tensor_scalar(te[:], te[:], float(NE - 1), None, ALU.min))
        v(lambda e: e.tensor_copy(tables["expert"][:], te[:]))
        v(lambda e: e.tensor_tensor(te[:, 0:SLOT_TILES // 2], cst[:, NG + NE + 8:NG + NE + 8 + SLOT_TILES:2],
                                    ends[:, NE - 1:NE].to_broadcast([P, SLOT_TILES // 2]), ALU.is_lt))
        v(lambda e: e.tensor_reduce(gs[:, 0:1], te[:, 0:SLOT_TILES // 2], AX.X, ALU.add))
        v(lambda e: e.tensor_copy(tables["live"][:], gs[:, 0:1]))
        zero, tok = sb("r_zero", [P, SLOT_TILES], I32), sb("r_tok", [P, NT], I32)
        G(lambda e: e.memset(zero[:], 0))
        G(lambda e: e.iota(tok[:], [[P, NT]], base=0, channel_multiplier=1))
        z = core.store[0](lambda e: e.dma_start(dram["slot_token"].rearrange("(p m) a -> p (m a)", p=P), zero[:]), after=[G.last()])
        G.wait(z, V.last(), G.last())
        for t in range(NT):
            for j in range(2):
                core.scatter(lambda e: e.indirect_dma_start(out=dram["slot_token"], out_offset=bass.IndirectOffsetOnAxis(
                    ap=tables["slot"][:, j, t:t + 1].bitcast(U32), axis=0), in_=tok[:, t:t + 1], in_offset=None))


def experts(core, dram, tables):
    T, V, A, G = core.T, core.V, core.A, core.G
    ident = tables["mats"][:, C_ID, :]
    with Room(core) as sb:
        ld = core.load
        w1, w3 = ([sb(f"e_{k}{b}", [P, KD, DE]) for b in range(2)] for k in ("w1", "w3"))
        w2 = [sb(f"e_w2{b}", [P, DE // P, D]) for b in range(2)]
        ids = sb("e_ids", [P, SLOT_TILES], I32)
        idb = [sb(f"e_idb{b}", [P, 1], I32) for b in range(2)]
        x = [sb(f"e_x{b}", [P, D]) for b in range(2)]
        xT = [sb(f"e_xT{b}", [P, KD, P]) for b in range(2)]
        g = [sb(f"e_g{b}", [P, DE]) for b in range(2)]
        gT = [sb(f"e_gT{b}", [P, DE // P, P]) for b in range(2)]
        y = [sb(f"e_y{b}", [P, D]) for b in range(2)]
        with core.nc.allow_non_contiguous_dma(reason="a slot's token on the slot's partition"):
            got = ld[0](lambda e: e.dma_start(ids[:], dram["slot_token"].rearrange("(m p) a -> p (m a)", p=P)))
        idle, nought = sb("e_idle", [P, 1]), sb("e_nought", [P, D])
        A.wait(V(lambda e: e.memset(nought[:], 0.0)))
        gathers = [Queue(core.nc, core.nc.gpsimd, f"expert_rows{b}_done", 16, 0) for b in range(2)]
        G(lambda e: e.memset(idle[:], 0.0))
        G.wait(got)

        def fetch(b, i, marks):
            prev = prev_of(marks)
            m = i * 2 + b
            if ld[1].counting:
                ex = 0
            else:
                ex = core.nc.sync.value_load(tables["expert"][0:1, bass.ds(m, 1)], min_val=0, max_val=NE - 1)
            out = []
            for j, (buf, name, kk) in enumerate(((w1, "exp_w1_2", KD), (w3, "exp_w3_2", KD), (w2, "exp_w2_2", DE // P))):
                n = 1 + 3 * b + j
                out.append(ld[n](lambda e: e.dma_start(buf[b][:], dram[name][bass.ds(ex, 1), :, :].rearrange("a (k p) n -> p (a k) n", p=P)),
                                 after=prev(f"w{j}{b}")))
            G(lambda e: e.tensor_copy(idb[b][:], ids[:, bass.ds(m, 1)]), after=prev(f"tx{b}"))
            G.wait(G.last())
            G(lambda e: e.tensor_tensor(idle[:], idle[:], idle[:], ALU.add))
            gather = gathers[b](lambda e: e.indirect_dma_start(out=x[b][:], out_offset=None, in_=dram["h2"],
                                                                   in_offset=bass.IndirectOffsetOnAxis(ap=idb[b][:, 0:1].bitcast(U32), axis=0)),
                                    )
            return out, gather

        def turn_x(b, gather, marks):
            before = prev_of(marks)
            T.wait(gather, *before(f"down{b}"))
            for q in range(2):
                t = core.tr([(lambda c=c: core.bank[:, 4 + q, 128 * c:128 * c + 128], lambda c=c: x[b][:, 512 * q + 128 * c:512 * q + 128 * c + 128])
                             for c in range(4)], ident, after=[last[f"x{q}"]] if f"x{q}" in last else prev_of(marks)(f"lx{q}"))
                o_, i_ = xT[b][:, 4 * q:4 * q + 4, :], core.bank[:, 4 + q, :].rearrange("p (c n) -> p c n", c=4)
                Q = (A, V)[q]
                last[f"x{q}"] = Q((lambda e: e.activation(o_, i_, ACT.Copy)) if q == 0 else (lambda e: e.tensor_copy(o_, i_)),
                                  after=[t] + before(f"up{b}"))
                marks[f"lx{q}"] = last[f"x{q}"]
            marks[f"tx{b}"] = T.last()
            return [last["x0"], last["x1"]]

        def up(b, w, ready, marks):
            T.wait(*ready)
            for j, buf in ((0, w1), (1, w3)):
                core.mm(core.bank[:, j, :], [(lambda k=k: xT[b][:, k, :], lambda k=k: buf[b][:, k, :]) for k in range(KD)],
                        after=[w[j]] + ([last["mul"]] if "mul" in last else prev_of(marks)("lmul")))
                marks[f"w{j}{b}"] = T.last()
            marks[f"up{b}"] = T.last()
            a = A(lambda e: e.activation(g[b][:], core.bank[:, 0, :], ACT.Silu), after=[T.last()] + prev_of(marks)(f"tg{b}"))
            last["mul"] = V(lambda e: e.tensor_tensor(g[b][:], g[b][:], core.bank[:, 1, :], ALU.mult), after=[a])
            marks["lmul"] = last["mul"]

        def turn_g(b, mul, marks):
            t = core.tr([(lambda c=c: core.bank[:, 6 + b, 128 * c:128 * c + 128], lambda c=c: g[b][:, 128 * c:128 * c + 128]) for c in range(4)],
                        ident, after=[mul] + prev_of(marks)(f"g{b}"))
            marks[f"tg{b}"] = t
            marks[f"g{b}"] = last[f"g{b}"] = A(lambda e: e.activation(gT[b][:].rearrange("p c n -> p (c n)"), core.bank[:, 6 + b, :], ACT.Copy),
                                               after=[t] + prev_of(marks)(f"down{b}"))

        def down(b, i, w, marks):
            T.wait(last[f"g{b}"], w[2])
            for half in range(2):
                Q = (A, V)[half]
                core.mm(core.bank[:, 2 + half, :], [(lambda k=k: gT[b][:, k, :], lambda k=k: w2[b][:, k, 512 * half:512 * half + 512])
                                                    for k in range(DE // P)],
                        after=[last[f"y{half}"]] if f"y{half}" in last else prev_of(marks)(f"ly{half}"))
                o_, i_ = y[b][:, 512 * half:512 * half + 512], core.bank[:, 2 + half, :]
                last[f"y{half}"] = marks[f"ly{half}"] = Q(
                    (lambda e: e.activation(o_, i_, ACT.Copy)) if half == 0 else (lambda e: e.tensor_copy(o_, i_)),
                    after=[T.last()] + prev_of(marks)(f"st{b}"))
            marks[f"down{b}"] = marks[f"w2{b}"] = T.last()
            marks[f"st{b}"] = core.store[b](lambda e: e.dma_start(dram["y"][bass.ds(i * 256 + 128 * b, 128), :], y[b][:]),
                                            after=[last["y0"], last["y1"]])

        last = {}

        def body(i, marks):
            last.clear()
            w, x_ = zip(*(fetch(b, i, marks) for b in range(2)))
            r0 = turn_x(0, x_[0], marks)
            up(0, w[0], r0, marks)
            mul0 = last["mul"]
            r1 = turn_x(1, x_[1], marks)
            turn_g(0, mul0, marks)
            up(1, w[1], r1, marks)
            down(0, i, w[0], marks)
            turn_g(1, last["mul"], marks)
            down(1, i, w[1], marks)

        def rest(i):
            for b in range(2):
                core.store[b](lambda e: e.dma_start(dram["y"][bass.ds(i * 256 + 128 * b, 128), :], nought[:]))

        live = core.nc.values_load(tables["live"][0:1, 0:1], min_val=0, max_val=SLOT_TILES // 2)
        core.loop(SLOT_TILES // 2, body, gathers, live, rest)


def combine(core, dram, tables):
    V, G = core.V, core.G
    with Room(core) as sb:
        gate = sb("o_gate", [P, D])
        y = [[sb(f"o_y{j}{b}", [P, D]) for b in range(2)] for j in range(2)]
        x2 = [sb(f"o_x{b}", [P, D]) for b in range(2)]
        V.wait(core.load[0](lambda e: e.dma_start(gate[:], row(dram["mod2"][0, 5 * D:6 * D]))))
        read, stored = {}, {}
        for t in range(NT):
            b = t % 2
            lx = core.load[1 + b](lambda e: e.dma_start(x2[b][:], dram["x2"][P * t:P * t + P, :]), after=stored.get(t - 2, []))
            got = [core.gather[2 * b + j](lambda e: e.indirect_dma_start(
                out=y[j][b][:], out_offset=None, in_=dram["y"],
                in_offset=bass.IndirectOffsetOnAxis(ap=tables["slot"][:, j, t:t + 1].bitcast(U32), axis=0)), after=read.get(t - 2, [])) for j in range(2)]
            V(lambda e: e.tensor_scalar(y[0][b][:], y[0][b][:], tables["weight"][:, 0, t:t + 1], None, ALU.mult), after=got[:1])
            V(lambda e: e.scalar_tensor_tensor(out=y[0][b][:], in0=y[1][b][:], scalar=tables["weight"][:, 1, t:t + 1], in1=y[0][b][:],
                                               op0=ALU.mult, op1=ALU.add), after=got[1:], own=True)
            V(lambda e: e.tensor_tensor(y[0][b][:], y[0][b][:], gate[:], ALU.mult), own=True)
            read[t] = [V(lambda e: e.tensor_tensor(x2[b][:], x2[b][:], y[0][b][:], ALU.add), own=True, after=[lx])]
            stored[t] = [core.store[b](lambda e: e.dma_start(dram["result"][P * t:P * t + P, :], x2[b][:]), after=[V.last()])]


SCRATCH = {"mods": (2, 3 * D), "mod2": (1, 6 * D), "uT": (DF, SEQ), "z": (SEQ, 2 * D), "xbcT": (CONV, SEQ + CTX), "mix": (SEQ, 2 * D), "xtok": (SEQ + CTX, P + CONV),
           "x1": (SEQ, D), "h1": (SEQ, D), "proj": (SEQ, COLS2), "fqT": (NAH, HD, SEQ), "fkT": (NAH, HD + 1, SEQ), "dqT": (NAH, HD, SEQ),
           "iqT": (NAH, HD, SEQ), "dkT": (HD, SEQ), "ikT": (HD, SEQ), "ofox": (SEQ, 512), "odsa": (SEQ, 512), "x2": (SEQ, D), "h2": (SEQ, D),
           "y": (SLOT_TILES * P, D)}
STAGES = (modulation, project_first, fourier, state_space, close_first, project_second, prepare_heads, attend, merge, route, experts, combine)


def program(nc, dram):
    for name, shape in SCRATCH.items():
        dram[name] = nc.dram_tensor(name, shape, F32).ap()
    dram["slot_token"] = nc.dram_tensor("slot_token", (SLOT_TILES * P, 1), I32).ap()
    with ExitStack() as ctx:
        core = Core(nc, ctx)
        with Room(core) as sb:
            tables = load_tables(core, sb, dram)
            for stage in STAGES:
                stage(core, dram, tables)


def kernel(**inputs):
    import concourse.bacc as bacc
    from concourse.bass_utils import run_bass_kernel_spmd

    nc = bacc.Bacc("TRN2", target_bir_lowering=False, num_devices=1)
    arrays, dram = {}, {}
    for name, a in {**inputs, **constants()}.items():
        a = np.asarray(a)
        if name in inputs and a.ndim > 1:
            a = a[0]
        arrays["in_" + name] = np.ascontiguousarray(a)
        dram[name] = nc.dram_tensor("in_" + name, a.shape, mybir.dt.from_np(a.dtype), kind="ExternalInput").ap()
    dram["result"] = nc.dram_tensor("result", (SEQ, D), F32, kind="ExternalOutput").ap()
    program(nc, dram)
    out = run_bass_kernel_spmd(nc, [arrays], core_ids=[0]).results[0]["result"]
    return out.reshape(1, SEQ, D)
```

```python
import numpy as np
import concourse.bass as bass
from concourse import mybir
from contextlib import ExitStack

F32, R32, I32 = mybir.dt.float32, mybir.dt.float32r, mybir.dt.int32
U32 = mybir.dt.uint32
ALU, ACT, AX = mybir.AluOpType, mybir.ActivationFunctionType, mybir.AxisListType
START = 4096


class Ticket:
    def __init__(self, queue, base, step, loop):
        self.queue, self.base, self.step, self.loop = queue, base, step, loop

    def last_round(self, back=1):
        return Ticket(self.queue, self.base - back * self.step, self.step, self.loop)

    def value(self):
        return self.base if self.loop is None else self.loop * self.step + self.base


class Queue:
    def __init__(self, nc, eng, name, unit=1, start=START):
        self.eng, self.unit, self.sem = eng, unit, nc.alloc_semaphore(name)
        self.n, self.step, self.loop, self.counting = start, 0, None, False
        self.bump = start > 0
        if start:
            eng.sem_inc(self.sem, start)

    def __call__(self, f, after=(), own=False, inc=True):
        self.wait(*after, *([self.last()] if own else []))
        if not self.counting:
            ins = f(self.eng)
            if inc:
                ins.then_inc(self.sem, self.unit)
        if inc:
            self.n += self.unit
        return self.last()

    def last(self):
        return Ticket(self, self.n, self.step, self.loop)

    def wait(self, *tickets):
        if self.counting:
            return
        latest = {}
        for t in tickets:
            k = (t.queue, t.step, t.loop is None)
            if k not in latest or latest[k].base < t.base:
                latest[k] = t
        for t in latest.values():
            self.eng.wait_ge(t.queue.sem, t.value())


def run_loop(nc, queues, trips, body, live=None, rest=None):
    before, marks = {q: q.n for q in queues}, {}
    for q in queues:
        q.counting = True
    body(0, marks)
    steps = {q: q.n - before[q] for q in queues}
    for t in marks.values():
        t.step = steps[t.queue]
    for q in queues:
        q.n, q.counting, q.step = before[q], False, steps[q]
    with nc.Fori(0, trips) as i:
        for q in queues:
            q.loop = i
        for t in marks.values():
            t.loop = i
        if live is None:
            body(i, dict(marks))
        else:
            with nc.If(i < live):
                body(i, dict(marks))
            with nc.Else():
                at = {q: q.n for q in queues}
                for q in queues:
                    q.n = before[q]
                rest(i)
                for q in queues:
                    q.n, moved = at[q], q.n > before[q]
                    if steps[q] and q.bump and not moved:
                        q.wait(Ticket(q, before[q], steps[q], i))
                        q.eng.sem_inc(q.sem, steps[q])
    for q in queues:
        q.n, q.step, q.loop = before[q] + trips * steps[q], 0, None
    return {k: Ticket(t.queue, t.base + (trips - 1) * t.step, 0, None) for k, t in marks.items()}
D, SEQ, CTX, P, KD = 1024, 1024, 256, 128, 8
NT, NC = SEQ // P, CTX // P
DF, DS, NBC, NST = 512, 1536, 4, 128
NH, HP, HG = 24, 64, 6
CONV, GRID_H, GRID_W = 2560, 16, 64
COL_Z, COL_XBC, COL_DT = 512, 2560, 5120
EPS, FAR = 1e-6, -1e30
C_ID, C_LE, C_GE, C_GT, C_LT, C_ONE = range(6)


class Core:
    def __init__(self, nc, ctx):
        self.nc, self.ctx = nc, ctx
        self.T, self.V, self.A, self.G = (Queue(nc, e, n) for e, n in (
            (nc.tensor, "pe_done"), (nc.vector, "dve_done"), (nc.scalar, "act_done"), (nc.gpsimd, "pool_done")))
        self.load = [Queue(nc, nc.sync, f"load{j}_done", 16) for j in range(12)]
        self.store = [Queue(nc, nc.scalar, f"store{j}_done", 16) for j in range(8)]
        self.scatter = Queue(nc, nc.gpsimd, "scatter_done", 16, 0)
        self.queues = [self.T, self.V, self.A, self.G] + self.load + self.store + [self.scatter]
        self.engines = [nc.tensor, nc.vector, nc.scalar, nc.gpsimd, nc.sync]
        self.bank = ctx.enter_context(nc.psum_tensor("banks", [P, 8, 512], F32))
        self.zero = ctx.enter_context(nc.sbuf_tensor("zero", [P, 1], F32))
        self.G.wait(self.V(lambda e: e.memset(self.zero[:], 0.0)))
        self.V.wait(self.V.last())

    def settle(self):
        for e in self.engines:
            for q in self.queues:
                if q.n:
                    e.wait_ge(q.sem, q.n)

    def loop(self, trips, body, more=(), live=None, rest=None):
        return run_loop(self.nc, self.queues + list(more), trips, body, live, rest)

    def mm(self, out, pairs, after=(), inc=True, start=True, stop=True):
        self.T.wait(*after)
        for n, (a, b) in enumerate(pairs):
            last = n == len(pairs) - 1
            self.T(lambda e: e.matmul(out, a(), b(), start=start and n == 0, stop=stop and last), inc=inc and last)
        return self.T.last()

    def tr(self, outs, ident, after=()):
        self.T.wait(*after)
        for n, (o, a) in enumerate(outs):
            self.T(lambda e: e.transpose(o(), a(), ident), inc=n == len(outs) - 1)
        return self.T.last()


def three(ah, al, bh, bl):
    return [(ah, bh), (ah, bl), (al, bh)]


def split(core, engine, hi, lo, src, after=(), free=()):
    if engine is None:
        h = core.A(lambda e: e.activation(hi, src, ACT.Copy), after=[*after, *free])
        return core.V(lambda e: e.tensor_tensor(lo, src, hi.bitcast(F32), ALU.subtract), after=[h, *free])
    zero = core.zero[:].unsqueeze(2).to_broadcast(list(src.shape))
    engine(lambda e: e.tensor_tensor(hi, src, zero, ALU.add), after=[*after, *free])
    return engine(lambda e: e.tensor_tensor(lo, src, hi.bitcast(F32), ALU.subtract), own=True)


class Room:
    def __init__(self, core):
        self.core, self.stack = core, ExitStack()

    def __call__(self, name, shape, dt=F32):
        return self.stack.enter_context(self.core.nc.sbuf_tensor(name, shape, dt))

    def __enter__(self):
        self.stack.__enter__()
        return self

    def __exit__(self, *a):
        self.core.settle()
        return self.stack.__exit__(*a)


def row(ap):
    return ap.partition_broadcast(P)


def over(ap, axis, n):
    a = ap.unsqueeze(axis)
    shape = list(a.shape)
    shape[axis] = n
    return a.to_broadcast(shape)


def modulation(core, dram, tables):
    with Room(core) as sb:
        T, V, A = core.T, core.V, core.A
        c = sb("mod_c", [P, 3, KD])
        cs = sb("mod_silu", [P, KD, 3])
        w = [sb(f"mod_w{b}", [P, KD, 512]) for b in range(2)]
        bias = [sb(f"mod_b{b}", [2, 512]) for b in range(2)]
        out = [sb(f"mod_o{b}", [2, 512]) for b in range(2)]
        got = None
        for j, name in enumerate(("c", "c_ctx", "c_2")):
            got = core.load[10](lambda e: e.dma_start(c[:, j, :], dram[name].rearrange("(p k) -> p k", k=KD)))
        silu = A(lambda e: e.activation(cs[:].rearrange("p k j -> p j k"), c[:], ACT.Silu), after=[got])
        T.wait(silu)
        for w_name, b_name, o_name, j0, m, n in (("w_ada", "b_ada", "mods", 0, 2, 6), ("ada_w_2", "ada_b_2", "mod2", 2, 1, 12)):
            wv = dram[w_name].rearrange("(p k) n -> p k n", k=KD)

            def body(i, marks):
                for b in range(2):
                    at = bass.ds(i * 1024 + 512 * b, 512)
                    prev = lambda x: [marks[x].last_round()] if x in marks else []
                    lw = core.load[b](lambda e: e.dma_start(w[b][:], wv[:, :, at]), after=prev(f"mm{b}"))
                    lb = core.load[2 + b](lambda e: e.dma_start(bias[b][0:m, :], dram[b_name][at].partition_broadcast(m)),
                                          after=prev(f"add{b}"))
                    t = core.mm(core.bank[0:m, b, :], [(lambda k=k: cs[:, k, j0:j0 + m], lambda k=k: w[b][:, k, :])
                                                       for k in range(KD)], after=[lw] + prev(f"add{b}"))
                    v = V(lambda e: e.tensor_tensor(out[b][0:m, :], core.bank[0:m, b, :], bias[b][0:m, :], ALU.add),
                          after=[t, lb] + prev(f"st{b}"))
                    marks[f"mm{b}"], marks[f"add{b}"] = t, v
                    marks[f"st{b}"] = core.store[b](lambda e: e.dma_start(dram[o_name][0:m, at], out[b][0:m, :]), after=[v])
            core.loop(n // 2, body)


class Norm:
    def __init__(self, core, sb, name):
        self.core = core
        self.sq = sb(name + "_sq", [P, D])
        self.ss = sb(name + "_ss", [P, 1])
        self.sd = sb(name + "_sd", [P, 1])
        self.rs = sb(name + "_rs", [P, 1])

    def squares(self, x, after):
        self.summed = self.core.V(lambda e: e.tensor_tensor_reduce(out=self.sq[:], in0=x, in1=x, scale=1.0 / D, scalar=0.0, op0=ALU.mult,
                                                                   op1=ALU.add, accum_out=self.ss[:]), after=after, own=True)

    def root(self, eps):
        self.rooted = self.core.A(lambda e: e.activation(self.sd[:], self.ss[:], ACT.Sqrt, bias=eps), after=[self.summed])

    def inverse(self):
        return self.core.V(lambda e: e.reciprocal(self.rs[:], self.sd[:]), after=[self.rooted])

    def rstd(self, x, eps, after):
        self.squares(x, after)
        self.root(eps)
        return self.inverse()

    def apply(self, out, x, gain, shift=None, after=()):
        v = self.core.V(lambda e: e.scalar_tensor_tensor(out=out, in0=x, scalar=self.rs[:, 0:1], in1=gain,
                                                         op0=ALU.mult, op1=ALU.mult), after=after, own=True)
        if shift is not None:
            v = self.core.V(lambda e: e.tensor_tensor(out, out, shift, ALU.add), own=True)
        return v


def gain_rows(core, gain, w_row, scale_row, shift, shift_row, tmp):
    core.load[0](lambda e: e.dma_start(gain, row(w_row)))
    core.load[0](lambda e: e.dma_start(tmp, row(scale_row)))
    got = core.load[0](lambda e: e.dma_start(shift, row(shift_row)))
    core.V(lambda e: e.scalar_tensor_tensor(out=gain, in0=tmp, scalar=1.0, in1=gain, op0=ALU.add, op1=ALU.mult), after=[got])
    return core.V.last()


def project_first(core, dram, tables):
    T, V, A, G = core.T, core.V, core.A, core.G
    ident = tables["mats"][:, C_ID, :]
    with Room(core) as sb:
        TOK = SEQ + CTX
        hh, hl = (sb(k, [P, KD, TOK], R32) for k in ("h_high", "h_low"))
        with Room(core) as sb1:
            norms = [Norm(core, sb1, f"n1{b}") for b in range(2)]
            gain, shift, tmp = (sb1(f"n1_{n}", [P, D]) for n in ("gain", "shift", "tmp"))
            x = [sb1(f"n1_x{b}", [P, D]) for b in range(2)]
            h = [sb1(f"n1_h{b}", [P, D]) for b in range(2)]
            for src, mod, n, at0 in ((dram["x"], 0, NT, 0), (dram["ctx"], 1, NC, SEQ)):
                mrow = dram["mods"][mod, :]
                rows_in = gain_rows(core, gain[:], dram["norm_w"], mrow[D:2 * D], shift[:], mrow[0:D], tmp[:])

                def body(i, marks):
                    prev = lambda k: [marks[k].last_round()] if k in marks else []
                    ld = [core.load[1 + b](lambda e: e.dma_start(x[b][:], src[bass.ds(i * 256 + 128 * b, 128), :]), after=prev(f"h{b}"))
                          for b in range(2)]
                    for b in range(2):
                        norms[b].squares(x[b][:], [ld[b]])
                    for b in range(2):
                        norms[b].root(tables["eps"][:, 0:1])
                    shifted = []
                    for b in range(2):
                        norms[b].inverse()
                        v = norms[b].apply(h[b][:], x[b][:], gain[:], None, after=prev(f"t{b}") + [rows_in])
                        marks[f"h{b}"] = v
                        shifted.append((V, G)[b](lambda e: e.tensor_tensor(h[b][:], h[b][:], shift[:], ALU.add), after=[v]))
                    for b in range(2):
                        v = shifted[b]
                        t = core.tr([(lambda k=k: core.bank[:, 2 * b + k // 4, 128 * (k % 4):128 * (k % 4) + 128],
                                      lambda k=k: h[b][:, 128 * k:128 * k + 128]) for k in range(KD)], ident,
                                    after=[v] + prev(f"ev{b}"))
                        marks[f"t{b}"] = t
                        for half in range(2):
                            part = lambda to: to[:, 4 * half:4 * half + 4, bass.ds(i * 256 + 128 * b + at0, 128)]
                            marks[f"ev{b}"] = split(core, None, part(hh), part(hl), core.bank[:, 2 * b + half, :].rearrange("p (k n) -> p k n", k=4), [t])
                core.loop(n // 2, body)
                core.V.wait(T.last(), A.last())
                core.nc.sync.wait_ge(V.sem, V.n)

        NCT = CONV // P
        taps = sb("taps", [P, NCT, 10])
        with Room(core) as sb1:
            flat = sb1("taps_flat", [10, CONV])
            core.load[0](lambda e: e.dma_start(flat[0:9, :], dram["conv_w"].rearrange("a b c -> (a b) c")))
            got = core.load[0](lambda e: e.dma_start(flat[9:10, :], dram["conv_b"].rearrange("(a c) -> a c", a=1)))
            t = core.tr([(lambda k=k: core.bank[:, 0, 10 * k:10 * k + 10], lambda k=k: flat[:, 128 * k:128 * k + 128])
                         for k in range(NCT)], tables["mats"][0:10, C_ID, 0:10], after=[got])
            V(lambda e: e.tensor_copy(taps[:].rearrange("p t j -> p (t j)"), core.bank[:, 0, 0:10 * NCT]), after=[t])

        z_raw = sb("zw_raw", [P, KD, 512])
        win = dram["w_in"].rearrange("(k p) n -> p k n", p=P)
        z_first = core.load[3](lambda e: e.dma_start(z_raw[:], win[:, :, COL_Z:COL_Z + 512]))
        with Room(core) as sb1:
            raw = [sb1(f"w1_raw{b}", [P, KD, 256]) for b in range(2)]
            w = [[sb1(f"w1_{k}{b}", [P, KD, 256], R32) for k in ("high", "low")] for b in range(2)]
            img = [sb1(f"img{b}", [P, GRID_H + 2, GRID_W + 2]) for b in range(2)]
            line = [sb1(f"line{b}", [P, CTX + 2]) for b in range(2)]
            acc = [sb1(f"acc{b}", [P, TOK]) for b in range(2)]
            tap = [sb1(f"tap{b}", [P, 10]) for b in range(2)]
            res = [sb1(f"res{b}", [P, TOK]) for b in range(2)]
            for b in range(2):
                G(lambda e: e.memset(img[b][:], 0.0))
                G(lambda e: e.memset(line[b][:], 0.0))
            zeroed = G.last()

            def products(s, b, wap, lw, wait, ctx_too, between=lambda: None):
                T.wait(lw, *wait)
                for half, n0, n in ((0, 0, 512), (1, 512, 512)) + (((2, 1024, 256),) if ctx_too else ()):
                    core.mm(core.bank[:, 3 * b + half, 0:n], [p for k in range(KD) for p in three(
                        *(lambda k=k, a=a: a[:, k, 128 * s:128 * s + 128] for a in wap), *(lambda k=k, a=a: a[:, k, n0:n0 + n] for a in (hh, hl)))])
                    if half == 0:
                        between()
                return T.last()

            for slab in range(2):
                lw = core.load[1 + slab](lambda e: e.dma_start(raw[slab][:], win[:, :, 256 * slab:256 * slab + 256]))
                lw = split(core, G, w[slab][0][:], w[slab][1][:], raw[slab][:], [lw])
                for s in range(2):
                    u_tile = 2 * slab + s
                    t = products(s, s, w[slab], lw, [A.last()] if u_tile > 1 else [], False)
                    a = A(lambda e: e.activation(res[s][:, 0:SEQ], core.bank[:, 3 * s:3 * s + 2, :].rearrange("p a n -> p (a n)"),
                                                 ACT.Copy), after=[t] + ([core.store[s].last()] if u_tile > 1 else []))
                    core.store[s](lambda e: e.dma_start(dram["uT"][128 * u_tile:128 * u_tile + 128, :], res[s][:, 0:SEQ]), after=[a])
            xt = [sb1(f"xt{b}", [P, NT + NC, P]) for b in range(2)]
            V(lambda e: e.memset(acc[1][:], 0.0))
            V(lambda e: e.memset(res[0][:], 0.0), after=[core.store[0].last()])
            V(lambda e: e.memset(tap[1][:], 0.0))
            before = [T.last(), A.last(), V.last(), zeroed, core.store[0].last(), core.store[1].last()]
            for q in (T, V, A, G, core.load[1], core.load[2]):
                q.wait(*before)

            def finish(s, i, j, conv, before, marks):
                marks[f"silu_{j}"] = A(lambda e: e.activation(res[s][:], acc[s][:], ACT.Silu, bias=tap[s][:, 9:10]),
                                       after=conv + before("st") + before("xturn"))
                marks[f"st_{j}"] = core.store[s](
                    lambda e: e.dma_start(dram["xbcT"][bass.ds(i * 512 + 128 * j, 128), :], res[s][:]), after=[A.last()])

            def turn(s, i, j, silu, before, marks):
                T.wait(*silu)
                for q, m in ((0, 4), (1, 4), (2, 2)):
                    bank = 6 + q % 2
                    t = core.tr([(lambda c=c: core.bank[:, bank, 128 * c:128 * c + 128], lambda c=c: res[s][:, 512 * q + 128 * c:512 * q + 128 * c + 128])
                                 for c in range(m)], ident, after=before(f"xe{q % 2}") if q < 2 else [first_ev])
                    ev = A(lambda e: e.activation(xt[s][:, 4 * q:4 * q + m, :], core.bank[:, bank, 0:128 * m].rearrange("p (c n) -> p c n", c=m),
                                                  ACT.Copy), after=[t] + (before("xst") if q == 0 else []))
                    if q == 0:
                        first_ev = ev
                    marks[f"xe{q % 2}_{j}"] = ev
                marks[f"xturn_{j}"] = T.last()
                marks[f"xst_{j}"] = core.store[2 + s](lambda e: e.dma_start(
                    dram["xtok"].rearrange("(t p) n -> p t n", p=P)[:, :, bass.ds(i * 512 + 128 * j, 128)], xt[s][:]), after=[ev])

            def body(i, marks):
                prev = lambda k: [marks[k].last_round()] if k in marks else []
                for slab in range(2):
                    lw = core.load[1 + slab](lambda e: e.dma_start(raw[slab][:], win[:, :, bass.ds(i * 512 + COL_XBC + 256 * slab, 256)]),
                                             after=prev(f"split{slab}"))
                    lw = split(core, G, w[slab][0][:], w[slab][1][:], raw[slab][:], [lw], prev(f"mm{slab}"))
                    marks[f"split{slab}"] = lw
                    for s in range(2):
                        first = slab == 0
                        j = 2 * slab + s
                        before = (lambda k: prev(k + str(2 + s))) if first else (lambda k: [marks[k + str(s)]] if k + str(s) in marks else [])
                        same = {"xe0": 1, "xe1": 1, "xst": 2, "st": 2, "xturn": 1, "silu": 1}
                        ago = lambda k, n: [marks[f"{k}_{j - n}"]] if j >= n and f"{k}_{j - n}" in marks else prev(f"{k}_{j - n + 4}")
                        of = lambda k: ago(k, same[k])
                        t = products(s, s, w[slab], lw, before("ev"), True, lambda: turn(s, i, j, of("silu"), of, marks))
                        marks[f"mm{slab}"] = t
                        A(lambda e: e.activation(img[s][:, 1:1 + GRID_H, 1:1 + GRID_W],
                                                 core.bank[:, 3 * s:3 * s + 2, :].rearrange("p a (r c) -> p (a r) c", c=GRID_W),
                                                 ACT.Copy), after=[t] + before("conv"))
                        A(lambda e: e.activation(line[s][:, 1:1 + CTX], core.bank[:, 3 * s + 2, 0:CTX], ACT.Copy))
                        a = A(lambda e: e.activation(tap[s][:], taps[:, bass.ds(i * 4 + j, 1), :].rearrange("p a n -> p (a n)"),
                                                     ACT.Copy))
                        marks[f"ev{j}"] = a
                        finish(1 - s, i, j, [marks[f"conv{j - 1}"]] if j else prev("conv3"), of, marks)
                        V.wait(a, *ago("silu", 1))
                        grid = acc[s][:, 0:SEQ].rearrange("p (r c) -> p r c", c=GRID_W)
                        for dy in range(3):
                            for dx in range(3):
                                src = img[s][:, dy:dy + GRID_H, dx:dx + GRID_W]
                                wt = tap[s][:, 3 * dy + dx:3 * dy + dx + 1]
                                if dy == dx == 0:
                                    V(lambda e: e.tensor_scalar(grid, src, wt, None, ALU.mult))
                                else:
                                    V(lambda e: e.scalar_tensor_tensor(out=grid, in0=src, scalar=wt, in1=grid,
                                                                       op0=ALU.mult, op1=ALU.add), own=True)
                        for dx in range(3):
                            wt = tap[s][:, 3 + dx:4 + dx]
                            if dx == 0:
                                V(lambda e: e.tensor_scalar(acc[s][:, SEQ:TOK], line[s][:, 0:CTX], wt, None, ALU.mult))
                            else:
                                V(lambda e: e.scalar_tensor_tensor(out=acc[s][:, SEQ:TOK], in0=line[s][:, dx:dx + CTX], scalar=wt,
                                                                   in1=acc[s][:, SEQ:TOK], op0=ALU.mult, op1=ALU.add), own=True)
                        marks[f"conv{j}"] = V.last()
            core.loop(NCT // 4, body)
            last = lambda k: [A.last(), T.last(), core.store[1].last(), core.store[2].last(), core.store[3].last()]
            finish(1, NCT // 4, 0, [V.last()], last, {})
            for s in range(2):
                turn(s, NCT // 4, s, [A.last()], last, {})

        zw = [[sb(f"zw_{k}{b}", [P, KD, 512], R32) for k in ("high", "low")] for b in range(2)]
        zo = [sb(f"zo{b}", [P, 512]) for b in range(4)]
        G.wait(z_first)

        def body(i, marks):
            prev = lambda k: [marks[k].last_round()] if k in marks else []
            for b in range(2):
                lw = [marks["raw0"]] if b and "raw0" in marks else prev("raw1")
                marks[f"split{b}"] = split(core, G, zw[b][0][:], zw[b][1][:], z_raw[:], lw, prev(f"mm{b}"))
                marks[f"raw{b}"] = core.load[3](lambda e: e.dma_start(z_raw[:], win[:, :, bass.ds(i * 1024 + COL_Z + 512 * b + 512, 512)]),
                                                after=[marks[f"split{b}"]])
                T.wait(marks[f"split{b}"])
                for m in range(NT):
                    n = NT * b + m
                    s = n % 4
                    old = lambda k: [marks[f"{k}{n - 4}"]] if n >= 4 else prev(f"{k}{n + 12}")
                    t = core.mm(core.bank[:, s, :], [p for k in range(KD) for p in three(
                        *(lambda k=k, a=a: a[:, k, 128 * m:128 * m + 128] for a in (hh, hl)), *(lambda k=k, a=a: a[:, k, :] for a in zw[b]))], after=old("ev"))
                    marks[f"mm{b}"] = t
                    marks[f"ev{n}"] = A(lambda e: e.activation(zo[s][:], core.bank[:, s, :], ACT.Silu), after=[t] + old("st"))
                    marks[f"st{n}"] = core.store[s](lambda e: e.dma_start(
                        dram["z"][128 * m:128 * m + 128, bass.ds(i * 1024 + 512 * b, 512)], zo[s][:]), after=[A.last()])
        core.loop(2, body)
        core.settle()
        wd = [sb(f"wd_{k}", [P, KD, 2 * NH], dt) for k, dt in (("raw", F32), ("high", R32), ("low", R32))]
        dtT = sb("dtT", [2 * NH, TOK])
        lw = core.load[0](lambda e: e.dma_start(wd[0][:], win[:, :, COL_DT:COL_DT + 2 * NH]))
        T.wait(split(core, V, wd[1][:], wd[2][:], wd[0][:], [lw]))
        for j, (n0, n) in enumerate(((0, 512), (512, 512), (1024, 256))):
            core.mm(core.bank[0:2 * NH, j, 0:n], [p for k in range(KD) for p in three(
                *(lambda k=k, a=a: a[:, k, :] for a in wd[1:]), *(lambda k=k, a=a: a[:, k, n0:n0 + n] for a in (hh, hl)))])
            A(lambda e: e.activation(dtT[:, n0:n0 + n], core.bank[0:2 * NH, j, 0:n], ACT.Copy), after=[T.last()])
        t = core.tr([(lambda m=m: core.bank[:, 3, 2 * NH * m:2 * NH * m + 2 * NH], lambda m=m: dtT[:, 128 * m:128 * m + 128])
                     for m in range(NT + NC)], tables["mats"][0:2 * NH, C_ID, 0:2 * NH], after=[A.last()])
        V(lambda e: e.tensor_copy(tables["dt"][:].rearrange("p t h -> p (t h)"), core.bank[:, 3, 0:480]), after=[t])


def fourier(core, dram, tables):
    T, V, A, G = core.T, core.V, core.A, core.G
    with Room(core) as sb:
        groups = sb("f_groups", [P, 256])
        uc = [sb(f"f_u{b}", [P, 4, P]) for b in range(2)]
        AC = sb("f_AC", [P, NT, 2, DF])
        CS = sb("f_CS", [P, 2, KD, SEQ])
        lhs = [sb(f"f_lhs{b}", [P, NT, 2, P]) for b in range(2)]
        mT = sb("f_mT", [P, 4, SEQ])
        g = core.load[0](lambda e: e.dma_start(groups[:], dram["dft_groups"]))
        big = [core.load[3 + j](lambda e: e.dma_start(CS[:, j, :, :], dram["dft_seq"][j].rearrange("(k p) n -> p k n", p=P)))
               for j in range(2)]
        uv = dram["uT"].rearrange("(c p) n -> p c n", p=P)
        T.wait(g)

        def body(i, marks):
            prev = lambda k: [marks[k].last_round()] if k in marks else []
            for b in range(2):
                ld = core.load[1 + b](lambda e: e.dma_start(uc[b][:], uv[:, :, bass.ds(i * 256 + 128 * b, 128)]), after=prev(f"t{b}"))
                T.wait(ld, *prev(f"ev{b}"))
                for ct in range(4):
                    t = T(lambda e: e.matmul(core.bank[:, 2 * b + ct // 2, 256 * (ct % 2):256 * (ct % 2) + 256], uc[b][:, ct, :],
                                             groups[:], start=True, stop=True), inc=ct == 3)
                marks[f"t{b}"] = T.last()
                for half in range(2):
                    for cs in range(2):
                        V(lambda e: e.tensor_copy(
                            AC[:, bass.ds(i * 2 + b, 1), cs, 256 * half:256 * half + 256].rearrange("p a (c n) -> p (a c) n", c=2),
                            core.bank[:, 2 * b + half, :].rearrange("p (c s n) -> p c s n", c=2, s=2)[:, :, cs, :]),
                          after=[T.last()])
                marks[f"ev{b}"] = V.last()
        core.loop(NT // 2, body)
        T.wait(*big)
        G.wait(V.last())

        def body(i, marks):
            prev = lambda k: [marks[k].last_round()] if k in marks else []
            for b in range(2):
                g = G(lambda e: e.tensor_copy(lhs[b][:].rearrange("p t s n -> p (t s) n"),
                                              AC[:, :, :, bass.ds(i * 256 + 128 * b, 128)].rearrange("p t s n -> p (t s) n")),
                      after=prev(f"t{b}"))
                T.wait(g, *prev(f"ev{b}"))
                for half in range(2):
                    core.mm(core.bank[:, 4 + 2 * b + half, :],
                            [(lambda k=k, s=s: lhs[b][:, k, s, :], lambda k=k, s=s: CS[:, s, k, 512 * half:512 * half + 512])
                             for k in range(KD) for s in range(2)])
                marks[f"t{b}"] = T.last()
                marks[f"ev{b}"] = A(lambda e: e.activation(mT[:, bass.ds(i * 2 + b, 1), :].rearrange("p a n -> p (a n)"),
                                                           core.bank[:, 4 + 2 * b:6 + 2 * b, :].rearrange("p a n -> p (a n)"),
                                                           ACT.Copy), after=[T.last()])
        core.loop(2, body)
        wf = sb("f_w", [P, 4, DF])
        bf = sb("f_b", [P, DF])
        z = [sb(f"f_z{b}", [P, DF]) for b in range(2)]
        o = [sb(f"f_o{b}", [P, DF]) for b in range(2)]
        l4 = [sb(f"f_l{b}", [P, 4, P]) for b in range(2)]
        core.load[0](lambda e: e.dma_start(wf[:], dram["w_fourier"].rearrange("(k p) n -> p k n", p=P)))
        got = core.load[0](lambda e: e.dma_start(bf[:], row(dram["b_fourier"])))
        T.wait(got)
        V.wait(got)
        G.wait(A.last())

        def body(i, marks):
            prev = lambda k: [marks[k].last_round()] if k in marks else []
            for b in range(2):
                lz = core.load[1 + b](lambda e: e.dma_start(z[b][:], dram["z"][bass.ds(i * 256 + 128 * b, 128), 0:DF]), after=prev(f"v{b}"))
                g = G(lambda e: e.tensor_copy(l4[b][:], mT[:, :, bass.ds(i * 256 + 128 * b, 128)]), after=prev(f"t{b}"))
                t = core.mm(core.bank[:, b, :], [(lambda k=k: l4[b][:, k, :], lambda k=k: wf[:, k, :]) for k in range(4)],
                            after=[g] + prev(f"v{b}"))
                marks[f"t{b}"] = t
                V(lambda e: e.tensor_tensor(o[b][:], core.bank[:, b, :], bf[:], ALU.add), after=[t] + prev(f"st{b}"))
                marks[f"v{b}"] = V(lambda e: e.tensor_tensor(o[b][:], o[b][:], z[b][:], ALU.mult), after=[lz], own=True)
                marks[f"st{b}"] = core.store[b](lambda e: e.dma_start(dram["mix"][bass.ds(i * 256 + 128 * b, 128), 0:DF], o[b][:]),
                                                after=[V.last()])
        core.loop(NT // 2, body)


def constants():
    k = np.arange(P)
    mats = np.stack([k[:, None] == k, k[:, None] <= k, k[:, None] >= k, k[:, None] > k, k[:, None] < k,
                     np.ones((P, P), bool)]).astype(np.float32)
    n = np.arange(SEQ)
    ang = 2 * np.pi * ((n[:, None] * n) % SEQ) / SEQ
    scale = 1.0 / np.sqrt(SEQ * 64.0)
    g = np.arange(64)
    small = 2 * np.pi * ((g[:, None] * g) % 64) / 64
    groups = np.zeros((P, 2, P))
    for b in range(2):
        groups[64 * b:64 * b + 64, 0, 64 * b:64 * b + 64] = np.cos(small)
        groups[64 * b:64 * b + 64, 1, 64 * b:64 * b + 64] = np.sin(small)
    return {"mats": mats, "dft_seq": np.stack([np.cos(ang) * scale, -np.sin(ang) * scale]).astype(np.float32),
            "dft_groups": groups.reshape(P, 256).astype(np.float32),
            "counts": np.concatenate([np.arange(4, 0, -1), np.arange(32, 0, -1), 128 * np.arange(8),
                                      np.arange(48)]).astype(np.float32),
            "rope_inv": (10000.0 ** (-np.arange(32, dtype=np.float64) / 32)).astype(np.float32),
            "far": np.stack([np.where(k[None, :] <= k[:, None], 0.0, FAR),
                             np.where(k[None, :] // 64 <= k[:, None] // 64, 0.0, FAR)]).astype(np.float32)}


def load_tables(core, sb, dram):
    t = {"mats": sb("mats", [P, 6, P]), "eps": sb("eps", [P, 1]), "dt": sb("dt", [P, NT + NC, 2 * NH]),
         "logits": sb("logits", [P, NT, 36]), "weight": sb("weight", [P, 2, NT]), "slot": sb("slot", [P, 2, NT], I32),
         "expert": sb("expert", [P, 48], I32), "live": sb("live", [P, 1], I32)}
    core.V(lambda e: e.memset(t["eps"][:], EPS))
    core.load[0](lambda e: e.dma_start(t["mats"][:], dram["mats"].rearrange("m p n -> p m n")))
    core.settle()
    return t


def decays(core, dram, tables, sb):
    T, V, A = core.T, core.V, core.A
    n = NT + NC
    t = {k: sb("s_" + k, [P, n, 2 * NH]) for k in ("dt", "a", "ec", "dec", "et")}
    with Room(core) as s1:
        bias, an = s1("s_bias", [P, 2 * NH]), s1("s_an", [P, 2 * NH])
        p, q = s1("s_p", [P, n, 2 * NH]), s1("s_q", [P, n, 2 * NH])
        core.load[0](lambda e: e.dma_start(bias[:], row(dram["dt_bias"].rearrange("a h -> (a h)"))))
        got = core.load[0](lambda e: e.dma_start(an[:], row(dram["a_log"].rearrange("a h -> (a h)"))))
        a = A(lambda e: e.activation(an[:], an[:], ACT.Exp), after=[got])
        V(lambda e: e.tensor_tensor(p[:], tables["dt"][:], over(bias[:], 1, n), ALU.add), after=[got])
        V(lambda e: e.tensor_scalar(q[:], p[:], -1.0, None, ALU.mult), own=True)
        V(lambda e: e.tensor_tensor(q[:], q[:], p[:], ALU.min), own=True)
        A(lambda e: e.activation(q[:], q[:], ACT.Exp), after=[V.last()])
        A(lambda e: e.activation(q[:], q[:], ACT.Ln, bias=1.0), own=True)
        V(lambda e: e.scalar_tensor_tensor(out=t["dt"][:], in0=p[:], scalar=0.0, in1=q[:], op0=ALU.max, op1=ALU.add),
          after=[A.last()])
        V(lambda e: e.scalar_tensor_tensor(out=t["a"][:], in0=t["dt"][:], scalar=-1.0, in1=over(an[:], 1, n),
                                           op0=ALU.mult, op1=ALU.mult), own=True, after=[a])
        T.wait(V.last())
        mats = tables["mats"]
        T(lambda e: e.matmul(core.bank[:, 0, 0:480], mats[:, C_LE, :], t["a"][:].rearrange("p t h -> p (t h)"), start=True, stop=True), inc=False)
        T(lambda e: e.matmul(core.bank[:, 1, 0:480], mats[:, C_GE, :], t["a"][:].rearrange("p t h -> p (t h)"), start=True, stop=True), inc=False)
        T(lambda e: e.matmul(core.bank[:, 2, 0:480], mats[:, C_ONE, :], t["a"][:].rearrange("p t h -> p (t h)"), start=True, stop=True))
        for half in range(2):
            cols = slice(NH * half, NH * half + NH)
            cum = core.bank[:, half, 0:480].rearrange("p (t h) -> p t h", h=2 * NH)[:, :, cols]
            tot = core.bank[:, 2, 0:480].rearrange("p (t h) -> p t h", h=2 * NH)[:, :, cols]
            A(lambda e: e.activation(t["ec"][:, :, cols], cum, ACT.Exp), after=[T.last()])
            A(lambda e: e.activation(t["et"][:, :, cols], tot, ACT.Exp))
            V(lambda e: e.tensor_copy(p[:, :, cols], cum), own=True, after=[A.last()])
            V(lambda e: e.tensor_tensor(q[:, :, cols], tot, p[:, :, cols], ALU.subtract), own=True)
            A(lambda e: e.activation(q[:, :, cols], q[:, :, cols], ACT.Exp), after=[V.last()])
            V(lambda e: e.tensor_tensor(t["dec"][:, :, cols], q[:, :, cols], t["dt"][:, :, cols], ALU.mult), after=[A.last()])
    return t


def heads(ap):
    return ap.rearrange("p (h d) -> p h d", d=HP)


def state_space(core, dram, tables):
    T, V, A, G = core.T, core.V, core.A, core.G
    ident = tables["mats"][:, C_ID, :]
    with Room(core) as sb:
        t = decays(core, dram, tables, sb)
        xb = [sb(f"s_xb{b}", [P, 2 * NBC, P]) for b in range(2)]
        Xs = [sb(f"s_X{b}", [P, DS + NBC * NST]) for b in range(2)]
        xds = [sb(f"s_xd{b}", [P, DS]) for b in range(2)]
        H = sb("s_H", [P, DS])
        HB = sb("s_HB", [P, NT, DS])
        xv = dram["xbcT"].rearrange("(t p) n -> p t n", p=P)

        def load_tokens(b, tile, free):
            return core.load[5 + b](lambda e: e.dma_start(Xs[b][:], dram["xtok"][bass.ds(tile * P, P), 2 * P:2 * P + DS + NBC * NST]), after=free)

        def load_channels(b, tile, free):
            return core.load[1 + b](lambda e: e.dma_start(xb[b][:], xv[:, 1 + DS // P:, bass.ds(tile * P, P)]), after=free)

        def weigh(tile, b, way, ready):
            return V(lambda e: e.tensor_tensor(heads(xds[b][:]), heads(Xs[b][:, 0:DS]),
                                               over(t["dec"][:, bass.ds(tile, 1), NH * way:NH * way + NH].rearrange("p a h -> p (a h)"), 2, HP),
                                               ALU.mult), after=ready)

        def state_step(tile, b, way, ready, weighed, free=((),) * 4, old=H[:], new=H[:]):
            X, xd = Xs[b], xds[b]
            T.wait(weighed)
            cols = slice(NH * way, NH * way + NH)
            for g in range(NBC):
                core.mm(core.bank[:, 2 + g, 0:384], [(lambda: X[:, DS + NST * g:DS + NST * g + NST],
                                                      lambda: xd[:, 384 * g:384 * g + 384])], after=free[g])
            done = T.last()
            V(lambda e: e.tensor_tensor(heads(new), heads(old),
                                        over(t["et"][:, bass.ds(tile, 1), cols].rearrange("p a h -> p (a h)"), 2, HP), ALU.mult), own=True, after=ready)
            return V(lambda e: e.tensor_tensor(new.rearrange("p (g n) -> p g n", g=NBC), new.rearrange("p (g n) -> p g n", g=NBC),
                                               core.bank[:, 2:6, 0:384], ALU.add), own=True, after=[done])

        V(lambda e: e.memset(H[:], 0.0))
        done = [V.last()]
        state = lambda tile: HB[:, bass.ds(tile, 1), :].rearrange("p a n -> p (a n)")
        for tile, new in ((9, H[:]), (8, HB[:, NT - 1, :])):
            got = [load_tokens(tile % 2, tile, [])]
            done = [state_step(tile, tile % 2, 1, done, weigh(tile, tile % 2, 1, got + done), (done,) * 4, H[:], new)]
        for q in (T, V, core.load[5]):
            q.wait(*done)

        def steps(tiles, marks, prev):
            weighed = []
            for b, tile in enumerate(tiles):
                ready = load_tokens(b, tile, prev(f"mm{b}"))
                weighed.append(weigh(tile, b, 1, [ready] + prev(f"mm{b}")))
            before = prev("step1")
            for b, tile in enumerate(tiles):
                before = [state_step(tile, b, 1, before, weighed[b], (before,) * 4, state(tile), state(tile - 1))]
                marks[f"step{b}"], marks[f"mm{b}"] = before[0], T.last()

        def body(i, marks):
            steps([i * -2 + (NT - 1 - b) for b in range(2)], marks, lambda k: [marks[k].last_round()] if k in marks else [])
        final = core.loop(NT // 2 - 1, body)
        steps([1], {}, lambda k: [final[k]])
        core.settle()

        V(lambda e: e.memset(H[:], 0.0))
        done = [V.last()]
        for tile in (8, 9):
            got = [load_tokens(tile % 2, tile, [])]
            done = [state_step(tile, tile % 2, 0, done, weigh(tile, tile % 2, 0, got + done), (done,) * 4)]

        LE, GE = tables["mats"][:, C_LE, :], tables["mats"][:, C_GE, :]
        cbs = [sb(f"s_cb{b}", [P, 2, NBC, P]) for b in range(2)]
        xfs2 = [[sb(f"s_xf{b}{w}", [P, DS]) for w in range(2)] for b in range(2)]
        R = [sb(f"s_R{w}", [P, HG, P]) for w in range(2)]
        E = [sb(f"s_E{b}", [P, HG, P]) for b in range(2)]
        M = [[sb(f"s_M{b}{w}", [P, HG, P]) for w in range(2)] for b in range(2)]
        yts = [sb(f"s_y{b}", [P, DS]) for b in range(2)]
        y2 = [sb(f"s_y2{w}", [P, 384]) for w in range(2)]
        sq = sb("s_sq", [P, 384])
        skip = sb("s_skip", [P, NH])
        nw = sb("s_nw", [P, DS])
        zt = [sb(f"s_z{b}", [P, DS]) for b in range(2)]
        ss, sd, rs = (sb(f"s_{k}", [P, NBC]) for k in ("ss", "sd", "rs"))
        core.load[0](lambda e: e.dma_start(skip[:], row(dram["d_skip"])))
        got = core.load[0](lambda e: e.dma_start(nw[:], row(dram["ssd_norm_w"])))
        for e in core.engines:
            e.wait_ge(core.load[0].sem, core.load[0].n)
            for x in (T, V, A):
                e.wait_ge(x.sem, x.n)

        ROUND = 4

        class Chunk:

            def __init__(self, i, j, marks):
                self.tile, self.j, self.b, self.marks = i * ROUND + j, j, j % 2, marks
                self.X, self.yt, self.cb, self.xf = Xs[self.b], yts[self.b], cbs[self.b], xfs2[self.b]
                self.dT, self.evE, self.mE, self.mG, self.yT, self.offs = {}, {}, {}, {}, {}, {}

            def ago(self, k, n):
                if self.j >= n:
                    return [self.marks[f"{k}{self.j - n}"]] if f"{k}{self.j - n}" in self.marks else []
                k = f"{k}{self.j - n + ROUND}"
                return [self.marks[k].last_round()] if k in self.marks else []

            def mark(self, k, t):
                self.marks[f"{k}{self.j}"] = t

            def col(self, name, a, n):
                return t[name][:, bass.ds(self.tile, 1), a:a + n].rearrange("p a h -> p (a h)")

            def head(self):
                b, tile, X = self.b, self.tile, self.X
                got, gx = load_channels(b, tile, self.ago("products", 2)), load_tokens(b, tile, self.ago("step", 2))
                self.lz = core.load[3 + b](lambda e: e.dma_start(zt[b][:], dram["z"][bass.ds(tile * P, P), DF:DF + DS]), after=self.ago("gate", 2))
                self.gx = gx
                for g in range(NBC):
                    core.mm(core.bank[:, 1, 128 * g:128 * g + 128], [(lambda: xb[b][:, g, :], lambda: xb[b][:, NBC + g, :])],
                            after=self.ago("lastE", 1) + [got] if g == 0 else [])
                cbt = T.last()
                for w, mask in ((0, LE), (1, GE)):
                    V(lambda e: e.tensor_tensor(self.cb[:, w, :, :], core.bank[:, 1, :].rearrange("p (g n) -> p g n", g=NBC),
                                                over(mask, 1, NBC), ALU.mult), after=[cbt] + self.ago("MG", 2) + self.ago("M", 2))
                self.cbv = V.last()
                self.differences(0)
                wait = [gx] + self.ago("products", 2)
                self.xfs = [Q(lambda e: e.tensor_tensor(heads(self.xf[w][:]), heads(X[:, 0:DS]), over(self.col("dt", NH * w, NH), 2, HP), ALU.mult),
                              after=wait) for w, Q in ((0, V), (1, G))]
                self.mark("xf", G.last())
                self.weights(0)
                self.differences(1)
                self.skipped = G(lambda e: e.tensor_tensor(heads(self.yt[:]), heads(X[:, 0:DS]), over(skip[:], 2, HP), ALU.mult),
                                 after=[gx] + self.ago("st", 2))
                self.mark("skip", G.last())

            def differences(self, g):
                rs_ = [Q(lambda e: e.tensor_tensor(R[w][:], over(mask, 1, HG), over(self.col("a", NH * w + HG * g, HG), 2, P), ALU.mult),
                         after=[self.dT[g - 1]] if g else self.ago("lastD", 1)) for w, Q, mask in ((0, V, LE), (1, G, GE))]
                T.wait(*rs_, *([self.evE[g - 1]] if g else self.ago("lastE", 1) + [self.cbv]))
                for half in range(2):
                    for w, m in ((0, C_GT), (1, C_LT)):
                        T(lambda e: e.matmul(core.bank[:, half, 0:384], tables["mats"][:, m, :],
                                             R[w][:, 3 * half:3 * half + 3, :].rearrange("p h n -> p (h n)"),
                                             start=w == 0, stop=w == 1), inc=half == 1 and w == 1)
                self.dT[g] = T.last()
                s = g % 2
                self.evE[g] = A(lambda e: e.activation(E[s][:].rearrange("p (a h) n -> p a (h n)", a=2), core.bank[:, 0:2, 0:384], ACT.Exp),
                                after=[self.dT[g]] + ([self.mE[g - 2], self.mG[g - 2]] if g > 1 else self.ago("M", 1) + self.ago("MG", 1)))

            def weights(self, g):
                s = g % 2
                wait = [self.evE[g], self.cbv] + ([self.yT[g - 2]] if g > 1 else self.ago(f"products_{g}_", 1))
                for w, Q, m in ((0, V, self.mE), (1, G, self.mG)):
                    m[g] = Q(lambda e: e.tensor_tensor(M[s][w][:], E[s][:], over(self.cb[:, w, g, :], 1, HG), ALU.mult), after=wait)

            def products(self, g):
                s, y0, b = g % 2, 2 + 3 * (g % 2), self.b
                T.wait(self.mE[g], self.mG[g], *self.xfs, *([self.offs[g - 2]] if g > 1 else self.ago("step", 1) + self.ago("gathered", 1)))
                for h in range(HG):
                    c0 = HP * (HG * g + h)
                    for w in range(2):
                        T(lambda e: e.matmul(core.bank[:, y0, HP * h:HP * h + HP], M[s][w][:, h, :], self.xf[w][:, c0:c0 + HP],
                                             start=w == 0, stop=w == 1), inc=False)
                T(lambda e: e.matmul(core.bank[:, y0 + 1, 0:384], xb[b][:, NBC + g, :], H[:, 384 * g:384 * g + 384], start=True, stop=True), inc=False)
                T(lambda e: e.matmul(core.bank[:, y0 + 2, 0:384], xb[b][:, NBC + g, :],
                                     HB[:, bass.ds(self.tile, 1), 384 * g:384 * g + 384].rearrange("p a n -> p (a n)"), start=True, stop=True))
                self.yT[g] = T.last()
                if g > 1:
                    self.mark(f"products_{g - 2}_", T.last())
                self.mark("products", T.last())

            def gather(self, g):
                y0 = 2 + 3 * (g % 2)
                y = self.yt[:, 384 * g:384 * g + 384]
                for w in range(2):
                    V(lambda e: e.tensor_tensor(heads(y2[w][:]), heads(core.bank[:, y0 + 1 + w, 0:384]),
                                                over(self.col("ec", NH * w + HG * g, HG), 2, HP), ALU.mult),
                      after=[self.yT[g]] + ([self.offs[g - 1]] if g else self.ago("gathered", 1)))
                V(lambda e: e.tensor_tensor(y, y, core.bank[:, y0, 0:384], ALU.add), after=[self.skipped])
                for w in range(2):
                    V(lambda e: e.tensor_tensor(y, y, y2[w][:], ALU.add), own=True)
                self.offs[g] = V.last()
                self.mark("gathered", V.last())

            def groups(self, ahead, between):
                for g in range(NBC):
                    if g + 1 < NBC:
                        self.weights(g + 1)
                    if g == 1:
                        weighed = weigh(self.tile, self.b, 0, [self.gx] + self.ago("step", 1))
                    self.products(g)
                    if g + 2 < NBC:
                        self.differences(g + 2)
                    if g == NBC - 1:
                        self.mark("M", self.mE[3]), self.mark("MG", self.mG[3]), self.mark("lastD", self.dT[3]), self.mark("lastE", self.evE[3])
                        ahead()
                    self.gather(g)
                    if g == 0:
                        between()
                even, odd = [self.offs[2]], [self.offs[3]]
                self.mark("step", state_step(self.tile, self.b, 0, [self.yT[3]], weighed, (even, even, even, odd)))

            def gate(self):
                yt = self.yt
                V(lambda e: e.tensor_tensor(yt[:], yt[:], zt[self.b][:], ALU.mult), own=True, after=[self.lz, self.offs[3]])
                self.mark("gate", V.last())
                for g in range(NBC):
                    y = yt[:, 384 * g:384 * g + 384]
                    V(lambda e: e.tensor_tensor_reduce(out=sq[:], in0=y, in1=y, scale=1.0 / 384, scalar=0.0, op0=ALU.mult, op1=ALU.add,
                                                       accum_out=ss[:, g:g + 1]), own=True)
                A(lambda e: e.activation(sd[:], ss[:], ACT.Sqrt, bias=tables["eps"][:, 0:1]), after=[V.last()])
                V(lambda e: e.reciprocal(rs[:], sd[:]), after=[A.last()])
                for g in range(NBC):
                    y = yt[:, 384 * g:384 * g + 384]
                    V(lambda e: e.scalar_tensor_tensor(out=y, in0=y, scalar=rs[:, g:g + 1], in1=nw[:, 384 * g:384 * g + 384],
                                                       op0=ALU.mult, op1=ALU.mult), own=g == 0)
                self.mark("st", core.store[self.b](lambda e: e.dma_start(dram["mix"][bass.ds(self.tile * P, P), DF:DF + DS], yt[:]), after=[V.last()]))

        def body(i, marks):
            chunks = [Chunk(i, j, marks) for j in range(ROUND)]
            chunks[0].head()
            for j, c in enumerate(chunks):
                more = j + 1 < ROUND
                c.groups(chunks[j + 1].head if more else lambda: None, chunks[j - 1].gate if j else lambda: None)
            chunks[-1].gate()
        core.loop(NT // ROUND, body)


def prev_of(marks):
    return lambda k: [marks[k].last_round()] if k in marks else []


def ago_of(marks, j, size):
    def ago(k, n):
        if j >= n:
            return [marks[f"{k}{j - n}"]] if f"{k}{j - n}" in marks else []
        k = f"{k}{j - n + size}"
        return [marks[k].last_round()] if k in marks else []
    return ago


def turn_rows(core, out, src, n, ident, banks, after, free):
    for q in range((n + 3) // 4):
        m = min(4, n - 4 * q)
        bank = banks[q % len(banks)]
        wait = ([] if q else list(after)) + (free[q % len(banks)] if q < len(banks) else [evs[q - len(banks)]])
        if q == 0:
            evs = []
        t = core.tr([(lambda j=j: core.bank[:, bank, 128 * j:128 * j + 128],
                      lambda j=j: src[:, 128 * (4 * q + j):128 * (4 * q + j) + 128]) for j in range(m)], ident, after=wait)
        evs.append(core.A(lambda e: e.activation(out[:, 4 * q:4 * q + m, :],
                                                 core.bank[:, bank, 0:128 * m].rearrange("p (j n) -> p j n", j=m), ACT.Copy), after=[t]))
    return t, evs[-1]


def close_first(core, dram, tables):
    T, V, A = core.T, core.V, core.A
    ident = tables["mats"][:, C_ID, :]
    with Room(core) as sb:
        KM = 2 * D // P
        w = sb("c_w", [P, KM, D])
        gate, fin, gain, shift = (sb("c_" + k, [P, D]) for k in ("gate", "fin", "gain", "shift"))
        y, x1, h = (sb("c_" + k, [P, D]) for k in ("y", "x1", "h"))
        x = [sb(f"c_xin{b}", [P, D]) for b in range(2)]
        mix = [sb(f"c_mix{b}", [P, 2 * D]) for b in range(2)]
        mT = [sb(f"c_mT{b}", [P, KM, P]) for b in range(2)]
        norm = Norm(core, sb, "c_n")
        wl = []
        for j in range(4):
            quarter = Queue(core.nc, core.nc.gpsimd, f"w_out_in{j}", 16, 0)
            wl.append(quarter(lambda e: e.dma_start(w[:, 4 * j:4 * j + 4, :], dram["w_out"].rearrange("(k p) n -> p k n", p=P)[:, 4 * j:4 * j + 4, :]),
                              after=wl[-1:]))
        core.load[9](lambda e: e.dma_start(gate[:], row(dram["mods"][0, 2 * D:3 * D])))
        gl = core.load[9](lambda e: e.dma_start(fin[:], row(dram["final_norm_w"])))
        m2 = dram["mod2"][0, :]
        gain_rows(core, gain[:], dram["norm1_g_2"], m2[D:2 * D], shift[:], m2[0:D], y[:])
        V.wait(gl)

        ROUND = 4

        def turn(i, j, marks):
            b, ago = j % 2, ago_of(marks, j, ROUND)
            at = bass.ds(i * (ROUND * P) + P * j, P)
            lm = core.load[1 + b](lambda e: e.dma_start(mix[b][:], dram["mix"][at, :]), after=ago("turned", 2))
            lx = core.load[3 + b](lambda e: e.dma_start(x[b][:], dram["x"][at, :]), after=ago("x", 2))
            free = ago("ev", 1)
            T.wait(*ago("mm", 2))
            A.wait(*ago("mm", 2))
            t, ev = turn_rows(core, mT[b], mix[b][:], KM, ident, (4, 5, 6, 7), [lm], [free] * 4)
            marks[f"turned{j}"], marks[f"ev{j}"] = t, ev
            return lx, ev

        def close(i, j, marks, lx, ev):
            b, ago = j % 2, ago_of(marks, j, ROUND)
            at = bass.ds(i * (ROUND * P) + P * j, P)
            T.wait(ev, *ago("mul", 2))
            for q in range(4):
                for half in range(2):
                    core.mm(core.bank[:, 2 * b + half, :], [(lambda k=k: mT[b][:, k, :], lambda k=k: w[:, k, 512 * half:512 * half + 512])
                                                            for k in range(4 * q, 4 * q + 4)], after=[wl[q]] if j == 0 and half == 0 else [],
                            start=q == 0, stop=q == 3)
            marks[f"mm{j}"] = T.last()
            marks[f"mul{j}"] = V(lambda e: e.tensor_tensor(y[:], core.bank[:, 2 * b:2 * b + 2, :].rearrange("p a n -> p (a n)"), gate[:], ALU.mult),
                                 after=[T.last()], own=True)
            marks[f"x{j}"] = V(lambda e: e.tensor_tensor(y[:], y[:], x[b][:], ALU.add), after=[lx], own=True)
            V.wait(norm.rstd(y[:], tables["eps"][:, 0:1], [V.last()]))
            norm.apply(x1[:], y[:], fin[:], after=ago("stx", 1))
            marks[f"stx{j}"] = core.store[0](lambda e: e.dma_start(dram["x1"][at, :], x1[:]), after=[V.last()])
            V.wait(norm.rstd(x1[:], tables["eps"][:, 0:1], [V.last()]))
            norm.apply(h[:], x1[:], gain[:], shift[:], after=ago("sth", 1))
            marks[f"sth{j}"] = core.store[1](lambda e: e.dma_start(dram["h1"][at, :], h[:]), after=[V.last()])

        def body(i, marks):
            ready = turn(i, 0, marks)
            for j in range(ROUND):
                following = turn(i, j + 1, marks) if j + 1 < ROUND else None
                close(i, j, marks, *ready)
                ready = following
        core.loop(NT // ROUND, body)


COLS2 = 4816
C_FQ, C_FK, C_FV, C_FL, C_DQ, C_DK, C_DV, C_IQ, C_IK, C_IW, C_GF = 0, 512, 1024, 1536, 1544, 2056, 2120, 2184, 2696, 2760, 2768


def project_second(core, dram, tables):
    T, V, A, G = core.T, core.V, core.A, core.G
    ident = tables["mats"][:, C_ID, :]
    with Room(core) as sb:
        ld = core.load
        hh, hl = (sb(f"p_{k}", [P, KD, SEQ], R32) for k in ("high", "low"))
        raw = sb("p_raw", [P, KD, 512])
        w = [[sb(f"p_w_{k}{b}", [P, KD, 512], R32) for k in ("high", "low")] for b in range(2)]
        o = [sb(f"p_o{b}", [P, 512]) for b in range(4)]
        wv = dram["w_in_2"].rearrange("(k p) n -> p k n", p=P)

        columns = lambda c, n=512: (lambda e: e.dma_start(raw[:, :, 0:n], wv[:, :, c]))
        ld[3](columns(slice(0, 512)))
        with Room(core) as sb1:
            h = [sb1(f"p_h{b}", [P, D]) for b in range(2)]

            def body(i, marks):
                prev = prev_of(marks)
                for b in range(2):
                    ld = core.load[1 + b](lambda e: e.dma_start(h[b][:], dram["h1"][bass.ds(i * 256 + 128 * b, 128), :]), after=prev(f"t{b}"))
                    for half in range(2):
                        t = core.tr([(lambda k=k: core.bank[:, 2 * b + half, 128 * k:128 * k + 128],
                                      lambda k=k: h[b][:, 512 * half + 128 * k:512 * half + 128 * k + 128]) for k in range(4)], ident,
                                    after=[ld] + prev(f"ev{b}"))
                        marks[f"t{b}"] = t
                        part = lambda to: to[:, 4 * half:4 * half + 4, bass.ds(i * 256 + 128 * b, 128)]
                        marks[f"ev{b}"] = split(core, None, part(hh), part(hl), core.bank[:, 2 * b + half, :].rearrange("p (k n) -> p k n", k=4), [t])
            core.loop(NT // 2, body)

        def chunk(b, at, n, following, marks, prev, between=lambda m: None):
            loaded = [marks["raw0"]] if b and "raw0" in marks else prev("raw1")
            marks[f"split{b}"] = split(core, G, w[b][0][:, :, 0:n], w[b][1][:, :, 0:n], raw[:, :, 0:n], loaded, prev(f"mm{b}"))
            marks[f"raw{b}"] = ld[3](following, after=[marks[f"split{b}"]])
            T.wait(marks[f"split{b}"])
            for m in range(NT):
                j = NT * b + m
                s = j % 4
                old = lambda k: ([marks[f"{k}{j - 4}"]] if f"{k}{j - 4}" in marks else []) if j >= 4 else prev(f"{k}{j + 12}")
                t = core.mm(core.bank[:, s, 0:n], [p for k in range(KD) for p in three(
                    *(lambda k=k, a=a: a[:, k, 128 * m:128 * m + 128] for a in (hh, hl)), *(lambda k=k, a=a: a[:, k, 0:n] for a in w[b]))], after=old("pe"))
                marks[f"mm{b}"] = t
                Q, f = (A, lambda e: e.activation(o[s][:, 0:n], core.bank[:, s, 0:n], ACT.Copy)) if s % 2 else \
                       (V, lambda e: e.tensor_copy(o[s][:, 0:n], core.bank[:, s, 0:n]))
                marks[f"pe{j}"] = Q(f, after=[t] + old("ps"))
                marks[f"ps{j}"] = core.store[s](lambda e: e.dma_start(dram["proj"][128 * m:128 * m + 128, at], o[s][:, 0:n]), after=[Q.last()])
                between(m)

        def body(i, marks):
            for b in range(2):
                at = lambda c: bass.ds(i * 1024 + 512 * c, 512)
                chunk(b, at(b), 512, columns(at(b + 1)), marks, prev_of(marks))
        final = core.loop(2, body)
        marks = dict(final)
        pieces = head_tiles(core, dram, tables, sb, 4)
        chunk(0, slice(2048, 2560), 512, columns(slice(2560, C_GF), C_GF - 2560), marks, lambda k: [final[k]])
        chunk(1, slice(2560, C_GF), C_GF - 2560, columns(slice(COLS2 - 512, COLS2)), marks, lambda k: [final[k]])
        for q in (T, V, A, G, ld[1], ld[3]):
            q.wait(T.last(), V.last(), A.last(), G.last(), *(core.store[n].last() for n in range(4)), ld[3].last())

        def body(i, marks):
            for b in range(2):
                tiles = [pieces(i, 2 * b + c, marks) for c in range(2)]
                at = lambda c: bass.ds(i * -1024 + (COLS2 - 512 - 512 * c), 512)
                chunk(b, at(b), 512, columns(at(b + 1)), marks, prev_of(marks), lambda m: next(tiles[m // 4], None))
        core.loop(2, body)


ROPE_C1, ROPE_C2, ROPE_C3 = 6.28125, 0.0019353071693331003, 1.0253131677018246e-11
MAGIC = 1.5 * 2 ** 23


def head_tiles(core, dram, tables, sb, ROUND):
    T, V, A, G = core.T, core.V, core.A, core.G
    ident = tables["mats"][:, C_ID, :]
    ld = core.load
    gq, gk, dgq, dgk = (sb("h_" + k, [P, 64]) for k in ("gq", "gk", "dgq", "dgk"))
    bf = sb("h_bf", [P, 8])
    inv = sb("h_inv", [P, 32])
    posi, pos = sb("h_posi", [P, NT], I32), sb("h_pos", [P, NT])
    for t, k in ((gq, "qn_fox_2"), (gk, "kn_fox_2"), (dgq, "qn_dsa_2"), (dgk, "kn_dsa_2"), (bf, "b_fgt_2"), (inv, "rope_inv")):
        ld[0](lambda e: e.dma_start(t[:], row(dram[k])))
    with core.nc.allow_non_contiguous_dma(reason="one position a partition"):
        got = ld[0](lambda e: e.dma_start(posi[:], dram["positions_2"].rearrange("(t p) -> p t", p=P)))
    sq = sb("h_sq", [P, 2 * 512])
    ang, red, kk = (sq[:, 256 * k:256 * k + 256].rearrange("p (t n) -> p t n", t=NT) for k in range(3))
    cos, sin = sb("h_cos", [P, NT, 32]), sb("h_sin", [P, NT, 32])
    V(lambda e: e.tensor_copy(pos[:], posi[:]), after=[got])
    V(lambda e: e.tensor_tensor(ang, over(pos[:], 2, 32), over(inv[:], 1, NT), ALU.mult), own=True)
    for table, turn in ((sin, 0.0), (cos, 0.25)):
        V(lambda e: e.tensor_scalar(kk, ang, 1.0 / (2 * np.pi), turn, ALU.mult, ALU.add), own=True)
        V(lambda e: e.tensor_scalar(kk, kk, MAGIC, None, ALU.add), own=True)
        V(lambda e: e.tensor_scalar(kk, kk, -MAGIC, None, ALU.add), own=True)
        V(lambda e: e.scalar_tensor_tensor(out=red, in0=kk, scalar=-ROPE_C1, in1=ang, op0=ALU.mult, op1=ALU.add), own=True, after=[A.last()])
        V(lambda e: e.scalar_tensor_tensor(out=red, in0=kk, scalar=-ROPE_C2, in1=red, op0=ALU.mult, op1=ALU.add), own=True)
        V(lambda e: e.scalar_tensor_tensor(out=red, in0=kk, scalar=-ROPE_C3, in1=red, op0=ALU.mult, op1=ALU.add), own=True)
        if turn:
            V(lambda e: e.tensor_scalar(red, red, 2 * np.pi * turn, None, ALU.add), own=True)
        V(lambda e: e.tensor_scalar(red, red, 3.1415925, -3.1415925, ALU.min, ALU.max), own=True)
        A(lambda e: e.activation(table[:], red, ACT.Sin), after=[V.last()])
    V.wait(A.last())
    G.wait(A.last())

    x = [sb(f"h_x{b}", [P, C_GF]) for b in range(2)]
    ss, sd, rs = (sb("h_" + k, [P, 26]) for k in ("ss", "sd", "rs"))
    r1, r2, r3 = (sq[:, 256 * k:256 * k + 256].rearrange("p (h n) -> p h n", h=8) for k in range(3))
    lf, l2, ft, carry = (sb("h_" + k, [P, 8]) for k in ("lf", "l2", "ft", "carry"))
    turned = [[sb(f"h_t_{k}{b}", [P, 4, P], R32) for k in ("high", "low")] for b in range(2)]
    V(lambda e: e.memset(carry[:], 0.0))
    V.wait(V.last())

    turn = sb("h_turn", [P, 2, 32])
    rg = [sb(f"h_rg{n}", [P, 8, 32]) for n in range(3)]
    h3 = lambda ap, n=64: ap.rearrange("p (h d) -> p h d", d=n)

    def pieces(i, j, marks):
        b, ago = j % 2, ago_of(marks, j, ROUND)
        before = lambda k: ago(k, 1)
        at, ti = bass.ds(i * (ROUND * P) + P * j, P), i * ROUND + j
        X = x[b]


        def read(j):
            rows = bass.ds(i * (ROUND * P) + P * j, P)
            marks[f"x{j}"] = ld[1 + j % 2](lambda e: e.dma_start(x[j % 2][:], dram["proj"][rows, 0:C_GF]), after=ago_of(marks, j, ROUND)("t", 2))

        if j == 0:
            read(0)
        got = marks[f"x{j}"]
        ev = {}

        def turn_heads(which, ready):
            T.wait(*ready)
            for q in which:
                first, second, row0 = (("fqT", "fqT", 64), ("fkT", "fkl", 0), ("dqT", "dqT", 64), ("iqT", "iqT", 64))[q]
                col = (C_FQ, C_FK, C_DQ, C_IQ)[q]
                slot, bank = q % 2, 5 + q % 2
                t = core.tr([(lambda k=k: core.bank[:, bank, 128 * k:128 * k + 128], lambda k=k: X[:, col + 128 * k:col + 128 * k + 128]) for k in range(4)],
                            ident, after=[ev[q - 2]] if q > 1 else before(f"ev{q + 2}_"))
                ev[q] = split(core, None, *(to[:] for to in turned[slot]), core.bank[:, bank, :].rearrange("p (k n) -> p k n", k=4), [t],
                              [ld[5 + slot].last()] if q > 1 else before(f"st{slot}_"))
                ld[5 + slot].wait(ev[q])
                for hh in (1, 0):
                    for part, (name, row) in enumerate(((first, 0), (second, row0))):
                        ld[5 + slot](lambda e: e.dma_start(
                            dram[name][hh::2, row:row + 64, at].rearrange("h d n -> d h n"),
                            turned[slot][part][64 * hh:64 * hh + 64, :, :].bitcast(F32)))
                marks[f"st{slot}_{j}"] = ld[5 + slot].last()
                marks[f"ev{q}_{j}"] = ev[q]

        def rotate(Q, r, *cols):
            r1, r2, r3 = r
            for c, nh in zip(cols, (8, 1)):
                blk = h3(X[:, c:c + 64 * nh])
                a, bb = blk[:, :, 0:32], blk[:, :, 32:64]
                cs, sn = over(turn[:, 0, :], 1, nh), over(turn[:, 1, :], 1, nh)
                Q(lambda e: e.tensor_tensor(r1[:, 0:nh, :], a, sn, ALU.mult), own=True, after=[got, angles])
                Q(lambda e: e.tensor_tensor(r2[:, 0:nh, :], bb, sn, ALU.mult), own=True)
                Q(lambda e: e.tensor_tensor(r3[:, 0:nh, :], a, cs, ALU.mult), own=True)
                Q(lambda e: e.tensor_tensor(bb, bb, cs, ALU.mult), own=True)
                Q(lambda e: e.tensor_tensor(a, r3[:, 0:nh, :], r2[:, 0:nh, :], ALU.subtract), own=True)
                Q(lambda e: e.tensor_tensor(bb, bb, r1[:, 0:nh, :], ALU.add), own=True)

        for n, table in enumerate((cos, sin)):
            V(lambda e: e.tensor_copy(turn[:, n, :], table[:, bass.ds(ti, 1), :].rearrange("p a n -> p (a n)")), after=before("rot"), own=True)
        angles = V.last()
        rotate(G, rg, C_IQ, C_IK)
        indexed = marks[f"rot{j}"] = G.last()
        A(lambda e: e.activation(sq[:], X[:, C_FQ:C_FV], ACT.Square), after=[got] + before("sq2"))
        V(lambda e: e.tensor_reduce(ss[:, 0:16], h3(sq[:]), AX.X, ALU.add), after=[A.last()])
        A(lambda e: e.activation(sq[:, 0:576], X[:, C_DQ:C_DV], ACT.Square), after=[V.last()])
        v = V(lambda e: e.tensor_reduce(ss[:, 16:25], h3(sq[:, 0:576]), AX.X, ALU.add), after=[A.last()], own=True)
        A(lambda e: e.activation(sd[:, 0:25], ss[:, 0:25], ACT.Sqrt, bias=tables["eps"][:, 0:1], scale=1.0 / 64), after=[v])
        V(lambda e: e.reciprocal(rs[:, 0:25], sd[:, 0:25]), after=[A.last()])
        for c, r0, nh, gain, scale in ((C_FQ, 0, 8, gq, 0.125), (C_FK, 8, 8, gk, 1.0), (C_DQ, 16, 8, dgq, 0.125), (C_DK, 24, 1, dgk, 1.0)):
            blk = h3(X[:, c:c + 64 * nh])
            V(lambda e: e.tensor_tensor(blk, blk, over(rs[:, r0:r0 + nh], 2, 64), ALU.mult), own=True)
            V(lambda e: e.scalar_tensor_tensor(out=blk, in0=blk, scalar=scale, in1=over(gain[:], 1, nh), op0=ALU.mult, op1=ALU.mult), own=True)
        normed = V.last()
        V(lambda e: e.tensor_tensor(lf[:], X[:, C_FL:C_FL + 8], bf[:], ALU.add), own=True, after=before("ft"))
        V(lambda e: e.tensor_scalar(l2[:], lf[:], -1.0, None, ALU.mult), own=True)
        V(lambda e: e.tensor_tensor(l2[:], l2[:], lf[:], ALU.min), own=True)
        A(lambda e: e.activation(l2[:], l2[:], ACT.Exp), after=[V.last()])
        A(lambda e: e.activation(l2[:], l2[:], ACT.Ln, bias=1.0), own=True)
        V(lambda e: e.tensor_scalar(lf[:], lf[:], 0.0, None, ALU.min), own=True)
        gates = V(lambda e: e.tensor_tensor(lf[:], lf[:], l2[:], ALU.subtract), own=True, after=[A.last()])
        yield
        rotate(V, (r1, r2, r3), C_DQ, C_DK)
        ready = marks[f"sq2{j}"] = V.last()
        yield
        if j + 1 < ROUND:
            read(j + 1)
        turn_heads((0, 1), [normed])
        yield
        T.wait(gates, *before("carry"))
        T(lambda e: e.matmul(core.bank[:, 4, 0:8], tables["mats"][:, C_LE, :], lf[:], start=True, stop=True), inc=False)
        T(lambda e: e.matmul(core.bank[:, 4, 8:16], tables["mats"][:, C_ONE, :], lf[:], start=True, stop=True))
        V(lambda e: e.scalar_tensor_tensor(out=ft[:], in0=core.bank[:, 4, 0:8], scalar=-1.0, in1=carry[:], op0=ALU.mult, op1=ALU.subtract), after=[T.last()])
        V(lambda e: e.tensor_tensor(carry[:], carry[:], core.bank[:, 4, 8:16], ALU.add), own=True)
        marks[f"carry{j}"] = V.last()
        turn_heads((2, 3), [ready, indexed])
        core.tr([(lambda: core.bank[0:8, 7, 256:384], lambda: ft[:]),
                 (lambda: core.bank[0:64, 7, 0:128], lambda: X[:, C_DK:C_DK + 64]),
                 (lambda: core.bank[0:64, 7, 128:256], lambda: X[:, C_IK:C_IK + 64])], ident, after=before("ev4_") + [V.last()])
        marks[f"t{j}"] = T.last()
        marks[f"ft{j}"] = T.last()
        small = split(core, None, kx[0][:], kx[1][:], core.bank[0:64, 7, 0:256], [T.last()], before("st2"))
        marks[f"ev4_{j}"] = split(core, None, fx[0][:], fx[1][:], core.bank[0:8, 7, 256:384], [small])
        ld[7].wait(V.last())
        for part in (1, 0):
            ld[7](lambda e: e.dma_start(dram["dkT"][part, :, at], kx[part][:, 0:128].bitcast(F32)))
            ld[7](lambda e: e.dma_start(dram["ikT"][part, :, at], kx[part][:, 128:256].bitcast(F32)))
            ld[7](lambda e: e.dma_start(dram["fkl"][:, 64 + part, at], fx[part][:].bitcast(F32)))
        marks[f"st2{j}"] = ld[7].last()

    kx, fx = [sb(f"h_kx{b}", [64, 256], R32) for b in range(2)], [sb(f"h_fx{b}", [8, P], R32) for b in range(2)]

    return pieces


TOPK, NAH, HD = 256, 8, 64
DONE = -3e38


def attend(core, dram, tables):
    T, V, A = core.T, core.V, core.A
    ident = tables["mats"][:, C_ID, :]
    with Room(core) as sb:
        far = sb("a_far", [P, 2, SEQ])
        fkk, fkl = sb("a_fkk", [2 * HD, NAH, SEQ], R32), sb("a_fkl", [HD + 2, NAH, SEQ], R32)
        dkk, dkl, ikk, ikl = (sb(f"a_{k}", [n, SEQ], R32) for k, n in (("dkk", 2 * HD), ("dkl", HD), ("ikk", 2 * HD), ("ikl", HD)))
        fv, dv, iw = sb("a_fv", [P, NT, 512]), sb("a_dv", [P, NT, HD]), sb("a_iw", [P, NT, NAH])
        qt = {k: [sb(f"a_{k}{b}", [2 * HD, NAH, P], R32) for b in range(2)] for k in ("fox", "dsa", "idx")}
        qone = [sb(f"a_qone{b}", [HD + 2, NAH, P], R32) for b in range(2)]
        Sm, Pb, R = ([sb(f"a_{k}{b}", [P, SEQ]) for b in range(2)] for k in ("Sm", "Pb", "R"))
        PT = [sb(f"a_PT{b}", [P, NT, P]) for b in range(2)]
        score = [sb(f"a_score{b}", [P, SEQ]) for b in range(3)]
        best = sb("a_best", [P, 8])
        mx, nm, sm, rc = ([sb(f"a_{k}{b}", [P, 1]) for b in range(4)] for k in ("mx", "nm", "sm", "rc"))
        ob = {k: [sb(f"a_o{k}{b}", [P, 512]) for b in range(2)] for k in ("fox", "dsa")}

        V(lambda e: e.memset(far[:], 0.0))
        for b in range(2):
            V(lambda e: e.tensor_scalar(qone[b][HD:HD + 2, :, :], far[HD:HD + 2, 0, 0:SEQ].rearrange("p (h n) -> p h n", h=NAH), 1.0, None, ALU.add), own=True)
        ld = core.load
        index_in, keys_in = (Queue(core.nc, core.nc.gpsimd, k, 16, 0) for k in ("index_keys_in", "keys_in"))
        queries_in = [Queue(core.nc, core.nc.gpsimd, f"queries{n}_in", 16, 0) for n in range(6)]
        pv = dram["proj"].rearrange("(t p) n -> p t n", p=P)
        ld[8](lambda e: e.dma_start(iw[:], pv[:, :, C_IW:C_IW + NAH]))
        masks_in = ld[8](lambda e: e.dma_start(far[:, :, SEQ - P:SEQ], dram["far"].rearrange("m p n -> p m n")), after=[V.last()])
        halves = [slice(HD * half, HD * half + HD) for half in range(2)]
        for rows in halves:
            index_in(lambda e: e.dma_start(ikk[rows, :], dram["ikT"][0]))
        index_in(lambda e: e.dma_start(ikl[:], dram["ikT"][1]))
        ld[0](lambda e: e.dma_start(fv[:], pv[:, :, C_FV:C_FV + 512]))
        values_in = ld[0](lambda e: e.dma_start(dv[:], pv[:, :, C_DV:C_DV + HD]))
        T.wait(index_in.last())
        V.wait(masks_in)

        order = [("idx", 2), ("fox", 0), ("fox", 1), ("fox", 2), ("dsa", 0), ("dsa", 1), ("fox", 3), ("idx", 3), ("fox", 4), ("dsa", 2), ("idx", 4),
                 ("fox", 5), ("dsa", 3), ("idx", 5), ("fox", 6), ("idx", 6), ("dsa", 4), ("fox", 7), ("idx", 7), ("dsa", 5),
                 ("dsa", 6), ("dsa", 7)]
        units = [(kind, j, h) for kind, j in order for h in range(NAH)]
        qload, qfree, count = {}, {}, {}
        done = {k: {} for k in "SEXNO"}
        scored, biased, bias_read, stored = {}, {}, {}, {}
        pending = []

        def load_queries(kind, j):
            n = count[kind] = count.get(kind, -1) + 1
            src = dram[{"fox": "fqT", "dsa": "dqT", "idx": "iqT"}[kind]]
            stream = queries_in[2 * ("fox", "dsa", "idx").index(kind) + n % 2]
            buf = qt[kind][n % 2]
            free = [qfree[kind, n - 2]] if n > 1 else [V.last()]
            got = stream(lambda e: e.dma_start(buf[:], (src[:, :, P * j:P * j + P].rearrange("h d n -> d h n"))), after=free)
            if kind == "fox":
                got = stream(lambda e: e.dma_start(qone[n % 2][0:HD, :, :], (src[:, 0:HD, P * j:P * j + P].rearrange("h d n -> d h n"))))
            qload[kind, j] = (buf, qone[n % 2], got)
            qfree[kind, j, "n"] = n

        def round_of(j):
            s = score[j % 3][:, 0:P * (j + 1)]
            def go(last):
                V(lambda e: e.max(best[:], s), own=True, after=scored[j])
                V(lambda e: e.match_replace(s, best[:], s, DONE), own=True)
                if last:
                    biased[j] = V(lambda e: e.tensor_scalar(s, s, DONE, FAR, ALU.is_gt, ALU.mult), own=True)
            return go

        def fill(n=None, until=None):
            while pending and (n is None or n > 0) and (until is None or until not in biased):
                j, go, last = pending.pop(0)
                go(last)
                n = None if n is None else n - 1

        def step_s(n):
            kind, j, h = units[n]
            L = P * (j + 1)
            if h == 0 and (kind, j) not in qload:
                load_queries(kind, j)
            buf, ones, got = qload[kind, j]
            T.wait(got, *done["E"].get(n - 2, []), *([keys_in.last()] if kind != "idx" else []))
            high = (lambda: ones[:, h, :]) if kind == "fox" else (lambda: buf[0:HD, h, :])
            for c in range(0, L, 512):
                m = min(512, L - c)
                both, low = {"fox": (lambda: fkk[:, h, c:c + m], lambda: fkl[:, h, c:c + m]), "dsa": (lambda: dkk[:, c:c + m], lambda: dkl[:, c:c + m]),
                             "idx": (lambda: ikk[:, c:c + m], lambda: ikl[:, c:c + m])}[kind]
                core.mm(core.bank[:, 2 * (n % 2) + c // 512, 0:m], [(lambda: buf[:, h, :], both), (high, low)])
            done["S"][n] = T.last()
            if h == NAH - 1:
                qfree[kind, qfree[kind, j, "n"]] = T.last()
                later = [u for u in order[order.index((kind, j)) + 1:] if u[0] == kind]
                if later:
                    load_queries(kind, later[0][1])

        def step_e(n):
            kind, j, h = units[n]
            L = P * (j + 1)
            b = n % 2
            S = core.bank[:, 2 * b:2 * b + 2, :].rearrange("p a n -> p (a n)")[:, 0:L]
            if kind == "idx":
                s = score[j % 3][:, 0:L]
                a = A(lambda e: e.activation(R[b][:, 0:L], S, ACT.Relu), after=[done["S"][n]] + done["N"].get(b, []))
                w = iw[:, j, h:h + 1]
                if h == 0:
                    v = V(lambda e: e.tensor_scalar(s, R[b][:, 0:L], w, None, ALU.mult), after=[a] + bias_read.get(j - 3, []), own=True)
                else:
                    v = V(lambda e: e.scalar_tensor_tensor(out=s, in0=R[b][:, 0:L], scalar=w, in1=s, op0=ALU.mult, op1=ALU.add),
                          after=[a], own=True)
                done["N"][b] = [v]
                if h == NAH - 1:
                    d = s[:, L - P:L]
                    scored[j] = [V(lambda e: e.tensor_tensor(d, d, far[:, 1, SEQ - P:SEQ], ALU.add), own=True)]
                    pending.extend((j, round_of(j), r == TOPK // 8 - 1) for r in range(TOPK // 8))
                done["E"][n] = [a]
                return
            if kind == "fox":
                mask, more = far[:, 0, SEQ - L:SEQ], []
            elif j < TOPK // P:
                mask, more = far[:, 1, SEQ - L:SEQ], []
            else:
                fill(until=j)
                mask, more = score[j % 3][:, 0:L], [biased[j]]
            m4 = n % 4
            v = V(lambda e: e.tensor_tensor_reduce(out=Sm[b][:, 0:L], in0=S, in1=mask, scale=1.0, scalar=-3.4e38, op0=ALU.add,
                                                   op1=ALU.max, accum_out=mx[m4][:]), after=[done["S"][n]] + more + done["X"].get(n - 2, []) )
            if kind == "dsa" and h == NAH - 1:
                bias_read[j] = [v]
            v2 = V(lambda e: e.tensor_scalar(nm[m4][:], mx[m4][:], -1.0, None, ALU.mult), own=True)
            a = A(lambda e: e.activation(Pb[b][:, 0:L], Sm[b][:, 0:L], ACT.Exp, bias=nm[m4][:, 0:1], accum_out=sm[m4][:]),
                  after=[v2] + done["X"].get(n - 2, []))
            done["E"][n] = [v]
            done["P", n] = a

        def step_x(n):
            kind, j, h = units[n]
            if kind == "idx":
                return
            b = n % 2
            T.wait(done["P", n])
            evs = []
            for q in range((j + 4) // 4):
                m = min(4, j + 1 - 4 * q)
                t = core.tr([(lambda c=c: core.bank[:, 4 + q, 128 * c:128 * c + 128],
                              lambda c=c: Pb[b][:, 128 * (4 * q + c):128 * (4 * q + c) + 128]) for c in range(m)], ident,
                            after=bank_free.get(q, []))
                o_, i_ = PT[b][:, 4 * q:4 * q + m, :], core.bank[:, 4 + q, 0:128 * m].rearrange("p (c n) -> p c n", c=m)
                ev = A(lambda e: e.activation(o_, i_, ACT.Copy), after=[t] + pt_free.get(b, []))
                bank_free[q] = [ev]
                evs.append(ev)
            done["X"][n] = [T.last()]
            done["T", n] = evs
            m4 = n % 4
            done["R", n] = V(lambda e: e.reciprocal(rc[m4][:], sm[m4][:]), after=[done["P", n]])

        bank_free, pt_free = {}, {}

        def step_o(n):
            kind, j, h = units[n]
            if kind == "idx":
                return
            b, m4, slot = n % 2, n % 4, n % 2
            out = core.bank[:, 6 + slot, 0:HD]
            vals = (lambda k: fv[:, k, HD * h:HD * h + HD]) if kind == "fox" else (lambda k: dv[:, k, :])
            core.mm(out, [(lambda k=k: PT[b][:, k, :], lambda k=k: vals(k)) for k in range(j + 1)],
                    after=done["T", n] + done["O"].get(slot, []) + [values_in])
            pt_free[b] = [T.last()]
            o = ob[kind][j % 2]
            a = A(lambda e: e.activation(o[:, HD * h:HD * h + HD], out, ACT.Copy, scale=rc[m4][:, 0:1]),
                  after=[T.last(), done["R", n]] + (stored.get((kind, j - 2), []) if h == 0 else []))
            done["O"][slot] = [a]
            if h == NAH - 1:
                stored[kind, j] = [core.store[(kind == "dsa") * 2 + j % 2](
                    lambda e: e.dma_start(dram["o" + kind][P * j:P * j + P, :], o[:]), after=[a])]

        load_queries(*order[0])
        for rows in halves:
            keys_in(lambda e: e.dma_start(fkk[rows, :, :], dram["fkT"].rearrange("h d n -> d h n")))
            keys_in(lambda e: e.dma_start(dkk[rows, :], dram["dkT"][0]))
        keys_in(lambda e: e.dma_start(fkl[:], dram["fkl"].rearrange("h d n -> d h n")))
        keys_in(lambda e: e.dma_start(dkl[:], dram["dkT"][1]))
        N = len(units)
        for n in range(-2, N + 1):
            if n + 2 < N:
                step_s(n + 2)
            if 0 <= n + 1 < N:
                step_e(n + 1)
                fill(2)
            if 0 <= n < N:
                step_x(n)
            if 0 <= n - 1:
                step_o(n - 1)


NE, NG, EG, DE = 32, 4, 8, 512
SLOT_TILES = NE + 2 * SEQ // P


def merge(core, dram, tables):
    T, V, A, G = core.T, core.V, core.A, core.G
    ident = tables["mats"][:, C_ID, :]
    with Room(core) as sb:
        ld = core.load
        wp = [sb(f"m_wp{j}", [P, 4, D]) for j in range(2)]
        wo = sb("m_wo", [P, KD, D])
        wr = sb("m_wr", [P, KD, NG + NE])
        gate, gain, shift = (sb("m_" + k, [P, D]) for k in ("gate", "gain", "shift"))
        bg = sb("m_bg", [P, 2 * D])
        o = [sb(f"m_o{b}", [P, D]) for b in range(2)]
        gs = [sb(f"m_gs{b}", [P, 2 * D]) for b in range(2)]
        x = [sb(f"m_xin{b}", [P, D]) for b in range(2)]
        oT, mT, hT = (sb("m_" + k, [P, KD, P]) for k in ("oT", "mT", "hT"))
        m1, m2, x2, h = (sb("m_" + k, [P, D]) for k in ("m1", "m2", "x2", "h"))
        norm = Norm(core, sb, "m_n")
        st = core.store
        mod = dram["mod2"][0, :]
        st[6](lambda e: e.dma_start(bg[:], row(dram["b_gate_2"])))
        rows_in = st[6](lambda e: e.dma_start(gate[:], row(mod[2 * D:3 * D])))
        fox_in, dsa_in, out_in, router_in = (Queue(core.nc, core.nc.gpsimd, f"weights{n}_in", 16, 0) for n in range(4))
        weights = lambda k: dram[k].rearrange("(k p) n -> p k n", p=P)
        fox_in(lambda e: e.dma_start(wp[0][:], weights("w_proj_fox_2")))
        dsa_in(lambda e: e.dma_start(wp[1][:], weights("w_proj_dsa_2")), after=[fox_in.last()])
        out_in(lambda e: e.dma_start(wo[:], weights("w_out_2")), after=[dsa_in.last()])
        router_in(lambda e: e.dma_start(wr[:, :, 0:NG], weights("router_w_grp_2")))
        router_in(lambda e: e.dma_start(wr[:, :, NG:NG + NE], weights("router_w_exp_2")))
        proj_in, out_in, router_in = [fox_in.last(), dsa_in.last()], out_in.last(), router_in.last()
        gain_rows(core, gain[:], dram["norm2_g_2"], mod[4 * D:5 * D], shift[:], mod[3 * D:4 * D], m1[:])
        V.wait(rows_in)
        G.wait(rows_in)

        ROUND = 4
        flat = lambda j: core.bank[:, 2 * j:2 * j + 2, :].rearrange("p a n -> p (a n)")

        class Tile:

            def __init__(self, i, j, marks):
                self.b, self.j, self.marks, self.ago = j % 2, j, marks, ago_of(marks, j, ROUND)
                self.number, self.at = i * ROUND + j, bass.ds(i * (ROUND * P) + P * j, P)

            def mark(self, k, t):
                self.marks[f"{k}{self.j}"] = t

            def turn(self, out, src, ready, name):
                free = [turned[-1]] if turned else [self.marks["bank67"].last_round()] if "bank67" in self.marks else []
                t, ev = turn_rows(core, out, src, KD, ident, (6, 7), ready, [free, free])
                turned.append(ev)
                self.marks["bank67"] = ev
                self.mark(name, t)
                return ev

            def read(self):
                b, at = self.b, self.at
                ld[1 + b](lambda e: e.dma_start(o[b][:, 0:512], dram["ofox"][at, :]), after=self.ago("to", 2))
                l1 = ld[1 + b](lambda e: e.dma_start(o[b][:, 512:1024], dram["odsa"][at, :]))
                l2 = ld[3 + b](lambda e: e.dma_start(gs[b][:], dram["proj"][at, C_GF:C_GF + 2 * D]), after=self.ago("gs", 2))
                G(lambda e: e.tensor_tensor(gs[b][:], gs[b][:], bg[:], ALU.add), after=[l2])
                A.wait(*self.ago("proj", 1))
                self.oT = self.turn(oT, o[b][:], [l1], "to")
                self.sg = A(lambda e: e.activation(gs[b][:], gs[b][:], ACT.Sigmoid), after=[G.last()])

            def read_x(self):
                self.lx = ld[5 + self.b](lambda e: e.dma_start(x[self.b][:], dram["x1"][self.at, :]), after=self.ago("x2", 2))

            def project(self):
                b = self.b
                T.wait(self.oT)
                for j in range(2):
                    T.wait(*([proj_in[j]] if self.j == 0 else []))
                    for half in range(2):
                        core.mm(core.bank[:, 2 * j + half, :], [(lambda k=k: oT[:, 4 * j + k, :], lambda k=k: wp[j][:, k, 512 * half:512 * half + 512])
                                                                for k in range(4)], after=self.ago(f"m{j}", 1) + self.ago("logits", 3 if self.j else 1))
                    p = T.last()
                    V(lambda e: e.tensor_tensor((m1, m2)[j][:], flat(j), gs[b][:, D * j:D * j + D], ALU.mult), after=[p, self.sg] + self.ago("tm", 1), own=True)
                    self.mark(f"m{j}", V.last())
                self.mark("proj", p)
                self.mark("gs", V.last())
                self.m = V(lambda e: e.tensor_tensor(m1[:], m1[:], m2[:], ALU.add), own=True)

            def turn_merged(self):
                A.wait(*self.ago("wout", 1))
                self.mT = self.turn(mT, m1[:], [self.m], "tm")

            def close(self):
                at, b = self.at, self.b
                T.wait(self.mT, *self.ago("x2", 1), *([out_in] if self.j == 0 else []))
                for half in range(2):
                    core.mm(core.bank[:, 4 + half, :], [(lambda k=k: mT[:, k, :], lambda k=k: wo[:, k, 512 * half:512 * half + 512]) for k in range(KD)])
                self.mark("wout", T.last())
                V(lambda e: e.tensor_tensor(x2[:], flat(2), gate[:], ALU.mult), after=[T.last()] + self.ago("stx", 1), own=True)
                V(lambda e: e.tensor_tensor(x2[:], x2[:], x[b][:], ALU.add), own=True, after=[self.lx])
                self.mark("x2", V.last())
                self.mark("stx", core.store[0](lambda e: e.dma_start(dram["x2"][at, :], x2[:]), after=[V.last()]))
                V.wait(norm.rstd(x2[:], tables["eps"][:, 0:1], [V.last()]))
                self.h = norm.apply(h[:], x2[:], gain[:], shift[:], after=self.ago("sth", 1) + self.ago("th", 1))
                self.mark("sth", core.store[1](lambda e: e.dma_start(dram["h2"][at, :], h[:]), after=[self.h]))

            def turn_normed(self):
                A.wait(*self.ago("router", 1))
                self.hT = self.turn(hT, h[:], [self.h], "th")

            def router(self):
                T.wait(*([router_in] if self.j == 0 else []))
                core.mm(core.bank[:, 0, 0:NG + NE], [(lambda k=k: hT[:, k, :], lambda k=k: wr[:, k, :]) for k in range(KD)],
                        after=[self.hT, self.marks[f"m0{min(self.j + 2, ROUND - 1)}"]] + self.ago("logits", 1))
                self.mark("router", T.last())
                V(lambda e: e.tensor_copy(tables["logits"][:, bass.ds(self.number, 1), :].rearrange("p a n -> p (a n)"), core.bank[:, 0, 0:NG + NE]),
                  after=[T.last()])
                self.mark("logits", V.last())

        turned = []

        def body(i, marks):
            turned.clear()
            tiles = [Tile(i, j, marks) for j in range(ROUND)]
            tiles[0].read()
            tiles[0].read_x()
            for n in range(ROUND + 2):
                now = lambda k: 0 <= n - k < ROUND
                if now(0):
                    tiles[n].project()
                if n + 1 < ROUND:
                    tiles[n + 1].read()
                if now(2):
                    tiles[n - 2].turn_normed()
                if now(1):
                    tiles[n - 1].close()
                if 0 < n + 1 < ROUND:
                    tiles[n + 1].read_x()
                if now(2):
                    tiles[n - 2].router()
                if now(0):
                    tiles[n].turn_merged()
        core.loop(NT // ROUND, body)


def route(core, dram, tables):
    T, V, A, G = core.T, core.V, core.A, core.G
    with Room(core) as sb:
        ld = core.load
        v = lambda f: V(f, own=True)
        new = lambda name, *shape: sb("r_" + name, [P, *shape])
        bgr, bex = new("bgr", NG), new("bex", NE)
        cst = new("cst", NG + NE + 8 + SLOT_TILES)
        ld[0](lambda e: e.dma_start(bgr[:], row(dram["router_b_grp_2"])))
        ld[0](lambda e: e.dma_start(bex[:], row(dram["router_b_exp_2"])))
        got = ld[0](lambda e: e.dma_start(cst[:], row(dram["counts"])))
        zero = sb("r_zero", [P, SLOT_TILES], I32)
        G(lambda e: e.memset(zero[:], 0))
        core.store[0](lambda e: e.dma_start(dram["slot_token"].rearrange("(p m) a -> p (m a)", p=P), zero[:]), after=[G.last()])
        down4, down32 = cst[:, 0:NG], cst[:, NG:NG + NE]
        steps, tile_no = cst[:, NG + NE:NG + NE + 8], cst[:, NG + NE + 8:]
        V.wait(got)
        gl, eq, oh = new("gl", NT, NG), new("eq", NT, NG), new("oh", NT, NG)
        gm, gs, gw, t1, t2 = (new(k, NT) for k in ("gm", "gs", "gw", "t1", "t2"))
        el, q32, w32 = new("el", NT, NE), new("q32", NT, NE), new("w32", NT, NE)
        E = [new(f"E{j}", NT, NE) for j in range(2)]
        m = [new(f"m{j}", NT) for j in range(2)]
        lg = tables["logits"]
        W = tables["weight"]
        v(lambda e: e.tensor_tensor(gl[:], lg[:, :, 0:NG], over(bgr[:], 1, NT), ALU.add))
        v(lambda e: e.tensor_reduce(gm[:], gl[:], AX.X, ALU.max))
        v(lambda e: e.tensor_tensor(eq[:], gl[:], over(gm[:], 2, NG), ALU.is_equal))
        v(lambda e: e.tensor_tensor(eq[:], eq[:], over(down4, 1, NT), ALU.mult))
        v(lambda e: e.tensor_reduce(t1[:], eq[:], AX.X, ALU.max))
        v(lambda e: e.tensor_tensor(oh[:], eq[:], over(t1[:], 2, NG), ALU.is_equal))
        v(lambda e: e.tensor_tensor(gl[:], gl[:], over(gm[:], 2, NG), ALU.subtract))
        a = A(lambda e: e.activation(gl[:], gl[:], ACT.Exp), after=[V.last()])
        V.wait(a)
        v(lambda e: e.tensor_reduce(gs[:], gl[:], AX.X, ALU.add))
        v(lambda e: e.reciprocal(gw[:], gs[:]))
        v(lambda e: e.tensor_scalar(oh[:], oh[:], -1.0, -FAR, ALU.add, ALU.mult))
        v(lambda e: e.tensor_tensor(el[:], lg[:, :, NG:NG + NE], over(bex[:], 1, NT), ALU.add))
        el4 = el[:].rearrange("p t (g k) -> p (t g) k", k=EG)
        v(lambda e: e.tensor_tensor(el4, el4, over(oh[:].rearrange("p t g -> p (t g)"), 2, EG), ALU.add))
        for j in range(2):
            v(lambda e: e.tensor_reduce(m[j][:], el[:], AX.X, ALU.max))
            v(lambda e: e.tensor_tensor(q32[:], el[:], over(m[j][:], 2, NE), ALU.is_equal))
            v(lambda e: e.tensor_tensor(q32[:], q32[:], over(down32, 1, NT), ALU.mult))
            v(lambda e: e.tensor_reduce(t1[:], q32[:], AX.X, ALU.max))
            v(lambda e: e.tensor_tensor(E[j][:], q32[:], over(t1[:], 2, NE), ALU.is_equal))
            if j == 0:
                v(lambda e: e.scalar_tensor_tensor(out=el[:], in0=E[0][:], scalar=2 * FAR, in1=el[:], op0=ALU.mult, op1=ALU.add))
        v(lambda e: e.tensor_tensor(t2[:], m[1][:], m[0][:], ALU.subtract))
        a = A(lambda e: e.activation(t2[:], t2[:], ACT.Exp), after=[V.last()])
        V.wait(a)
        v(lambda e: e.tensor_scalar(t1[:], t2[:], 1.0, None, ALU.add))
        v(lambda e: e.reciprocal(t1[:], t1[:]))
        v(lambda e: e.tensor_tensor(W[:, 0, :], t1[:], gw[:], ALU.mult))
        v(lambda e: e.tensor_tensor(W[:, 1, :], W[:, 0, :], t2[:], ALU.mult))
        v(lambda e: e.tensor_tensor(w32[:], E[0][:], E[1][:], ALU.add))
        for j, c in ((0, C_LT), (1, C_ONE)):
            T(lambda e: e.matmul(core.bank[:, j, 0:NT * NE], tables["mats"][:, c, :], w32[:].rearrange("p t n -> p (t n)"), start=True, stop=True),
              after=[V.last()])
        rank, run, total = new("rank", NT, NE), new("run", NE), new("total", NT, NE)
        V.wait(T.last())
        v(lambda e: e.memset(run[:], 0.0))
        v(lambda e: e.tensor_copy(total[:].rearrange("p t n -> p (t n)"), core.bank[:, 1, 0:NT * NE]))
        for t in range(NT):
            v(lambda e: e.tensor_tensor(rank[:, t, :], core.bank[:, 0, NE * t:NE * t + NE], run[:], ALU.add))
            v(lambda e: e.tensor_tensor(run[:], run[:], total[:, t, :], ALU.add))
        cmp, inc = new("cmp", NE, 8), [new(f"inc{j}", NE) for j in range(2)]
        tiles = new("tiles", NE)
        v(lambda e: e.tensor_tensor(cmp[:], over(run[:], 2, 8), over(steps, 1, NE), ALU.is_gt))
        v(lambda e: e.tensor_reduce(tiles[:], cmp[:], AX.X, ALU.add))
        v(lambda e: e.tensor_copy(inc[0][:], tiles[:]))
        src = 0
        for d in (1, 2, 4, 8, 16):
            v(lambda e: e.tensor_copy(inc[1 - src][:, 0:d], inc[src][:, 0:d]))
            v(lambda e: e.tensor_tensor(inc[1 - src][:, d:NE], inc[src][:, d:NE], inc[src][:, 0:NE - d], ALU.add))
            src = 1 - src
        ends = inc[src]
        base = new("base", NE)
        v(lambda e: e.tensor_tensor(base[:], ends[:], tiles[:], ALU.subtract))
        v(lambda e: e.tensor_scalar(base[:], base[:], float(P), None, ALU.mult))
        v(lambda e: e.tensor_tensor(rank[:], rank[:], over(base[:], 1, NT), ALU.add))
        for j in range(2):
            v(lambda e: e.tensor_tensor(q32[:], E[j][:], rank[:], ALU.mult))
            v(lambda e: e.tensor_reduce(t1[:], q32[:], AX.X, ALU.add))
            v(lambda e: e.tensor_copy(tables["slot"][:, j, :], t1[:]))
        ge, te = new("ge", SLOT_TILES, NE), new("te", SLOT_TILES)
        v(lambda e: e.tensor_tensor(ge[:], over(tile_no, 2, NE), over(ends[:], 1, SLOT_TILES), ALU.is_ge))
        v(lambda e: e.tensor_reduce(te[:], ge[:], AX.X, ALU.add))
        v(lambda e: e.tensor_scalar(te[:], te[:], float(NE - 1), None, ALU.min))
        v(lambda e: e.tensor_copy(tables["expert"][:], te[:]))
        v(lambda e: e.tensor_tensor(te[:, 0:SLOT_TILES // 2], cst[:, NG + NE + 8:NG + NE + 8 + SLOT_TILES:2],
                                    ends[:, NE - 1:NE].to_broadcast([P, SLOT_TILES // 2]), ALU.is_lt))
        v(lambda e: e.tensor_reduce(gs[:, 0:1], te[:, 0:SLOT_TILES // 2], AX.X, ALU.add))
        v(lambda e: e.tensor_copy(tables["live"][:], gs[:, 0:1]))


def experts(core, dram, tables):
    T, V, A, G = core.T, core.V, core.A, core.G
    ident = tables["mats"][:, C_ID, :]
    with Room(core) as sb:
        ld = core.load
        w1, w3 = ([sb(f"e_{k}{b}", [P, KD, DE]) for b in range(2)] for k in ("w1", "w3"))
        w2 = [sb(f"e_w2{b}", [P, DE // P, D]) for b in range(2)]
        ids = sb("e_ids", [P, SLOT_TILES], I32)
        idb = [sb(f"e_idb{b}", [P, 1], I32) for b in range(2)]
        x = [sb(f"e_x{b}", [P, D]) for b in range(2)]
        xT = [sb(f"e_xT{b}", [P, KD, P]) for b in range(2)]
        g = [sb(f"e_g{b}", [P, DE]) for b in range(2)]
        gT = [sb(f"e_gT{b}", [P, DE // P, P]) for b in range(2)]
        y = [sb(f"e_y{b}", [P, D]) for b in range(2)]
        tok = sb("e_tok", [P, NT], I32)
        G(lambda e: e.iota(tok[:], [[P, NT]], base=0, channel_multiplier=1))
        G.wait(G.last())
        for t in range(NT):
            for j in range(2):
                core.scatter(lambda e: e.indirect_dma_start(out=dram["slot_token"], out_offset=bass.IndirectOffsetOnAxis(
                    ap=tables["slot"][:, j, t:t + 1].bitcast(U32), axis=0), in_=tok[:, t:t + 1], in_offset=None))
        A.wait(core.scatter.last())
        with core.nc.allow_non_contiguous_dma(reason="a slot's token on the slot's partition"):
            got = core.store[2](lambda e: e.dma_start(ids[:], dram["slot_token"].rearrange("(m p) a -> p (m a)", p=P)))
        idle, nought = sb("e_idle", [P, 1]), sb("e_nought", [P, D])
        A.wait(V(lambda e: e.memset(nought[:], 0.0)))
        gathers = [Queue(core.nc, core.nc.gpsimd, f"expert_rows{b}_done", 16, 0) for b in range(2)]
        G(lambda e: e.memset(idle[:], 0.0))
        G.wait(got)

        def fetch(b, i, marks):
            prev = prev_of(marks)
            m = i * 2 + b
            if ld[1].counting:
                ex = 0
            else:
                ex = core.nc.sync.value_load(tables["expert"][0:1, bass.ds(m, 1)], min_val=0, max_val=NE - 1)
            out = []
            for j, (buf, name, kk) in enumerate(((w1, "exp_w1_2", KD), (w3, "exp_w3_2", KD), (w2, "exp_w2_2", DE // P))):
                n = 1 + 3 * b + j
                out.append(ld[n](lambda e: e.dma_start(buf[b][:], dram[name][bass.ds(ex, 1), :, :].rearrange("a (k p) n -> p (a k) n", p=P)),
                                 after=prev(f"w{j}{b}")))
            G(lambda e: e.tensor_copy(idb[b][:], ids[:, bass.ds(m, 1)]), after=prev(f"tx{b}"))
            G.wait(G.last())
            G(lambda e: e.tensor_tensor(idle[:], idle[:], idle[:], ALU.add))
            gather = gathers[b](lambda e: e.indirect_dma_start(out=x[b][:], out_offset=None, in_=dram["h2"],
                                                                   in_offset=bass.IndirectOffsetOnAxis(ap=idb[b][:, 0:1].bitcast(U32), axis=0)))
            return out, gather

        def turn_x(b, gather, marks):
            before = prev_of(marks)
            T.wait(gather, *before(f"down{b}"))
            for q in range(2):
                t = core.tr([(lambda c=c: core.bank[:, 4 + q, 128 * c:128 * c + 128], lambda c=c: x[b][:, 512 * q + 128 * c:512 * q + 128 * c + 128])
                             for c in range(4)], ident, after=[last[f"x{q}"]] if f"x{q}" in last else prev_of(marks)(f"lx{q}"))
                o_, i_ = xT[b][:, 4 * q:4 * q + 4, :], core.bank[:, 4 + q, :].rearrange("p (c n) -> p c n", c=4)
                Q = (A, V)[q]
                last[f"x{q}"] = Q((lambda e: e.activation(o_, i_, ACT.Copy)) if q == 0 else (lambda e: e.tensor_copy(o_, i_)),
                                  after=[t] + before(f"up{b}"))
                marks[f"lx{q}"] = last[f"x{q}"]
            marks[f"tx{b}"] = T.last()
            return [last["x0"], last["x1"]]

        def up(b, w, ready, marks):
            T.wait(*ready)
            for j, buf in ((0, w1), (1, w3)):
                core.mm(core.bank[:, j, :], [(lambda k=k: xT[b][:, k, :], lambda k=k: buf[b][:, k, :]) for k in range(KD)],
                        after=[w[j]] + ([last["mul"]] if "mul" in last else prev_of(marks)("lmul")))
                marks[f"w{j}{b}"] = T.last()
            marks[f"up{b}"] = T.last()
            a = A(lambda e: e.activation(g[b][:], core.bank[:, 0, :], ACT.Silu), after=[T.last()] + prev_of(marks)(f"tg{b}"))
            last["mul"] = V(lambda e: e.tensor_tensor(g[b][:], g[b][:], core.bank[:, 1, :], ALU.mult), after=[a])
            marks["lmul"] = last["mul"]

        def turn_g(b, mul, marks):
            t = core.tr([(lambda c=c: core.bank[:, 6 + b, 128 * c:128 * c + 128], lambda c=c: g[b][:, 128 * c:128 * c + 128]) for c in range(4)],
                        ident, after=[mul] + prev_of(marks)(f"g{b}"))
            marks[f"tg{b}"] = t
            marks[f"g{b}"] = last[f"g{b}"] = A(lambda e: e.activation(gT[b][:].rearrange("p c n -> p (c n)"), core.bank[:, 6 + b, :], ACT.Copy),
                                               after=[t] + prev_of(marks)(f"down{b}"))

        def down(b, i, w, marks):
            T.wait(last[f"g{b}"], w[2])
            for half in range(2):
                Q = (A, V)[half]
                core.mm(core.bank[:, 2 + half, :], [(lambda k=k: gT[b][:, k, :], lambda k=k: w2[b][:, k, 512 * half:512 * half + 512])
                                                    for k in range(DE // P)],
                        after=[last[f"y{half}"]] if f"y{half}" in last else prev_of(marks)(f"ly{half}"))
                o_, i_ = y[b][:, 512 * half:512 * half + 512], core.bank[:, 2 + half, :]
                last[f"y{half}"] = marks[f"ly{half}"] = Q(
                    (lambda e: e.activation(o_, i_, ACT.Copy)) if half == 0 else (lambda e: e.tensor_copy(o_, i_)),
                    after=[T.last()] + prev_of(marks)(f"st{b}"))
            marks[f"down{b}"] = marks[f"w2{b}"] = T.last()
            marks[f"st{b}"] = core.store[b](lambda e: e.dma_start(dram["y"][bass.ds(i * 256 + 128 * b, 128), :], y[b][:]),
                                            after=[last["y0"], last["y1"]])

        last = {}

        def body(i, marks):
            last.clear()
            w, x_ = zip(*(fetch(b, i, marks) for b in range(2)))
            r0 = turn_x(0, x_[0], marks)
            up(0, w[0], r0, marks)
            mul0 = last["mul"]
            r1 = turn_x(1, x_[1], marks)
            turn_g(0, mul0, marks)
            up(1, w[1], r1, marks)
            down(0, i, w[0], marks)
            turn_g(1, last["mul"], marks)
            down(1, i, w[1], marks)

        def rest(i):
            for b in range(2):
                core.store[b](lambda e: e.dma_start(dram["y"][bass.ds(i * 256 + 128 * b, 128), :], nought[:]))

        live = core.nc.values_load(tables["live"][0:1, 0:1], min_val=0, max_val=SLOT_TILES // 2)
        core.loop(SLOT_TILES // 2, body, gathers, live, rest)


def combine(core, dram, tables):
    V, G = core.V, core.G
    with Room(core) as sb:
        gate = sb("o_gate", [P, D])
        DEPTH = 4
        y = [[sb(f"o_y{j}{b}", [P, D]) for b in range(DEPTH)] for j in range(2)]
        x2 = [sb(f"o_x{b}", [P, D]) for b in range(DEPTH)]
        gathers = [[Queue(core.nc, core.nc.gpsimd, f"rows{j}{b}_in", 16, 0) for b in range(DEPTH)] for j in range(2)]
        V.wait(core.load[0](lambda e: e.dma_start(gate[:], row(dram["mod2"][0, 5 * D:6 * D]))))
        read, stored = {}, {}
        for t in range(NT):
            b = t % DEPTH
            lx = core.load[1 + b](lambda e: e.dma_start(x2[b][:], dram["x2"][P * t:P * t + P, :]), after=stored.get(t - DEPTH, []))
            got = [gathers[j][b](lambda e: e.indirect_dma_start(
                out=y[j][b][:], out_offset=None, in_=dram["y"],
                in_offset=bass.IndirectOffsetOnAxis(ap=tables["slot"][:, j, t:t + 1].bitcast(U32), axis=0)), after=read.get(t - DEPTH, [])) for j in range(2)]
            V(lambda e: e.tensor_scalar(y[0][b][:], y[0][b][:], tables["weight"][:, 0, t:t + 1], None, ALU.mult), after=got[:1])
            V(lambda e: e.scalar_tensor_tensor(out=y[0][b][:], in0=y[1][b][:], scalar=tables["weight"][:, 1, t:t + 1], in1=y[0][b][:],
                                               op0=ALU.mult, op1=ALU.add), after=got[1:], own=True)
            V(lambda e: e.tensor_tensor(y[0][b][:], y[0][b][:], gate[:], ALU.mult), own=True)
            read[t] = [V(lambda e: e.tensor_tensor(x2[b][:], x2[b][:], y[0][b][:], ALU.add), own=True, after=[lx])]
            stored[t] = [core.store[b](lambda e: e.dma_start(dram["result"][P * t:P * t + P, :], x2[b][:]), after=[V.last()])]


SCRATCH = {"mods": (2, 3 * D), "mod2": (1, 6 * D), "uT": (DF, SEQ), "z": (SEQ, 2 * D), "xbcT": (P + CONV, SEQ + CTX), "mix": (SEQ, 2 * D), "xtok": (SEQ + CTX, 2 * P + CONV),
           "x1": (SEQ, D), "h1": (SEQ, D), "proj": (SEQ, COLS2), "fqT": (NAH, 2 * HD, SEQ), "fkT": (NAH, HD, SEQ), "fkl": (NAH, HD + 2, SEQ), "dqT": (NAH, 2 * HD, SEQ),
           "iqT": (NAH, 2 * HD, SEQ), "dkT": (2, HD, SEQ), "ikT": (2, HD, SEQ), "ofox": (SEQ, 512), "odsa": (SEQ, 512), "x2": (SEQ, D), "h2": (SEQ, D),
           "y": (SLOT_TILES * P, D)}
STAGES = (modulation, project_first, fourier, state_space, close_first, project_second, attend, merge, route, experts, combine)


def program(nc, dram):
    for name, shape in SCRATCH.items():
        dram[name] = nc.dram_tensor(name, shape, F32).ap()
    dram["slot_token"] = nc.dram_tensor("slot_token", (SLOT_TILES * P, 1), I32).ap()
    with ExitStack() as ctx:
        core = Core(nc, ctx)
        with Room(core) as sb:
            tables = load_tables(core, sb, dram)
            for stage in STAGES:
                stage(core, dram, tables)


def kernel(**inputs):
    import concourse.bacc as bacc
    from concourse.bass_utils import run_bass_kernel_spmd

    nc = bacc.Bacc("TRN2", target_bir_lowering=False, num_devices=1)
    arrays, dram = {}, {}
    for name, a in {**inputs, **constants()}.items():
        a = np.asarray(a)
        if name in inputs and a.ndim > 1:
            a = a[0]
        arrays["in_" + name] = np.ascontiguousarray(a)
        dram[name] = nc.dram_tensor("in_" + name, a.shape, mybir.dt.from_np(a.dtype), kind="ExternalInput").ap()
    dram["result"] = nc.dram_tensor("result", (SEQ, D), F32, kind="ExternalOutput").ap()
    program(nc, dram)
    out = run_bass_kernel_spmd(nc, [arrays], core_ids=[0]).results[0]["result"]
    return out.reshape(1, SEQ, D)
```
